# Optimizing a Trainium2 kernel written in Bass

```python
import jax, jax.numpy as jnp
from jax import lax
import numpy as np

D_MODEL = 1024
BATCH = 1
SEQ = 256
DEPTH = 1
DEC_BATCH = 8
DEC_SEQ = 16
PAST_LEN = 128

CHUNK = 64
MIX_WIDTH = D_MODEL
HEAD_DIM = 64
ATTN_WIDTH = MIX_WIDTH // 2
ATTN_HEADS = ATTN_WIDTH // HEAD_DIM
CONV_DIM = MIX_WIDTH - ATTN_WIDTH
CONV_GROUPS = CONV_DIM // HEAD_DIM
CONV_K = 3
PROJ_COLS = 3 * ATTN_WIDTH + ATTN_HEADS + 3 * CONV_DIM
Q_BLOCK = 128
N_GROUPS = 4
EXPERTS_PER_GROUP = 8
TOP_K_IN_GROUP = 2
D_EXPERT = 256
RMS_EPS = 1e-6
FORGET_BIAS_INIT = 3.0

kernel_name = "hybrid_fox_shortconv_hiermoe_stream_step"

def rmsnorm(x, g):
    xf = x.astype(jnp.float32)
    y = xf * lax.rsqrt(jnp.mean(xf * xf, axis=-1, keepdims=True) + RMS_EPS)
    return (y * g.astype(jnp.float32)).astype(x.dtype)

def project(xn, w_in, b_forget):
    bsz, t = xn.shape[0], xn.shape[1]
    p = xn @ w_in
    A, H, C = ATTN_WIDTH, ATTN_HEADS, CONV_DIM
    q, k, v, f, bg, cg, h = jnp.split(p, [A, 2 * A, 3 * A, 3 * A + H, 3 * A + H + C, 3 * A + H + 2 * C], axis=-1)
    q = q.reshape(bsz, t, H, HEAD_DIM)
    k = k.reshape(bsz, t, H, HEAD_DIM)
    v = v.reshape(bsz, t, H, HEAD_DIM)
    lf = jax.nn.log_sigmoid(f.astype(jnp.float32) + b_forget.astype(jnp.float32))
    return q, k, v, lf, bg, cg, h

def fox_prompt(q, k, v, lf):
    bsz, s_len = q.shape[0], q.shape[1]
    nb = s_len // Q_BLOCK
    scale = HEAD_DIM ** -0.5
    cT = jnp.cumsum(lf, axis=1).transpose(0, 2, 1)
    kf = k.astype(jnp.float32)
    qb_all = q.astype(jnp.float32).reshape(bsz, nb, Q_BLOCK, ATTN_HEADS, HEAD_DIM).transpose(1, 0, 2, 3, 4)
    cq_all = cT.reshape(bsz, ATTN_HEADS, nb, Q_BLOCK).transpose(2, 0, 1, 3)
    kpos = jnp.arange(s_len)

    def block(args):
        qb, cqb, i = args
        s = jnp.einsum('bqhd,bkhd->bhqk', qb, kf) * scale + (cqb[..., None] - cT[:, :, None, :])
        qpos = i * Q_BLOCK + jnp.arange(Q_BLOCK)
        s = jnp.where(kpos[None, :] <= qpos[:, None], s, -jnp.inf)
        p = jax.nn.softmax(s, axis=-1)
        return jnp.einsum('bhqk,bkhd->bqhd', p.astype(v.dtype), v)

    o = lax.map(block, (qb_all, cq_all, jnp.arange(nb)))
    return o.transpose(1, 0, 2, 3, 4).reshape(bsz, s_len, ATTN_WIDTH)

def fox_sample(q, k, v, lf, cache_k, cache_v, cache_lf):
    bsz, t = q.shape[0], q.shape[1]
    p_len = cache_k.shape[1]
    scale = HEAD_DIM ** -0.5
    lf_p = cache_lf.astype(jnp.float32)
    c_past = jnp.cumsum(lf_p, axis=1) - jnp.sum(lf_p, axis=1, keepdims=True)
    c_new = jnp.cumsum(lf, axis=1)
    ck = jnp.concatenate([c_past, c_new], axis=1).transpose(0, 2, 1)
    keys = jnp.concatenate([cache_k.astype(k.dtype), k], axis=1)
    vals = jnp.concatenate([cache_v.astype(v.dtype), v], axis=1)
    s = jnp.einsum('bqhd,bkhd->bhqk', q.astype(jnp.float32), keys.astype(jnp.float32)) * scale
    s = s + (c_new.transpose(0, 2, 1)[..., None] - ck[:, :, None, :])
    mask = jnp.arange(p_len + t)[None, :] <= (p_len + jnp.arange(t))[:, None]
    s = jnp.where(mask, s, -jnp.inf)
    p = jax.nn.softmax(s, axis=-1)
    o = jnp.einsum('bhqk,bkhd->bqhd', p.astype(vals.dtype), vals)
    return o.reshape(bsz, t, ATTN_WIDTH)

def short_conv(bg, u, conv_state, conv_w):
    t = u.shape[1]
    up = jnp.concatenate([conv_state.astype(u.dtype), u], axis=1)
    y = conv_w[0] * up[:, 0:t]
    for i in range(1, CONV_K):
        y = y + conv_w[i] * up[:, i:i + t]
    return bg * y, up[:, -(CONV_K - 1):]

def hier_moe(xn, w_rg, b_rg, w_re, b_re, w_gu, w_dn):
    lead = xn.shape[:-1]
    t = xn.reshape(-1, D_MODEL)
    pg = jax.nn.softmax((t @ w_rg).astype(jnp.float32) + b_rg.astype(jnp.float32), axis=-1)
    pg_top, g_top = lax.top_k(pg, 1)
    le = jnp.einsum('nd,gde->nge', t, w_re).astype(jnp.float32) + b_re.astype(jnp.float32)
    le_sel = jnp.take_along_axis(le, g_top[:, :, None], axis=1)[:, 0]
    pe_top, e_top = lax.top_k(jax.nn.softmax(le_sel, axis=-1), TOP_K_IN_GROUP)
    w_top = pe_top / jnp.sum(pe_top, axis=-1, keepdims=True) * pg_top
    w_group = jnp.sum(jax.nn.one_hot(e_top, EXPERTS_PER_GROUP, dtype=jnp.float32) * w_top[..., None], axis=1)
    comb = jax.nn.one_hot(g_top[:, 0], N_GROUPS, dtype=jnp.float32)[:, :, None] * w_group[:, None, :]
    out = jnp.zeros_like(t)
    for gi in range(N_GROUPS):
        gate, up = jnp.split(jnp.einsum('nd,edf->nef', t, w_gu[gi]), 2, axis=-1)
        hmid = jax.nn.silu(gate) * up * comb[:, gi, :, None].astype(t.dtype)
        out = out + jnp.einsum('nef,efd->nd', hmid, w_dn[gi])
    return out.reshape(*lead, D_MODEL)

def trunk_layer(x, attend, conv_state, norm_mix_g, w_in, b_forget, conv_w, norm_attn_g, norm_conv_g,
                w_out, norm_ffn_g, w_router_group, b_router_group, w_router_expert, b_router_expert,
                w_expert_gate_up, w_expert_down):
    xn = rmsnorm(x, norm_mix_g)
    q, k, v, lf, bg, cg, h = project(xn, w_in, b_forget)
    o_a = attend(q, k, v, lf)
    o_b, new_conv = short_conv(bg, cg * h, conv_state, conv_w)
    merged = jnp.concatenate([rmsnorm(o_a, norm_attn_g), rmsnorm(o_b, norm_conv_g)], axis=-1)
    x = x + merged @ w_out
    x = x + hier_moe(rmsnorm(x, norm_ffn_g), w_router_group, b_router_group, w_router_expert,
                     b_router_expert, w_expert_gate_up, w_expert_down)
    return x, k, v, lf, new_conv

def setup_inputs(seed: int = 0) -> dict:
    key = jax.random.key(seed)
    ks = jax.random.split(key, 20)
    nrm = jax.random.normal
    f32 = jnp.float32
    return {
        "x_prompt": nrm(ks[0], (BATCH, SEQ, D_MODEL), f32),
        "x_sample": nrm(ks[1], (DEC_BATCH, DEC_SEQ, D_MODEL), f32),
        "cache_k": nrm(ks[2], (DEPTH, DEC_BATCH, PAST_LEN, ATTN_HEADS, HEAD_DIM), f32),
        "cache_v": nrm(ks[3], (DEPTH, DEC_BATCH, PAST_LEN, ATTN_HEADS, HEAD_DIM), f32),
        "cache_logf": jax.nn.log_sigmoid(FORGET_BIAS_INIT + nrm(ks[4], (DEPTH, DEC_BATCH, PAST_LEN, ATTN_HEADS), f32)),
        "state_conv": nrm(ks[5], (DEPTH, DEC_BATCH, CONV_K - 1, CONV_DIM), f32),
        "norm_mix_g": 1.0 + 0.02 * nrm(ks[6], (DEPTH, D_MODEL), f32),
        "w_in": nrm(ks[7], (DEPTH, D_MODEL, PROJ_COLS), f32) * D_MODEL ** -0.5,
        "b_forget": FORGET_BIAS_INIT + 0.5 * nrm(ks[8], (DEPTH, ATTN_HEADS), f32),
        "conv_w": nrm(ks[9], (DEPTH, CONV_K, CONV_DIM), f32) * CONV_K ** -0.5,
        "norm_attn_g": 1.0 + 0.02 * nrm(ks[10], (DEPTH, ATTN_WIDTH), f32),
        "norm_conv_g": 1.0 + 0.02 * nrm(ks[11], (DEPTH, CONV_DIM), f32),
        "w_out": nrm(ks[12], (DEPTH, MIX_WIDTH, D_MODEL), f32) * MIX_WIDTH ** -0.5,
        "norm_ffn_g": 1.0 + 0.02 * nrm(ks[13], (DEPTH, D_MODEL), f32),
        "w_router_group": nrm(ks[14], (DEPTH, D_MODEL, N_GROUPS), f32) * D_MODEL ** -0.5,
        "b_router_group": 0.01 * nrm(ks[15], (DEPTH, N_GROUPS), f32),
        "w_router_expert": nrm(ks[16], (DEPTH, N_GROUPS, D_MODEL, EXPERTS_PER_GROUP), f32) * D_MODEL ** -0.5,
        "b_router_expert": 0.01 * nrm(ks[17], (DEPTH, N_GROUPS, EXPERTS_PER_GROUP), f32),
        "w_expert_gate_up": nrm(ks[18], (DEPTH, N_GROUPS, EXPERTS_PER_GROUP, D_MODEL, 2 * D_EXPERT), f32) * D_MODEL ** -0.5,
        "w_expert_down": nrm(ks[19], (DEPTH, N_GROUPS, EXPERTS_PER_GROUP, D_EXPERT, D_MODEL), f32) * D_EXPERT ** -0.5,
        "norm_final_g": 1.0 + 0.02 * nrm(jax.random.fold_in(key, 99), (D_MODEL,), f32),
    }

def reference(x_prompt, x_sample, cache_k, cache_v, cache_logf, state_conv, norm_mix_g, w_in, b_forget,
              conv_w, norm_attn_g, norm_conv_g, w_out, norm_ffn_g, w_router_group, b_router_group,
              w_router_expert, b_router_expert, w_expert_gate_up, w_expert_down, norm_final_g):
    yp, ys = x_prompt, x_sample
    kp_l, vp_l, lfp_l, cvp_l = [], [], [], []
    ks_l, vs_l, lfs_l, cvs_l = [], [], [], []
    for l in range(DEPTH):
        w = (norm_mix_g[l], w_in[l], b_forget[l], conv_w[l], norm_attn_g[l], norm_conv_g[l], w_out[l],
             norm_ffn_g[l], w_router_group[l], b_router_group[l], w_router_expert[l], b_router_expert[l],
             w_expert_gate_up[l], w_expert_down[l])
        zero_conv = jnp.zeros((yp.shape[0], CONV_K - 1, CONV_DIM), yp.dtype)
        yp, kp, vp, lfp, cvp = trunk_layer(yp, fox_prompt, zero_conv, *w)
        ck, cv, clf = cache_k[l], cache_v[l], cache_logf[l]
        attend_s = lambda q, k, v, lf, ck=ck, cv=cv, clf=clf: fox_sample(q, k, v, lf, ck, cv, clf)
        ys, kn, vn, lfn, cvn = trunk_layer(ys, attend_s, state_conv[l], *w)
        kp_l.append(kp); vp_l.append(vp); lfp_l.append(lfp); cvp_l.append(cvp)
        ks_l.append(kn); vs_l.append(vn); lfs_l.append(lfn); cvs_l.append(cvn)
    y_prompt = rmsnorm(yp, norm_final_g)
    y_sample = rmsnorm(ys, norm_final_g)
    new_k_prompt = jnp.stack(kp_l, axis=0)
    new_v_prompt = jnp.stack(vp_l, axis=0)
    new_logf_prompt = jnp.stack(lfp_l, axis=0)
    new_conv_prompt = jnp.stack(cvp_l, axis=0)
    new_k_sample = jnp.stack(ks_l, axis=0)
    new_v_sample = jnp.stack(vs_l, axis=0)
    new_logf_sample = jnp.stack(lfs_l, axis=0)
    new_conv_sample = jnp.stack(cvs_l, axis=0)
    return (y_prompt, y_sample, new_k_prompt, new_v_prompt, new_logf_prompt, new_conv_prompt,
            new_k_sample, new_v_sample, new_logf_sample, new_conv_sample)


_drawn_inputs = setup_inputs


def setup_inputs(seed=0):
    import zlib

    import numpy as np

    out = dict(_drawn_inputs(seed))
    spreads = {}
    factors = {'norm_attn_g': 11.781,
     'norm_conv_g': 11.954,
     'b_router_group': 64.0,
     'b_router_expert': 33.192,
     'norm_final_g': 8.105,
     'norm_ffn_g': 5.068}
    for name, (base, spread) in spreads.items():
        noise = np.random.default_rng([zlib.crc32(name.encode()), seed]).standard_normal(out[name].shape)
        drawn = base * np.exp(spread * noise) if base else spread * noise
        out[name] = __import__('jax').numpy.asarray(drawn.astype(out[name].dtype))
    for name, factor in factors.items():
        out[name] = (out[name] * factor).astype(out[name].dtype)
    return out
```

```python
import concourse.bass as bass
from concourse import mybir
from contextlib import ExitStack

P = 128
D = 1024
KT = D // P
SEQ = 256
NB = 8
NQ = 16
PAST = 128
H = 8
HD = 64
A = H * HD
C = D - A
CT = C // P
NTOK = SEQ + NB * NQ
TT = NTOK // P
QT = SEQ // P
G = 4
EG = 8
E = G * EG
F = 256
FT = F // P
EPS = 1e-6
NEG = -1.0e30
SLOTS = 64
LIST = NTOK
PAIRS = 2 * NTOK
EMPTY = 3 * NTOK
RING = 4
MAXOV = PAIRS // SLOTS
OVROWS = 16 * -(-(MAXOV + 1) // 16)
LAST = E // RING - 1
CONSTS = 21
UNITS = 2 * H + NB


def build(nc, a, o):
    f32 = mybir.dt.float32
    i32 = mybir.dt.int32
    u32 = mybir.dt.uint32
    ALU = mybir.AluOpType
    ACT = mybir.ActivationFunctionType
    AX = mybir.AxisListType.X

    xn_dram = nc.dram_tensor("xn_rows", [NTOK, D], f32, kind="Internal").ap()
    pair_dram = nc.dram_tensor("pair_rows", [PAIRS, D], f32, kind="Internal").ap()
    table_dram = nc.dram_tensor("slot_table", [E * LIST, 1], i32, kind="Internal").ap()

    w_in = a["w_in"].rearrange("(p k) n -> p k n", k=KT)
    w_gu = a["w_expert_gate_up"].rearrange("e (p k) n -> e p (k n)", k=KT)
    w_dn = a["w_expert_down"].rearrange("e (j p) n -> e p j n", p=P)
    cols = {"q": 0, "k": A, "v": 2 * A, "f": 3 * A, "B": 3 * A + H, "C": 3 * A + H + C, "h": 3 * A + H + 2 * C}

    ctx = ExitStack()
    with ctx:
        def sb(name, shape, dt=f32):
            return ctx.enter_context(nc.sbuf_tensor(name, shape, dt))

        def sem(name):
            return ctx.enter_context(nc.semaphore(name))

        gu_ring = sb("gu_ring", [P, RING, KT * 2 * F])
        dn_ring = sb("dn_ring", [P, RING, FT * D])
        chunk = {
            "q": gu_ring[:, 0, :].rearrange("p (k n) -> p k n", k=KT),
            "k": gu_ring[:, 1, :].rearrange("p (k n) -> p k n", k=KT),
            "v": gu_ring[:, 2, :].rearrange("p (k n) -> p k n", k=KT),
            "B": gu_ring[:, 3, :].rearrange("p (k n) -> p k n", k=KT),
            "C": dn_ring[:, 0:2, :].rearrange("p r (k n) -> p (r k) n", n=C),
            "h": dn_ring[:, 2:4, :].rearrange("p r (k n) -> p (r k) n", n=C),
        }
        wo = [gu_ring[:, 0, :].rearrange("p (c n) -> p c n", c=CT),
              gu_ring[:, 1, :].rearrange("p (c n) -> p c n", c=CT)]

        X = sb("X", [P, TT, D])
        r_xs = sb("r_xs", [P, 4096])
        xs = r_xs[:, 0:TT * D].rearrange("p (t k q) -> p t k q", t=TT, k=KT)
        ck = [r_xs[:, 512 * i:512 * i + 512] for i in range(4)]
        cv = [r_xs[:, 2048 + 512 * i:2048 + 512 * i + 512] for i in range(4)]
        yp = [r_xs[:, 1024 * i:1024 * i + 1024] for i in range(4)]
        y_rows = [r_xs[0:SLOTS, 1024 * i:1024 * i + 1024] for i in range(2)]
        r_xT = sb("r_xT", [P, KT * NTOK])
        xT = r_xT[:, :].rearrange("p (k t) -> p k t", k=KT)
        x2T = r_xT[:, 0:TT * D].rearrange("p (t k q) -> p t k q", t=TT, k=KT)
        xg = [r_xT[0:SLOTS, 1024 * i:1024 * i + 1024] for i in range(2)]
        xgT = [r_xT[:, 2048 + 512 * i:2048 + 512 * i + KT * SLOTS].rearrange("p (k s) -> p k s", k=KT) for i in range(2)]
        yo = [r_xT[:, D * t:D * (t + 1)] for t in range(TT)]
        r_qz = sb("r_qz", [P, H * NTOK])
        qz = r_qz[:, 0:H * SEQ].rearrange("p (h t) -> p h t", h=H)
        qs = r_qz[:, H * SEQ:].rearrange("p (c b s q) -> p c b s q", c=CT, b=NB, s=2)
        xn2 = r_qz[:, 0:TT * D].rearrange("p (t d) -> p t d", t=TT)
        r_kT = sb("r_kT", [P, CT, NTOK])
        kT = r_kT
        glu = [r_kT[0:SLOTS, :, :].rearrange("p c t -> p (c t)")[:, 2 * F * i:2 * F * (i + 1)] for i in range(2)]
        V = sb("V", [P, TT, A])
        BT = sb("BT", [P, CT, NTOK])
        oB = sb("oB", [P, CT, NTOK])
        r_U = sb("r_U", [P, CT * (SEQ + 2 + NB * (NQ + 2))])
        Up = r_U[:, 0:CT * (SEQ + 2)].rearrange("p (c t) -> p c t", c=CT)
        Us = r_U[:, CT * (SEQ + 2):].rearrange("p (c b t) -> p c b t", c=CT, b=NB)
        sqB = r_U[:, 0:CT * NTOK].rearrange("p (c t) -> p c t", c=CT)
        sqA = BT
        oT = sb("oT", [P, CT, NTOK])
        r_kc = sb("r_kc", [P, 2, 512])
        krow = [r_kc[:, i, :] for i in range(2)]
        kc = [r_kc[:, i, :].rearrange("p (c s) -> p c s", c=CT) for i in range(2)]
        r_sc = sb("r_sc", [P, 512])
        scores = [r_sc[:, 256 * i:256 * (i + 1)] for i in range(2)]
        last_row = r_sc[0:2 + 2 * NB, :]
        r_pr = sb("r_pr", [P, 512])
        probs = [r_pr[:, 256 * i:256 * (i + 1)] for i in range(2)]
        small = r_pr[0:5 * CT, 0:P]
        pnorm = [sb(f"pnorm{i}", [P, 256]) for i in range(2)]
        pT = [sb(f"pT{i}", [P, 256]) for i in range(2)]
        tmpc = sb("tmpc", [P, NTOK])
        gbc = r_kc[:, :, :].rearrange("p i n -> p (i n)")

        ident = sb("ident", [P, P])
        ones = sb("ones", [P, P])
        t_le = sb("t_le", [P, P])
        t_lt = sb("t_lt", [P, P])
        t_gt = sb("t_gt", [P, P])
        t_str = sb("t_str", [P, P])
        causal = sb("causal", [P, P])
        causal_s = sb("causal_s", [P, NQ])
        iota_q = sb("iota_q", [P, NQ])
        iota_e = sb("iota_e", [P, E])
        tok_id = sb("tok_id", [P, TT])
        pid = sb("pid", [P, 1], i32)
        pmod_i = sb("pmod_i", [P, 1], i32)
        pmod = sb("pmod", [P, 1])
        same_q = sb("same_q", [P, NQ])
        of_stream = sb("of_stream", [P, NB])

        gmix = sb("gmix", [P, KT])
        smallT = sb("smallT", [P, 5 * CT])
        gA = smallT[:, 0:CT]
        gB = smallT[:, CT:2 * CT]
        cw = smallT[:, 2 * CT:5 * CT].rearrange("p (i c) -> p i c", i=3)
        state = krow[0][0:2 * NB, :]
        last = sb("last", [P, CT, 2 + 2 * NB])
        wf = sb("wf", [P, KT, H])
        bf = sb("bf", [P, H])
        wr = sb("wr", [P, KT, G + E])
        br = sb("br", [P, G + E])
        lfc = sb("lfc", [P, NB, H])
        lf = sb("lf", [P, TT, H])
        fa = sb("fa", [P, TT, H])
        fb = sb("fb", [P, TT, H])
        fz = sb("fz", [P, TT, H])
        cum = sb("cum", [P, TT, H])
        nc_p = sb("nc_p", [P, SEQ])
        lfn = sb("lfn", [P, H, NQ])
        lfx = [sb(f"lfx{i}", [P, H, NQ]) for i in range(2)]
        cmul = pT[0][:, 0:H * NQ].rearrange("p (h q) -> p h q", h=H)
        cq_s = sb("cq_s", [P, NB])
        nmax = sb("nmax", [P, 2])
        psum_ = sb("rowsum", [P, 2])
        rrec = sb("rrec", [P, 2])
        ss = sb("ss", [P, 6])
        nv = sb("nv", [P, 6])
        nln = sb("nln", [P, 6])
        nr0 = sb("nr0", [P, 6])
        nt = sb("nt", [P, 6])
        rs1 = sb("rs1", [P, TT])
        rs_ab = sb("rs_ab", [P, 6])
        rs2 = sb("rs2", [P, TT])
        rs3 = sb("rs3", [P, TT])
        taken = [0]

        def over_v(shape, dt=f32):
            n = 1
            for m in shape[1:]:
                n *= m
            ap = V_flat[0:shape[0], taken[0]:taken[0] + n]
            taken[0] += n + n % 2
            assert taken[0] <= TT * A
            if dt != f32:
                ap = ap.bitcast(dt)
            if len(shape) == 3:
                ap = ap.rearrange("p (a b) -> p a b", a=shape[1])
            if len(shape) == 4:
                ap = ap.rearrange("p (a b c) -> p a b c", a=shape[1], b=shape[2])
            return ap

        V_flat = V[:, :, :].rearrange("p t a -> p (t a)")
        lg = over_v([P, TT, 8 + E])
        top = over_v([P, TT, 8])
        topi = over_v([P, TT, 8], u32)
        gidx = over_v([P, TT])
        goh = over_v([P, TT, G])
        ge = over_v([P, TT, G])
        gs = over_v([P, TT])
        etop = over_v([P, TT, 8])
        etopi = over_v([P, TT, 8], u32)
        eid = over_v([P, TT, 2])
        oh = over_v([P, 2, TT, E])
        ohs = over_v([P, TT, E])
        rk = over_v([P, TT, E])
        cnt = over_v([P, E])
        ohr = over_v([P, TT, E])
        pos = over_v([P, 2, TT])
        posi = sb("posi", [P, 2, TT], u32)
        pairv = sb("pairv", [P, 2, TT], i32)
        wt = over_v([P, 2, TT])
        wd = over_v([P, TT])
        empty = tmpc[:, 0:E * LIST // P].bitcast(i32)
        tab = over_v([E, SLOTS], i32)
        tabf = over_v([E, SLOTS])
        slotf = over_v([SLOTS, E])
        sge = over_v([SLOTS, E])
        gat_i = over_v([SLOTS, E], u32)
        sca_i = over_v([SLOTS, E], u32)
        gidx_now = [sb(f"gidx_now{i}", [SLOTS, 1], u32) for i in range(2)]
        sidx_now = [sb(f"sidx_now{i}", [SLOTS, 1], u32) for i in range(2)]
        ovc = over_v([P, E])
        ovt = over_v([P, E])
        ovi = over_v([P, E])
        ovx = over_v([P, E])
        ovr = over_v([P, 4])
        ov_regs = sb("ov_regs", [1, 3 * OVROWS], i32)
        hT = over_v([P, FT, SLOTS])
        vtab = sb("vtab", [SLOTS, 1], i32)
        vtabf = sb("vtabf", [SLOTS, 2])

        banks = [ctx.enter_context(nc.psum_tensor(f"bank{i}", [P, 512], f32)) for i in range(8)]
        bT, bG, bS, bO = banks[0:2], banks[2:4], banks[4:6], banks[6:8]

        ld_x = [sem(f"ld_x{t}") for t in range(TT)]
        ld_chunk = {c: sem(f"ld_{c}") for c in "qkvBCh"}
        ld_wo = [sem("ld_woA"), sem("ld_woB")]
        ld_small = sem("ld_small")
        ld_rt = sem("ld_rt")
        ld_gain = sem("ld_gain")
        ld_ck = [sem(f"ld_ck{i}") for i in range(4)]
        ld_cv = [sem(f"ld_cv{i}") for i in range(4)]
        consts = sem("consts")
        act_chain = sem("act_chain")
        dve_chain = sem("dve_chain")
        ss1_done = sem("ss1_done")
        nv1_done = sem("nv1_done")
        nr1_done = sem("nr1_done")
        xs_done = sem("xs_done")
        t_full = sem("t_full")
        t_evac = sem("t_evac")
        g_full = sem("g_full")
        g_evac_act = sem("g_evac_act")
        g_evac_dve = sem("g_evac_dve")
        qz_zero = sem("qz_zero")
        f_full = sem("f_full")
        fz_done = sem("fz_done")
        sp_done = sem("sp_done")
        lf_done = sem("lf_done")
        lfx_done = sem("lfx_done")
        decay_full = sem("decay_full")
        decay_done = sem("decay_done")
        cmul_done = sem("cmul_done")
        cq_full = sem("cq_full")
        s_full = sem("s_full")
        s_evac = sem("s_evac")
        nmax_done = sem("nmax_done")
        exp_done = sem("exp_done")
        pn_done = sem("pn_done")
        pv_full = sem("pv_full")
        o_evac = sem("o_evac")
        conv_done = sem("conv_done")
        last_done = sem("last_done")
        sq_done = sem("sq_done")
        ssab_full = sem("ssab_full")
        nvab_done = sem("nvab_done")
        nrab_done = sem("nrab_done")
        gain_done = sem("gain_done")
        out_full = sem("out_full")
        outa_evac = sem("outa_evac")
        lg_evac = sem("lg_evac")
        x1_done = sem("x1_done")
        ss2_done = sem("ss2_done")
        nv2_done = sem("nv2_done")
        nr2_done = sem("nr2_done")
        xn2_done = sem("xn2_done")
        x2t_full = sem("x2t_full")
        x2t_evac = sem("x2t_evac")
        lg_full = sem("lg_full")
        gmax_done = sem("gmax_done")
        gexp_done = sem("gexp_done")
        oh_done = sem("oh_done")
        rk_full = sem("rk_full")
        pos_done = sem("pos_done")
        tabf_done = sem("tabf_done")
        slot_full = sem("slot_full")
        idx_done = sem("idx_done")
        ovr_done = sem("ovr_done")
        ovr_full = sem("ovr_full")
        ovr_regs = sem("ovr_regs")
        st_out = sem("st_out")
        st_v = sem("st_v")
        st_krow = [sem(f"st_krow{i}") for i in range(2)]
        st_empty = sem("st_empty")
        st_xn = sem("st_xn")
        st_table = sem("st_table")
        ld_tab = sem("ld_tab")
        ld_gu = [sem(f"ld_gu{i}") for i in range(RING)]
        ld_dn = [sem(f"ld_dn{i}") for i in range(RING)]
        gidx_set = sem("gidx_set")
        gathered = [sem(f"gathered{i}") for i in range(2)]
        sidx_set = sem("sidx_set")
        scattered = [sem(f"scattered{i}") for i in range(2)]
        xgt_full = sem("xgt_full")
        xgt_evac = sem("xgt_evac")
        gu_full = sem("gu_full")
        gexp = sem("gexp")
        glu_c = sem("glu_chain")
        glu_done = sem("glu_done")
        ht_full = sem("ht_full")
        ht_evac = sem("ht_evac")
        y_full = sem("y_full")
        y_evac_a = sem("y_evac_a")
        y_evac_d = sem("y_evac_d")
        xg_zero = sem("xg_zero")
        pe_paced = sem("pe_paced")
        pool_paced = sem("pool_paced")
        ov_w = sem("ov_w")
        ov_tab = sem("ov_tab")
        ov_idx = sem("ov_idx")
        ov_gat = sem("ov_gat")
        ov_xt = sem("ov_xt")
        ov_xe = sem("ov_xe")
        ov_gu = sem("ov_gu")
        ov_ex = sem("ov_ex")
        ov_c = sem("ov_chain")
        ov_glu = sem("ov_glu")
        ov_ht = sem("ov_ht")
        ov_he = sem("ov_he")
        ld_pair = [sem(f"ld_pair{i}") for i in range(4)]
        ss3_done = sem("ss3_done")
        y2_done = sem("y2_done")
        nv3_done = sem("nv3_done")
        nr3_done = sem("nr3_done")
        out_done = sem("out_done")
        st_y = sem("st_y")

        T_SMALL, T_STATE, T_X, T_K = 0, 1, 2, 2 + KT
        t_jobs = T_K + TT
        t_kc, t_p = {}, {}
        for n in range(UNITS + 3):
            if 2 * H <= n + 1 < UNITS:
                t_kc[n + 1 - 2 * H] = t_jobs
                t_jobs += 1
            if 0 <= n - 1 < UNITS:
                t_p[n - 1] = t_jobs
                t_jobs += 1
        T_LAST = t_jobs
        t_jobs += 1
        g_kinds = ["q"] * CT + ["k"] * CT + ["v"] * TT + ["C", "h", "B"] * CT
        G_FILL = 2 * CT + TT
        g_place = []
        na = nd = 0
        for kind in g_kinds:
            if kind == "h":
                nd += 1
                g_place.append((g_evac_dve, nd))
            else:
                na += 1
                g_place.append((g_evac_act, na))
        fill_at = {}
        for f in range(3 * CT):
            fill_at.setdefault(1 + (f * 20) // (3 * CT), []).append(G_FILL + f)

        def unit(n):
            return (n // QT, n % QT) if n < 2 * H else (None, n - 2 * H)

        block = ctx.enter_context(nc.Block())

        @block.sync
        def _(sp):
            for t in range(TT):
                sp.dma_start(X[:, t, :], a["x"][t * P:(t + 1) * P, :]).then_inc(ld_x[t], 16)
            for c in "qkvChB":
                sp.dma_start(chunk[c], w_in[:, :, cols[c]:cols[c] + 512]).then_inc(ld_chunk[c], 16)
            sp.wait_ge(t_full, T_X + KT)
            for b in range(4):
                sp.dma_start(ck[b], a["cache_k"][b]).then_inc(ld_ck[b], 16)
                sp.dma_start(cv[b], a["cache_v"][b]).then_inc(ld_cv[b], 16)
            for half, job in ((0, CT), (1, 2 * CT)):
                sp.wait_ge(g_full, job)
                sp.dma_start(wo[half], a["w_out"][half * A:(half + 1) * A, :].rearrange("(c p) n -> p c n", p=P)).then_inc(ld_wo[half], 16)
            for b in range(4, NB):
                sp.wait_ge(t_full, t_kc[b - 4] + 1)
                sp.dma_start(ck[b - 4], a["cache_k"][b]).then_inc(ld_ck[b - 4], 16)
                sp.wait_ge(pv_full, 2 * H + b - 4 + 1)
                sp.dma_start(cv[b - 4], a["cache_v"][b]).then_inc(ld_cv[b - 4], 16)
            sp.wait_ge(g_full, G_FILL + 3 * CT)
            for e in (2, 3):
                sp.dma_start(gu_ring[:, e, :], w_gu[e]).then_inc(ld_gu[e], 16)
            for e in range(RING):
                sp.dma_start(dn_ring[:, e, :].rearrange("p (j n) -> p j n", j=FT), w_dn[e]).then_inc(ld_dn[e], 16)
            sp.wait_ge(out_full, TT)
            for e in (0, 1):
                sp.dma_start(gu_ring[:, e, :], w_gu[e]).then_inc(ld_gu[e], 16)
            with sp.Fori(1, E // RING) as i:
                for u in range(RING):
                    sp.wait_ge(gu_full, i * RING + (u + 1 - RING))
                    sp.dma_start(gu_ring[:, u, :], w_gu[i * RING + u]).then_inc(ld_gu[u], 16)
                    sp.wait_ge(y_full, i * RING + (u + 1 - RING))
                    sp.dma_start(dn_ring[:, u, :].rearrange("p (j n) -> p j n", j=FT), w_dn[i * RING + u]).then_inc(ld_dn[u], 16)
            sp.wait_ge(ovr_regs, 1)
            sp.wait_ge(y_full, E)
            n_ov = sp.value_load(ov_regs[0:1, 2 * OVROWS:2 * OVROWS + 1], min_val=0, max_val=MAXOV)
            with sp.If(n_ov > 0):
                with sp.Fori(0, n_ov) as i:
                    sp.wait_ge(y_full, i + E)
                    e = sp.value_load(ov_regs[0:1, bass.ds(i, 1)], min_val=0, max_val=E - 1)
                    sp.dma_start(gu_ring[:, 0, :], w_gu[e]).then_inc(ov_w, 16)
                    sp.dma_start(dn_ring[:, 0, :].rearrange("p (j n) -> p j n", j=FT), w_dn[e]).then_inc(ov_w, 16)

        @block.gpsimd
        def _(pool):
            g = nc.gpsimd
            g.memset(ident[:, :], 0.0).then_inc(consts, 1)
            g.memset(ones[:, :], 1.0).then_inc(consts, 1)
            pool.wait_ge(consts, 2)
            g.affine_select(out=ident[:, :], in_=ident[:, :], compare_op=ALU.not_equal, fill=1.0, base=0,
                            pattern=[[-1, P]], channel_multiplier=1).then_inc(consts, 1)
            g.affine_select(out=t_le[:, :], in_=ones[:, :], compare_op=ALU.is_ge, fill=0.0, base=0,
                            pattern=[[1, P]], channel_multiplier=-1).then_inc(consts, 1)
            g.affine_select(out=t_lt[:, :], in_=ones[:, :], compare_op=ALU.is_ge, fill=0.0, base=-1,
                            pattern=[[1, P]], channel_multiplier=-1).then_inc(consts, 1)
            g.affine_select(out=t_gt[:, :], in_=ones[:, :], compare_op=ALU.is_ge, fill=0.0, base=-1,
                            pattern=[[-1, P]], channel_multiplier=1).then_inc(consts, 1)
            g.memset(causal[:, :], 0.0).then_inc(consts, 1)
            pool.wait_ge(consts, 7)
            g.affine_select(out=t_str[:, :].rearrange("p (b q) -> p b q", b=NB),
                            in_=t_le[:, :].rearrange("p (b q) -> p b q", b=NB), compare_op=ALU.is_ge, fill=0.0,
                            base=0, pattern=[[-NQ, NB], [0, NQ]], channel_multiplier=1).then_inc(consts, 1)
            g.affine_select(out=causal[:, :], in_=causal[:, :], compare_op=ALU.is_ge, fill=NEG, base=0,
                            pattern=[[-1, P]], channel_multiplier=1).then_inc(consts, 1)
            g.affine_select(out=of_stream[:, :], in_=ones[:, 0:NB], compare_op=ALU.is_ge, fill=0.0, base=0,
                            pattern=[[-NQ, NB]], channel_multiplier=1).then_inc(consts, 1)
            pool.wait_ge(consts, 10)
            g.affine_select(out=of_stream[:, :], in_=of_stream[:, :], compare_op=ALU.is_ge, fill=0.0, base=NQ - 1,
                            pattern=[[NQ, NB]], channel_multiplier=-1).then_inc(consts, 1)
            g.iota(iota_q[:, :], [[1, NQ]], base=0, channel_multiplier=0,
                   allow_small_or_imprecise_dtypes=True).then_inc(consts, 1)
            g.iota(iota_e[:, :], [[1, E]], base=0, channel_multiplier=0,
                   allow_small_or_imprecise_dtypes=True).then_inc(consts, 1)
            g.iota(tok_id[:, :], [[P, TT]], base=0, channel_multiplier=1,
                   allow_small_or_imprecise_dtypes=True).then_inc(consts, 1)
            g.iota(pid[:, :], [[0, 1]], base=0, channel_multiplier=1).then_inc(consts, 1)
            g.iota(pairv[:, :, :].rearrange("p c t -> p (c t)"), [[P, 2 * TT]], base=0,
                   channel_multiplier=1).then_inc(consts, 1)
            g.memset(nc_p[:, :], 0.0).then_inc(consts, 1)
            g.memset(empty, EMPTY).then_inc(consts, 1)
            g.memset(r_qz[:, :], 0.0).then_inc(qz_zero, 1)
            g.memset(pnorm[0][:, :], 0.0).then_inc(consts, 1)
            g.memset(pnorm[1][:, :], 0.0).then_inc(consts, 1)
            g.memset(Up[:, :, 0:2], 0.0).then_inc(consts, 1)
            pool.wait_ge(consts, CONSTS)
            pool.dma_start(table_dram.rearrange("(p n) o -> p (n o)", p=P), empty).then_inc(st_empty, 16)
            for t in range(TT):
                kdst = o["k_p"][t * P:(t + 1) * P, :] if t < QT else o["k_s"]
                pool.wait_ge(t_evac, T_K + t + 1)
                pool.dma_start(kdst, krow[t % 2]).then_inc(st_krow[t % 2], 16)
            pool.wait_ge(lf_done, 1)
            pool.dma_start(o["lf_p"].rearrange("(t p) h -> p t h", p=P), lf[:, 0:QT, :]).then_inc(st_out, 16)
            pool.dma_start(o["lf_s"], lf[:, QT, :]).then_inc(st_out, 16)
            for t in range(TT):
                vdst = o["v_p"][t * P:(t + 1) * P, :] if t < QT else o["v_s"]
                pool.wait_ge(*g_place[2 * CT + t])
                pool.dma_start(vdst, V[:, t, :]).then_inc(st_v, 16)
            for b in range(NB):
                if b == 0:
                    pool.wait_ge(ld_small, 8 * 16)
                if b >= 2:
                    pool.wait_ge(s_full, 2 * H + b - 1)
                g.tensor_copy(lfx[b % 2][:, :, :], lfc[:, b, :].unsqueeze(2).to_broadcast([P, H, NQ])).then_inc(lfx_done, 1)
            pool.wait_ge(t_evac, T_LAST + 1)
            pool.dma_start(o["conv_p"], last_row[0:2, :]).then_inc(st_out, 16)
            pool.dma_start(o["conv_s"], last_row[2:2 + 2 * NB, :]).then_inc(st_out, 16)
            for t in range(TT):
                pool.wait_ge(xn2_done, t + 1)
                pool.dma_start(xn_dram[t * P:(t + 1) * P, :], xn2[:, t, :]).then_inc(st_xn, 16)
            pool.wait_ge(st_empty, 16)
            pool.wait_ge(pos_done, 1)
            for c in range(2):
                for t in range(TT):
                    pool.indirect_dma_start(table_dram, bass.IndirectOffsetOnAxis(posi[:, c, t:t + 1], 0),
                                            pairv[:, c, t:t + 1], None).then_inc(st_table, 16)
            pool.wait_ge(st_table, 6 * 16)
            pool.dma_start(tab[:, :], table_dram.rearrange("(e l) o -> e (l o)", e=E)[:, 0:SLOTS]).then_inc(ld_tab, 16)
            pool.wait_ge(lg_full, TT)
            for i in range(2):
                g.memset(xg[i], 0.0).then_inc(xg_zero, 1)
            pool.wait_ge(xg_zero, 2)
            pool.wait_ge(idx_done, 1)
            pool.wait_ge(st_xn, TT * 16)

            def gather(e, buf):
                g.tensor_copy(gidx_now[buf][:, :], gat_i[:, bass.ds(e, 1)]).then_inc(gidx_set, 1)
                pool.wait_ge(gidx_set, e + 1)
                pool.sem_inc(pool_paced, 1)
                pool.indirect_dma_start(xg[buf], None, xn_dram,
                                        bass.IndirectOffsetOnAxis(gidx_now[buf][:, 0:1], 0),
                                        bounds_check=NTOK - 1, oob_is_err=False).then_inc(gathered[buf], 16)

            def step(e, u, i, first, has_two_more):
                buf = u % 2
                if has_two_more:
                    pool.wait_ge(xgt_full, e + 1)
                    gather(e + 2, buf)
                if not (first and u < 2):
                    pool.wait_ge(scattered[buf], (i * (RING // 2) + u // 2) * 16)
                g.tensor_copy(sidx_now[buf][:, :], sca_i[:, bass.ds(e, 1)]).then_inc(sidx_set, 1)
                pool.wait_ge(sidx_set, e + 1)
                pool.wait_ge(y_evac_a, e + 1)
                pool.wait_ge(y_evac_d, e + 1)
                pool.sem_inc(pool_paced, 1)
                pool.indirect_dma_start(pair_dram, bass.IndirectOffsetOnAxis(sidx_now[buf][:, 0:1], 0),
                                        y_rows[buf], None,
                                        bounds_check=PAIRS - 1, oob_is_err=False).then_inc(scattered[buf], 16)

            gather(0, 0)
            gather(1, 1)
            for u in range(RING):
                step(u, u, 0, True, True)
            with pool.Fori(1, LAST) as i:
                for u in range(RING):
                    step(i * RING + u, u, i, False, True)
            for u in range(RING):
                step(LAST * RING + u, u, LAST, False, u < RING - 2)
            pool.wait_ge(scattered[0], E // 2 * 16)
            pool.wait_ge(scattered[1], E // 2 * 16)
            pool.wait_ge(ovr_regs, 1)
            n_ov = pool.value_load(ov_regs[0:1, 2 * OVROWS:2 * OVROWS + 1], min_val=0, max_val=MAXOV)
            with pool.If(n_ov > 0):
                with pool.Fori(0, n_ov) as i:
                    row = pool.value_load(ov_regs[0:1, bass.ds(i + OVROWS, 1)], min_val=0, max_val=E * LIST - SLOTS)
                    pool.dma_start(vtab[:, :], table_dram[bass.ds(row, SLOTS), :]).then_inc(ov_tab, 16)
                    pool.wait_ge(ov_idx, i + 1)
                    pool.sem_inc(pool_paced, 1)
                    pool.indirect_dma_start(xg[0], None, xn_dram,
                                            bass.IndirectOffsetOnAxis(gidx_now[0][:, 0:1], 0),
                                            bounds_check=NTOK - 1, oob_is_err=False).then_inc(ov_gat, 16)
                    pool.wait_ge(y_evac_a, i + (E + 1))
                    pool.wait_ge(y_evac_d, i + (E + 1))
                    pool.sem_inc(pool_paced, 1)
                    pool.indirect_dma_start(pair_dram, bass.IndirectOffsetOnAxis(sidx_now[0][:, 0:1], 0),
                                            y_rows[0], None,
                                            bounds_check=PAIRS - 1, oob_is_err=False).then_inc(scattered[0], 16)
                    pool.wait_ge(scattered[0], i * 16 + (E // 2 * 16 + 16))
            for t in range(TT):
                for c in range(2):
                    if t >= 2:
                        pool.wait_ge(y2_done, t - 1)
                    pool.dma_start(yp[2 * (t % 2) + c], pair_dram[c * NTOK + t * P:c * NTOK + (t + 1) * P, :])\
                        .then_inc(ld_pair[2 * (t % 2) + c], 16)
            pool.wait_ge(st_krow[0], 32)
            pool.wait_ge(st_krow[1], 16)
            pool.wait_ge(st_out, 16 * 4)

        @block.scalar
        def _(act):
            s = nc.scalar
            chain = [0]

            def link(ins):
                chain[0] += 1
                ins.then_inc(act_chain, 1)
                act.wait_ge(act_chain, chain[0])

            act.dma_start(gmix[:, :], a["norm_mix_g"].rearrange("(p k) -> p k", k=KT)).then_inc(ld_small, 16)
            act.dma_start(small[0:CT, :], a["norm_attn_g"].rearrange("(c p) -> c p", p=P)).then_inc(ld_small, 16)
            act.dma_start(small[CT:2 * CT, :], a["norm_conv_g"].rearrange("(c p) -> c p", p=P)).then_inc(ld_small, 16)
            act.dma_start(small[2 * CT:5 * CT, :], a["conv_w"].rearrange("i (c p) -> (i c) p", p=P)).then_inc(ld_small, 16)
            act.dma_start(state, a["state_conv"]).then_inc(ld_small, 16)
            act.dma_start(bf[:, :], a["b_forget"].partition_broadcast(P)).then_inc(ld_small, 16)
            act.dma_start(wf[:, :, :], w_in[:, :, cols["f"]:cols["f"] + H]).then_inc(ld_small, 16)
            act.dma_start(lfc[:, :, :], a["cache_logf"].rearrange("b s h -> s b h")).then_inc(ld_small, 16)
            act.dma_start(wr[:, :, 0:G], a["w_router_group"].rearrange("(p k) g -> p k g", k=KT)).then_inc(ld_rt, 16)
            for gi in range(G):
                act.dma_start(wr[:, :, G + gi * EG:G + (gi + 1) * EG],
                              a["w_router_expert"][gi].rearrange("(p k) e -> p k e", k=KT)).then_inc(ld_rt, 16)
            act.dma_start(br[:, 0:G], a["b_router_group"].partition_broadcast(P)).then_inc(ld_rt, 16)
            act.dma_start(br[:, G:G + E], a["b_router_expert"].partition_broadcast(P)).then_inc(ld_rt, 16)

            for t in range(TT):
                act.wait_ge(ld_x[t], 16)
                s.activation(xs[:, t, :, :].rearrange("p k q -> p (k q)"), X[:, t, :], ACT.Square,
                             accum_out=ss[:, t:t + 1]).then_inc(ss1_done, 1)
            act.wait_ge(nv1_done, 1)
            link(s.activation(nln[:, 0:TT], nv[:, 0:TT], ACT.Ln))
            s.activation(nr0[:, 0:TT], nln[:, 0:TT], ACT.Exp, scale=-0.5).then_inc(nr1_done, 1)

            act.wait_ge(ld_small, 8 * 16)
            act.wait_ge(t_full, T_SMALL + 1)
            s.activation(smallT[:, :], bT[T_SMALL % 2][:, 0:5 * CT], ACT.Copy).then_inc(t_evac, 1)
            act.wait_ge(t_full, T_STATE + 1)
            s.activation(Us[:, :, :, 0:2], bT[T_STATE % 2][:, 0:CT * 2 * NB].rearrange("p (c b i) -> p c b i", c=CT, b=NB),
                         ACT.Copy).then_inc(t_evac, 1)
            for k in range(KT):
                act.wait_ge(t_full, T_X + k + 1)
                s.activation(xT[:, k, :], bT[(T_X + k) % 2][:, 0:NTOK], ACT.Copy, scale=gmix[:, k:k + 1]).then_inc(t_evac, 1)

            act.wait_ge(fz_done, 1)
            link(s.activation(fb[:, :, :], fa[:, :, :], ACT.Exp, scale=-1.0))
            s.activation(fa[:, :, :], fb[:, :, :], ACT.Ln, bias=1.0).then_inc(sp_done, 1)

            def g_copy(j):
                kind, bank = g_kinds[j], bG[j % 2]
                act.wait_ge(g_full, j + 1)
                if kind == "q":
                    if j == 0:
                        act.wait_ge(qz_zero, 1)
                    for half in range(2):
                        rows = slice(half * HD, (half + 1) * HD)
                        s.activation(qz[rows, 2 * j + half, :], bank[rows, 0:SEQ], ACT.Copy, scale=HD ** -0.5)
                        ins = s.activation(qs[rows, j, :, half, :], bank[rows, SEQ:NTOK].rearrange("p (b q) -> p b q", b=NB),
                                           ACT.Copy, scale=HD ** -0.5)
                elif kind == "k":
                    ins = s.activation(kT[:, j - CT, :], bank[:, 0:NTOK], ACT.Copy)
                elif kind == "v":
                    ins = s.activation(V[:, j - 2 * CT, :], bank[:, :], ACT.Copy)
                else:
                    ct = (j - G_FILL) // 3
                    dst = oB if kind == "C" else BT
                    ins = s.activation(dst[:, ct, :], bank[:, 0:NTOK], ACT.Copy)
                ins.then_inc(g_evac_act, 1)

            for j in range(2 * CT):
                g_copy(j)
            for t in range(TT):
                act.wait_ge(t_full, T_K + t + 1)
                if t >= 2:
                    act.wait_ge(st_krow[t % 2], 16)
                s.activation(krow[t % 2], bT[(T_K + t) % 2][:, :], ACT.Copy).then_inc(t_evac, 1)
            for t in range(TT):
                g_copy(2 * CT + t)

            for n in range(UNITS + 3):
                if 2 * H <= n + 1 < UNITS:
                    b = n + 1 - 2 * H
                    j = t_kc[b]
                    act.wait_ge(t_full, j + 1)
                    if b < 2:
                        act.wait_ge(st_krow[b], 32 if b == 0 else 16)
                    if b >= 2:
                        act.wait_ge(s_full, 2 * H + b - 2 + 1)
                    s.activation(kc[b % 2], bT[j % 2][:, :].rearrange("p (c s) -> p c s", c=CT), ACT.Copy).then_inc(t_evac, 1)
                if n < UNITS:
                    hd, q = unit(n)
                    w = PAST + NQ if hd is None else (q + 1) * P
                    act.wait_ge(nmax_done, n + 1)
                    if n >= 2:
                        act.wait_ge(pn_done, n - 1)
                    s.activation(probs[n % 2][:, 0:w], scores[n % 2][:, 0:w], ACT.Exp, bias=nmax[:, n % 2:n % 2 + 1],
                                 accum_out=psum_[:, n % 2:n % 2 + 1]).then_inc(exp_done, 1)
                for j in fill_at.get(n, []):
                    if g_kinds[j] != "h":
                        g_copy(j)
                if 0 <= n - 1 < UNITS:
                    m = n - 1
                    hd, q = unit(m)
                    w = 256 if hd is None else (q + 1) * P
                    act.wait_ge(t_full, t_p[m] + 1)
                    if m >= 2:
                        act.wait_ge(pv_full, m - 1)
                    s.activation(pT[m % 2][:, 0:w], bT[t_p[m] % 2][:, 0:w], ACT.Copy).then_inc(t_evac, 1)

            act.wait_ge(s_full, UNITS)
            act.dma_start(gbc, a["norm_ffn_g"].partition_broadcast(P)).then_inc(ld_gain, 16)
            act.wait_ge(conv_done, CT)
            s.activation(sqB[:, :, :], oB[:, :, :], ACT.Square).then_inc(sq_done, 1)
            act.wait_ge(o_evac, UNITS)
            s.activation(sqA[:, :, :], oT[:, :, :], ACT.Square).then_inc(sq_done, 1)
            act.wait_ge(sq_done, 2)
            for ct in range(CT):
                s.activation(oB[:, ct, :], oB[:, ct, :], ACT.Copy, scale=gB[:, ct:ct + 1]).then_inc(gain_done, 1)
            for ct in range(CT):
                s.activation(oT[:, ct, :], oT[:, ct, :], ACT.Copy, scale=gA[:, ct:ct + 1]).then_inc(gain_done, 1)
            act.wait_ge(t_full, T_LAST + 1)
            s.activation(last_row, bT[T_LAST % 2][0:2 + 2 * NB, :], ACT.Copy).then_inc(t_evac, 1)
            act.wait_ge(nvab_done, 1)
            link(s.activation(nln[:, 0:6], nv[:, 0:6], ACT.Ln))
            s.activation(nr0[:, 0:6], nln[:, 0:6], ACT.Exp, scale=-0.5).then_inc(nrab_done, 1)

            for t in range(TT):
                act.wait_ge(x1_done, t + 1)
                s.activation(xn2[:, t, :], X[:, t, :], ACT.Square, accum_out=ss[:, t:t + 1]).then_inc(ss2_done, 1)
                act.wait_ge(nv2_done, t + 1)
                link(s.activation(nln[:, t:t + 1], nv[:, t:t + 1], ACT.Ln))
                s.activation(nr0[:, t:t + 1], nln[:, t:t + 1], ACT.Exp, scale=-0.5).then_inc(nr2_done, 1)
                for half in range(2):
                    act.wait_ge(x2t_full, 2 * t + half + 1)
                    s.activation(x2T[:, t, 4 * half:4 * half + 4, :], bT[half][:, :].rearrange("p (k q) -> p k q", k=4),
                                 ACT.Copy).then_inc(x2t_evac, 1)
            act.wait_ge(xn2_done, TT)
            act.dma_start(gbc, a["norm_final_g"].partition_broadcast(P)).then_inc(ld_gain, 16)
            act.wait_ge(gmax_done, 1)
            s.activation(ge[:, :, :], ge[:, :, :], ACT.Exp).then_inc(gexp_done, 1)
            act.wait_ge(gmax_done, 2)
            s.activation(wd[:, :], wd[:, :], ACT.Exp).then_inc(gexp_done, 1)

            def rows_evac(e, buf, first):
                act.wait_ge(xgt_full, e + 1)
                if not first:
                    act.wait_ge(gu_full, e - 1)
                s.activation(xgT[buf], bT[buf][:, 0:KT * SLOTS].rearrange("p (k q) -> p k q", k=KT), ACT.Copy).then_inc(xgt_evac, 1)

            def gate_exp(e, buf, first):
                act.wait_ge(gu_full, e + 1)
                if not first:
                    act.wait_ge(glu_done, e - 1)
                s.activation(glu[buf][:, 0:F], bG[buf][0:SLOTS, 0:F], ACT.Exp, scale=-1.0).then_inc(gexp, 1)

            def step(e, u, i, first, has_next):
                if has_next:
                    rows_evac(e + 1, (u + 1) % 2, first and u == 0)
                act.wait_ge(ht_full, e + 1)
                if not (first and u == 0):
                    act.wait_ge(y_full, e)
                s.activation(hT[:, :, :], bS[0][:, 0:FT * SLOTS].rearrange("p (j q) -> p j q", j=FT), ACT.Copy).then_inc(ht_evac, 1)
                if has_next:
                    gate_exp(e + 1, (u + 1) % 2, first and u == 0)
                act.wait_ge(y_full, e + 1)
                if not (first and u < 2):
                    act.wait_ge(scattered[u % 2], (i * (RING // 2) + u // 2) * 16)
                s.activation(y_rows[u % 2][:, 0:512], bO[0][0:SLOTS, :], ACT.Copy).then_inc(y_evac_a, 1)

            rows_evac(0, 0, True)
            gate_exp(0, 0, True)
            for u in range(RING):
                step(u, u, 0, True, True)
            with act.Fori(1, LAST) as i:
                for u in range(RING):
                    step(i * RING + u, u, i, False, True)
            for u in range(RING):
                step(LAST * RING + u, u, LAST, False, u < RING - 1)
            act.wait_ge(ovr_regs, 1)
            n_ov = act.value_load(ov_regs[0:1, 2 * OVROWS:2 * OVROWS + 1], min_val=0, max_val=MAXOV)
            with act.If(n_ov > 0):
                with act.Fori(0, n_ov) as i:
                    act.wait_ge(ov_xt, i + 1)
                    s.activation(xgT[0], bT[0][:, 0:KT * SLOTS].rearrange("p (k q) -> p k q", k=KT), ACT.Copy).then_inc(ov_xe, 1)
                    act.wait_ge(ov_gu, i + 1)
                    s.activation(glu[0][:, 0:F], bG[0][0:SLOTS, 0:F], ACT.Exp, scale=-1.0).then_inc(ov_ex, 1)
                    act.wait_ge(ov_ht, i + 1)
                    s.activation(hT[:, :, :], bS[0][:, 0:FT * SLOTS].rearrange("p (j q) -> p j q", j=FT), ACT.Copy).then_inc(ov_he, 1)
                    act.wait_ge(y_full, i + (E + 1))
                    act.wait_ge(scattered[0], i * 16 + E // 2 * 16)
                    s.activation(y_rows[0][:, 0:512], bO[0][0:SLOTS, :], ACT.Copy).then_inc(y_evac_a, 1)
            for t in range(TT):
                act.wait_ge(y2_done, t + 1)
                s.activation(yo[t], X[:, t, :], ACT.Square, accum_out=ss[:, t:t + 1]).then_inc(ss3_done, 1)
                act.wait_ge(nv3_done, t + 1)
                link(s.activation(nln[:, t:t + 1], nv[:, t:t + 1], ACT.Ln))
                s.activation(nr0[:, t:t + 1], nln[:, t:t + 1], ACT.Exp, scale=-0.5).then_inc(nr3_done, 1)
                act.wait_ge(out_done, t + 1)
                act.dma_start(o["y_p"][t * P:(t + 1) * P, :] if t < QT else o["y_s"], yo[t]).then_inc(st_y, 16)
            act.wait_ge(st_y, 16 * TT)

        @block.vector
        def _(dve):
            v = nc.vector
            chain = [0]

            def link(ins):
                chain[0] += 1
                ins.then_inc(dve_chain, 1)
                dve.wait_ge(dve_chain, chain[0])

            def inv_sqrt(out, n0, n1, done, count):
                dve.wait_ge(done, count)
                link(v.tensor_tensor(nt[:, n0:n1], nr0[:, n0:n1], nr0[:, n0:n1], ALU.mult))
                link(v.tensor_tensor(nt[:, n0:n1], nt[:, n0:n1], nv[:, n0:n1], ALU.mult))
                link(v.tensor_scalar(nt[:, n0:n1], nt[:, n0:n1], -0.5, 1.5, ALU.mult, ALU.add))
                link(v.tensor_tensor(out, nt[:, n0:n1], nr0[:, n0:n1], ALU.mult))

            dve.wait_ge(consts, CONSTS)
            link(v.tensor_single_scalar(pmod_i[:, :], pid[:, :], NQ - 1, ALU.bitwise_and))
            link(v.tensor_copy(pmod[:, :], pmod_i[:, :]))
            link(v.tensor_scalar(causal_s[:, :], iota_q[:, :], pmod[:, 0:1], NEG, ALU.is_gt, ALU.mult))
            link(v.tensor_scalar(same_q[:, :], iota_q[:, :], pmod[:, 0:1], None, ALU.is_equal))

            dve.wait_ge(ss1_done, TT)
            v.tensor_scalar(nv[:, 0:TT], ss[:, 0:TT], 1.0 / D, EPS, ALU.mult, ALU.add).then_inc(nv1_done, 1)
            inv_sqrt(rs1[:, :], 0, TT, nr1_done, 1)
            for t in range(TT):
                v.tensor_scalar(xs[:, t, :, :], X[:, t, :].rearrange("p (q k) -> p k q", k=KT), rs1[:, t:t + 1], None,
                                ALU.mult).then_inc(xs_done, 1)

            dve.wait_ge(ld_small, 8 * 16)
            dve.wait_ge(f_full, 1)
            link(v.tensor_tensor(fz[:, :, :], bS[0][:, 0:TT * H].rearrange("p (t h) -> p t h", t=TT),
                                 bf[:, :].unsqueeze(1).to_broadcast([P, TT, H]), ALU.add))
            v.scalar_tensor_tensor(fa[:, :, :], fz[:, :, :], -1.0, fz[:, :, :], ALU.mult, ALU.max).then_inc(fz_done, 1)
            dve.wait_ge(sp_done, 1)
            v.scalar_tensor_tensor(lf[:, :, :], fz[:, :, :], 0.0, fa[:, :, :], ALU.min, ALU.subtract).then_inc(lf_done, 1)
            dve.wait_ge(decay_full, 1)
            link(v.tensor_copy(cum[:, :, :], bS[1][:, 0:TT * H].rearrange("p (t h) -> p t h", t=TT)))
            v.tensor_single_scalar(nc_p[0:H, :], bS[1][0:H, 32:32 + SEQ], -1.0, ALU.mult)
            v.tensor_single_scalar(lfn[:, :, :], lf[:, QT, :].unsqueeze(2).to_broadcast([P, H, NQ]), -1.0, ALU.mult)
            v.tensor_tensor(cmul[:, :, :], same_q[:, :].unsqueeze(1).to_broadcast([P, H, NQ]),
                            cum[:, QT, :].unsqueeze(2).to_broadcast([P, H, NQ]), ALU.mult).then_inc(cmul_done, 1)
            dve.wait_ge(cq_full, 1)
            v.tensor_copy(cq_s[:, :], bS[0][:, 0:NB]).then_inc(decay_done, 1)
            dve.wait_ge(decay_done, 1)

            def softmax_max(n):
                hd, q = unit(n)
                sc, bank = scores[n % 2], bS[n % 2]
                dve.wait_ge(s_full, n + 1)
                if n >= 2:
                    dve.wait_ge(exp_done, n - 1)
                if hd is None:
                    cq = cq_s[:, q:q + 1]
                    v.tensor_scalar(sc[:, 0:PAST], bank[:, 0:PAST], cq, None, ALU.add)
                    ins = v.scalar_tensor_tensor(sc[:, PAST:PAST + NQ], bank[:, PAST:PAST + NQ], cq, causal_s[:, :], ALU.add, ALU.add)
                    w = PAST + NQ
                else:
                    cq = cum[:, q, hd:hd + 1]
                    if q:
                        v.tensor_scalar(sc[:, 0:P], bank[:, 0:P], cq, None, ALU.add)
                    ins = v.scalar_tensor_tensor(sc[:, q * P:(q + 1) * P], bank[:, q * P:(q + 1) * P], cq, causal[:, :], ALU.add, ALU.add)
                    w = (q + 1) * P
                ins.then_inc(s_evac, 1)
                dve.wait_ge(s_evac, n + 1)
                v.reduce_max(nmax[:, n % 2:n % 2 + 1], sc[:, 0:w], AX, negate=True).then_inc(nmax_done, 1)

            def softmax_norm(n):
                hd, q = unit(n)
                r = rrec[:, n % 2:n % 2 + 1]
                dve.wait_ge(exp_done, n + 1)
                link(v.reciprocal(r, psum_[:, n % 2:n % 2 + 1]))
                if n >= 2:
                    dve.wait_ge(t_full, t_p[n - 2] + 1)
                if hd is None:
                    link(v.memset(pnorm[n % 2][:, PAST:PAST + P], 0.0))
                    v.tensor_scalar(pnorm[n % 2][:, 0:PAST], probs[n % 2][:, 0:PAST], r, None, ALU.mult)
                    v.tensor_scalar(pnorm[n % 2][:, PAST + NQ * q:PAST + NQ * (q + 1)], probs[n % 2][:, PAST:PAST + NQ],
                                    r, None, ALU.mult).then_inc(pn_done, 1)
                else:
                    w = (q + 1) * P
                    v.tensor_scalar(pnorm[n % 2][:, 0:w], probs[n % 2][:, 0:w], r, None, ALU.mult).then_inc(pn_done, 1)

            def out_evac_unit(n):
                hd, q = unit(n)
                bank = bO[n % 2]
                dve.wait_ge(pv_full, n + 1)
                if hd is None:
                    for half in range(2):
                        rows = slice(half * HD, (half + 1) * HD)
                        src = bank[rows, 0:CT * 2 * NQ].rearrange("p (c s q) -> p c s q", c=CT, s=2)[:, :, half, :]
                        ins = v.tensor_copy(oT[rows, :, SEQ + q * NQ:SEQ + (q + 1) * NQ], src)
                else:
                    rows = slice((hd % 2) * HD, (hd % 2 + 1) * HD)
                    ins = v.tensor_copy(oT[rows, hd // 2, q * P:(q + 1) * P], bank[rows, 0:P])
                ins.then_inc(o_evac, 1)

            def conv_in(j):
                ct = (j - G_FILL) // 3
                bank = bG[j % 2]
                dve.wait_ge(*g_place[j - 1])
                dve.wait_ge(g_full, j + 1)
                v.tensor_tensor(Up[:, ct, 2:2 + SEQ], bank[:, 0:SEQ], oB[:, ct, 0:SEQ], ALU.mult)
                v.tensor_tensor(Us[:, ct, :, 2:2 + NQ], bank[:, SEQ:NTOK].rearrange("p (b q) -> p b q", b=NB),
                                oB[:, ct, SEQ:NTOK].rearrange("p (b q) -> p b q", b=NB), ALU.mult).then_inc(g_evac_dve, 1)
                dve.wait_ge(g_evac_dve, ct + 1)
                v.tensor_copy(last[:, ct, 0:2], Up[:, ct, SEQ:SEQ + 2])
                v.tensor_copy(last[:, ct, 2:2 + 2 * NB].rearrange("p (b i) -> p b i", b=NB), Us[:, ct, :, NQ:NQ + 2])\
                    .then_inc(last_done, 1)

            def conv(ct):
                dve.wait_ge(*g_place[G_FILL + 3 * ct + 2])
                tp = tmpc[:, 0:SEQ]
                ts = tmpc[:, SEQ:NTOK].rearrange("p (b q) -> p b q", b=NB)
                w = [cw[:, i, ct:ct + 1] for i in range(3)]
                v.tensor_scalar(tp, Up[:, ct, 0:SEQ], w[0], None, ALU.mult)
                link(v.tensor_scalar(ts, Us[:, ct, :, 0:NQ], w[0], None, ALU.mult))
                for i in (1, 2):
                    v.scalar_tensor_tensor(tp, Up[:, ct, i:i + SEQ], w[i], tp, ALU.mult, ALU.add)
                    link(v.scalar_tensor_tensor(ts, Us[:, ct, :, i:i + NQ], w[i], ts, ALU.mult, ALU.add))
                v.tensor_tensor(oB[:, ct, :], tmpc[:, :], BT[:, ct, :], ALU.mult).then_inc(conv_done, 1)

            dve.wait_ge(st_empty, 16)
            ready = []
            for n in range(UNITS + 3):
                if 0 <= n - 1 < UNITS:
                    softmax_norm(n - 1)
                if n < UNITS:
                    softmax_max(n)
                for ct in ready:
                    conv(ct)
                ready = []
                for j in fill_at.get(n, []):
                    if g_kinds[j] == "h":
                        conv_in(j)
                    if g_kinds[j] == "B":
                        ready.append((j - G_FILL) // 3)
                if 0 <= n - 3 < UNITS:
                    out_evac_unit(n - 3)

            dve.wait_ge(ssab_full, 1)
            v.tensor_scalar(nv[:, 0:6], bT[0][:, 0:6], 1.0 / A, EPS, ALU.mult, ALU.add).then_inc(nvab_done, 1)
            inv_sqrt(rs_ab[:, :], 0, 6, nrab_done, 1)
            dve.wait_ge(st_v, 16 * TT)
            link(v.memset(lg[:, :, 0:8], NEG))
            for t in range(TT):
                bB = bG if t % 2 == 0 else bO
                dve.wait_ge(out_full, t + 1)
                for j in range(2):
                    cs = slice(512 * j, 512 * j + 512)
                    ins = v.scalar_tensor_tensor(X[:, t, cs], bS[j][:, :], rs_ab[:, t:t + 1], X[:, t, cs], ALU.mult, ALU.add)
                ins.then_inc(outa_evac, 1)
                dve.wait_ge(outa_evac, t + 1)
                for j in range(2):
                    cs = slice(512 * j, 512 * j + 512)
                    ins = v.scalar_tensor_tensor(X[:, t, cs], bB[j][:, :], rs_ab[:, TT + t:TT + t + 1], X[:, t, cs], ALU.mult, ALU.add)
                ins.then_inc(x1_done, 1)
                dve.wait_ge(ss2_done, t + 1)
                v.tensor_scalar(nv[:, t:t + 1], ss[:, t:t + 1], 1.0 / D, EPS, ALU.mult, ALU.add).then_inc(nv2_done, 1)
                inv_sqrt(rs2[:, t:t + 1], t, t + 1, nr2_done, t + 1)
                if t == 0:
                    dve.wait_ge(ld_gain, 16)
                v.scalar_tensor_tensor(xn2[:, t, :].rearrange("p (k q) -> p k q", k=KT),
                                       X[:, t, :].rearrange("p (q k) -> p k q", k=KT), rs2[:, t:t + 1],
                                       gbc.rearrange("p (q k) -> p k q", k=KT), ALU.mult, ALU.mult).then_inc(xn2_done, 1)
                if t == 0:
                    dve.wait_ge(ld_rt, 7 * 16)
                dve.wait_ge(lg_full, t + 1)
                v.tensor_tensor(lg[:, t, 0:G], bT[0][:, 0:G], br[:, 0:G], ALU.add)
                v.tensor_tensor(lg[:, t, 8:8 + E], bT[0][:, G:G + E], br[:, G:G + E], ALU.add).then_inc(lg_evac, 1)
            dve.wait_ge(lg_evac, TT)

            for t in range(TT):
                link(v.max(top[:, t, :], lg[:, t, 0:8]))
                v.max_index(topi[:, t, :], top[:, t, :], lg[:, t, 0:8])
            v.tensor_tensor(ge[:, :, :], lg[:, :, 0:G], top[:, :, 0:1].to_broadcast([P, TT, G]), ALU.subtract).then_inc(gmax_done, 1)
            dve.wait_ge(gmax_done, 1)
            link(v.tensor_copy(gidx[:, :], topi[:, :, 0]))
            for t in range(TT):
                ins = v.tensor_scalar(goh[:, t, :], iota_e[:, 0:G], gidx[:, t:t + 1], None, ALU.is_equal)
            link(ins)
            link(v.tensor_scalar(goh[:, :, :], goh[:, :, :], -NEG, NEG, ALU.mult, ALU.add))
            for t in range(TT):
                el = lg[:, t, 8:8 + E]
                link(v.tensor_tensor(el.rearrange("p (g e) -> p g e", g=G), el.rearrange("p (g e) -> p g e", g=G),
                                     goh[:, t, :].unsqueeze(2).to_broadcast([P, G, EG]), ALU.add))
                link(v.max(etop[:, t, :], el))
                link(v.max_index(etopi[:, t, :], etop[:, t, :], el))
            v.tensor_tensor(wd[:, :], etop[:, :, 1], etop[:, :, 0], ALU.subtract).then_inc(gmax_done, 1)
            link(v.tensor_copy(eid[:, :, :], etopi[:, :, 0:2]))
            for c in range(2):
                for t in range(TT):
                    ins = v.tensor_scalar(oh[:, c, t, :], iota_e[:, :], eid[:, t, c:c + 1], None, ALU.is_equal)
            link(ins)
            v.tensor_tensor(ohs[:, :, :], oh[:, 0, :, :], oh[:, 1, :, :], ALU.add).then_inc(oh_done, 1)
            dve.wait_ge(gexp_done, 2)
            link(v.reduce_sum(gs[:, :], ge[:, :, :], AX))
            link(v.tensor_scalar_add(wt[:, 1, :], wd[:, :], 1.0))
            link(v.tensor_tensor(gs[:, :], gs[:, :], wt[:, 1, :], ALU.mult))
            link(v.reciprocal(wt[:, 0, :], gs[:, :]))
            v.tensor_tensor(wt[:, 1, :], wt[:, 0, :], wd[:, :], ALU.mult)
            dve.wait_ge(rk_full, 1)
            v.tensor_copy(rk[:, :, :], bT[0][:, 0:TT * E].rearrange("p (t e) -> p t e", t=TT))
            link(v.tensor_copy(cnt[:, :], bT[0][:, TT * E:(TT + 1) * E]))
            for c in range(2):
                link(v.tensor_tensor(ohr[:, :, :], oh[:, c, :, :], rk[:, :, :], ALU.mult))
                link(v.reduce_sum(pos[:, c, :], ohr[:, :, :], AX))
                link(v.scalar_tensor_tensor(pos[:, c, :], eid[:, :, c], float(LIST), pos[:, c, :], ALU.mult, ALU.add))
            v.tensor_copy(posi[:, :, :], pos[:, :, :]).then_inc(pos_done, 1)
            link(v.tensor_scalar(ovc[:, :], cnt[:, :], float(SLOTS), None, ALU.is_gt))
            for j in range(2, (LIST + SLOTS - 1) // SLOTS):
                link(v.scalar_tensor_tensor(ovc[:, :], cnt[:, :], float(SLOTS * j), ovc[:, :], ALU.is_gt, ALU.add))
            link(v.tensor_tensor_scan(ovi[:, :], ovc[:, :], ovc[:, :], 0.0, ALU.add, ALU.max))
            link(v.tensor_scalar(ovt[:, :], ovi[:, :], tok_id[:, 0:1], None, ALU.is_le))
            link(v.reduce_sum(ovr[:, 0:1], ovt[:, :], AX))
            link(v.tensor_tensor(ovx[:, :], ovt[:, :], ovc[:, :], ALU.mult))
            link(v.reduce_sum(ovr[:, 3:4], ovx[:, :], AX))
            link(v.tensor_tensor(ovr[:, 3:4], tok_id[:, 0:1], ovr[:, 3:4], ALU.subtract))
            link(v.tensor_scalar(ovr[:, 3:4], ovr[:, 3:4], 1.0, float(SLOTS), ALU.add, ALU.mult))
            link(v.scalar_tensor_tensor(ovr[:, 1:2], ovr[:, 0:1], float(LIST), ovr[:, 3:4], ALU.mult, ALU.add))
            v.tensor_copy(ovr[:, 2:3], ovi[:, E - 1:E]).then_inc(ovr_done, 1)
            dve.wait_ge(ovr_full, 1)
            v.tensor_copy(ov_regs[:, :], bG[0][0:1, 0:3 * OVROWS]).then_inc(ovr_regs, 1)
            dve.wait_ge(ld_tab, 16)
            v.tensor_copy(tabf[:, :], tab[:, :]).then_inc(tabf_done, 1)
            dve.wait_ge(slot_full, 1)
            link(v.tensor_copy(slotf[:, :], bT[1][0:SLOTS, 0:E]))
            link(v.tensor_scalar(sge[:, :], slotf[:, :], float(NTOK), float(NTOK), ALU.is_ge, ALU.mult))
            v.tensor_copy(sca_i[:, :], slotf[:, :])
            v.tensor_tensor(gat_i[:, :], slotf[:, :], sge[:, :], ALU.subtract).then_inc(idx_done, 1)

            def swiglu(e, buf, first):
                gl, bank = glu[buf], bG[buf]
                dve.wait_ge(gexp, e + 1)
                v.tensor_scalar_add(gl[:, 0:F], gl[:, 0:F], 1.0).then_inc(glu_c, 1)
                dve.wait_ge(glu_c, e * 3 + 1)
                v.reciprocal(gl[:, 0:F], gl[:, 0:F]).then_inc(glu_c, 1)
                dve.wait_ge(glu_c, e * 3 + 2)
                v.tensor_tensor(gl[:, 0:F], gl[:, 0:F], bank[0:SLOTS, 0:F], ALU.mult).then_inc(glu_c, 1)
                dve.wait_ge(glu_c, e * 3 + 3)
                if not first:
                    dve.wait_ge(ht_full, e - 1)
                v.tensor_tensor(gl[:, F:2 * F], gl[:, 0:F], bank[0:SLOTS, F:2 * F], ALU.mult).then_inc(glu_done, 1)

            def step(e, u, i, first, has_next):
                if has_next:
                    swiglu(e + 1, (u + 1) % 2, first and u == 0)
                dve.wait_ge(y_full, e + 1)
                if not (first and u < 2):
                    dve.wait_ge(scattered[u % 2], (i * (RING // 2) + u // 2) * 16)
                v.tensor_copy(y_rows[u % 2][:, 512:D], bO[1][0:SLOTS, :]).then_inc(y_evac_d, 1)

            swiglu(0, 0, True)
            for u in range(RING):
                step(u, u, 0, True, True)
            with dve.Fori(1, LAST) as i:
                for u in range(RING):
                    step(i * RING + u, u, i, False, True)
            for u in range(RING):
                step(LAST * RING + u, u, LAST, False, u < RING - 1)
            n_ov = dve.value_load(ov_regs[0:1, 2 * OVROWS:2 * OVROWS + 1], min_val=0, max_val=MAXOV)
            with dve.If(n_ov > 0):
                with dve.Fori(0, n_ov) as i:
                    dve.wait_ge(ov_tab, i * 16 + 16)
                    v.tensor_copy(vtabf[:, 0:1], vtab[:, :]).then_inc(ov_c, 1)
                    dve.wait_ge(ov_c, i * 5 + 1)
                    v.tensor_copy(sidx_now[0][:, :], vtabf[:, 0:1])
                    v.tensor_scalar(vtabf[:, 1:2], vtabf[:, 0:1], float(NTOK), float(NTOK), ALU.is_ge, ALU.mult).then_inc(ov_c, 1)
                    dve.wait_ge(ov_c, i * 5 + 2)
                    v.tensor_tensor(gidx_now[0][:, :], vtabf[:, 0:1], vtabf[:, 1:2], ALU.subtract).then_inc(ov_idx, 1)
                    gl, bank = glu[0], bG[0]
                    dve.wait_ge(ov_ex, i + 1)
                    v.tensor_scalar_add(gl[:, 0:F], gl[:, 0:F], 1.0).then_inc(ov_c, 1)
                    dve.wait_ge(ov_c, i * 5 + 3)
                    v.reciprocal(gl[:, 0:F], gl[:, 0:F]).then_inc(ov_c, 1)
                    dve.wait_ge(ov_c, i * 5 + 4)
                    v.tensor_tensor(gl[:, 0:F], gl[:, 0:F], bank[0:SLOTS, 0:F], ALU.mult).then_inc(ov_c, 1)
                    dve.wait_ge(ov_c, i * 5 + 5)
                    v.tensor_tensor(gl[:, F:2 * F], gl[:, 0:F], bank[0:SLOTS, F:2 * F], ALU.mult).then_inc(ov_glu, 1)
                    dve.wait_ge(y_full, i + (E + 1))
                    dve.wait_ge(scattered[0], i * 16 + E // 2 * 16)
                    v.tensor_copy(y_rows[0][:, 512:D], bO[1][0:SLOTS, :]).then_inc(y_evac_d, 1)

            dve.wait_ge(ld_gain, 32)
            for t in range(TT):
                for c in range(2):
                    dve.wait_ge(ld_pair[2 * (t % 2) + c], 16 * (t // 2 + 1))
                    ins = v.scalar_tensor_tensor(X[:, t, :], yp[2 * (t % 2) + c], wt[:, c, t:t + 1], X[:, t, :], ALU.mult, ALU.add)
                    if c == 0:
                        link(ins)
                ins.then_inc(y2_done, 1)
            for t in range(TT):
                dve.wait_ge(ss3_done, t + 1)
                v.tensor_scalar(nv[:, t:t + 1], ss[:, t:t + 1], 1.0 / D, EPS, ALU.mult, ALU.add).then_inc(nv3_done, 1)
                inv_sqrt(rs3[:, t:t + 1], t, t + 1, nr3_done, t + 1)
                v.scalar_tensor_tensor(yo[t], X[:, t, :], rs3[:, t:t + 1], gbc, ALU.mult, ALU.mult).then_inc(out_done, 1)

        @block.tensor
        def _(pe):
            te = nc.tensor

            def mm(out, lhsT, rhs, start=True, stop=True, **kw):
                return te.matmul(out, lhsT, rhs, start=start, stop=stop, **kw)

            def t_bank(j):
                if j >= 2:
                    pe.wait_ge(t_evac, j - 1)
                return bT[j % 2]

            def project(j):
                kind = g_kinds[j]
                if j >= 2:
                    pe.wait_ge(*g_place[j - 2])
                bank = bG[j % 2]
                first_of = {"q": 0, "k": CT, "v": 2 * CT}
                n = j - first_of[kind] if kind in first_of else (j - G_FILL) // 3
                if n == 0:
                    pe.wait_ge(ld_chunk[kind], 16)
                w = chunk[kind]
                for k in range(KT):
                    if kind == "v":
                        ins = mm(bank[:, :], xT[:, k, n * P:(n + 1) * P], w[:, k, :], k == 0, k == KT - 1)
                    else:
                        ins = mm(bank[:, 0:NTOK], w[:, k, n * P:(n + 1) * P], xT[:, k, :], k == 0, k == KT - 1)
                ins.then_inc(g_full, 1)

            pe.wait_ge(consts, 3)
            pe.wait_ge(ld_small, 8 * 16)
            te.transpose(t_bank(T_SMALL)[:, 0:5 * CT], small, ident[0:5 * CT, 0:5 * CT]).then_inc(t_full, 1)
            for ct in range(CT):
                ins = te.transpose(bT[T_STATE % 2][:, ct * 2 * NB:(ct + 1) * 2 * NB], state[:, ct * P:(ct + 1) * P],
                                   ident[0:2 * NB, 0:2 * NB])
            ins.then_inc(t_full, 1)
            pe.wait_ge(xs_done, TT)
            for k in range(KT):
                bank = t_bank(T_X + k)
                for t in range(TT):
                    ins = te.transpose(bank[:, t * P:(t + 1) * P], xs[:, t, k, :], ident[:, :])
                ins.then_inc(t_full, 1)
            pe.wait_ge(t_evac, T_X + KT)
            for t in range(TT):
                for k in range(KT):
                    ins = mm(bS[0][:, t * H:(t + 1) * H], xT[:, k, t * P:(t + 1) * P], wf[:, k, :], k == 0, k == KT - 1)
            ins.then_inc(f_full, 1)
            for j in range(2 * CT):
                project(j)
            for t in range(TT):
                bank = t_bank(T_K + t)
                if t == 0:
                    pe.wait_ge(*g_place[2 * CT - 1])
                for ct in range(CT):
                    ins = te.transpose(bank[:, ct * P:(ct + 1) * P], kT[:, ct, t * P:(t + 1) * P], ident[:, :])
                ins.then_inc(t_full, 1)
            pe.wait_ge(consts, CONSTS)
            pe.wait_ge(lf_done, 1)
            tri = [t_le, t_le, t_str]
            for t in range(TT):
                mm(bS[1][:, t * H:(t + 1) * H], tri[t][:, :], lf[:, t, :], True, t != 1)
                if t == 1:
                    mm(bS[1][:, H:2 * H], ones[:, :], lf[:, 0, :], False, True)
            for t in range(QT):
                dst = bS[1][0:H, 32 + t * P:32 + (t + 1) * P]
                mm(dst, lf[:, t, :], tri[t][:, :], True, t != 1)
                if t == 1:
                    ins = mm(dst, lf[:, 0, :], ones[:, :], False, True)
            ins.then_inc(decay_full, 1)
            for t in range(TT):
                project(2 * CT + t)
            pe.wait_ge(cmul_done, 1)
            mm(bS[0][:, 0:NB], cmul[:, :, :].rearrange("p h q -> p (h q)"), of_stream[:, :]).then_inc(cq_full, 1)

            def scores_of(n):
                hd, q = unit(n)
                bank = bS[n % 2]
                if n == 0:
                    pe.wait_ge(decay_done, 1)
                if n >= 2:
                    pe.wait_ge(s_evac, n - 1)
                if hd is None:
                    b = q
                    new = slice(SEQ + b * NQ, SEQ + (b + 1) * NQ)
                    pe.wait_ge(t_evac, t_kc[b] + 1)
                    pe.wait_ge(lfx_done, b + 1)
                    mm(bank[:, 0:PAST], lfx[b % 2][:, :, :].rearrange("p h q -> p (h q)"), t_gt[:, :],
                       True, False, skip_group_check=True)
                    mm(bank[:, PAST:PAST + NQ], lfn[:, :, :].rearrange("p h q -> p (h q)"), t_str[:, b * NQ:(b + 1) * NQ],
                       False, False, skip_group_check=True)
                    for c in range(CT):
                        rows = slice(2 * NQ * c, 2 * NQ * (c + 1))
                        lhsT = qs[:, c, b, :, :].rearrange("p s q -> p (s q)")
                        mm(bank[rows, 0:PAST], lhsT, kc[b % 2][:, c, :], False, True, skip_group_check=True)
                        ins = mm(bank[rows, PAST:PAST + NQ], lhsT, kT[:, c, new], False, True, skip_group_check=True)
                else:
                    w = (q + 1) * P
                    mm(bank[:, 0:w], ident[:, hd:hd + 1].to_broadcast([P, P]), nc_p[:, 0:w], True, False)
                    ins = mm(bank[:, 0:w], qz[:, hd, q * P:(q + 1) * P], kT[:, hd // 2, 0:w], False, True)
                ins.then_inc(s_full, 1)

            def probs_transpose(n):
                hd, q = unit(n)
                blocks = 2 if hd is None else q + 1
                bank = t_bank(t_p[n])
                pe.wait_ge(pn_done, n + 1)
                for k in range(blocks):
                    ins = te.transpose(bank[:, k * P:(k + 1) * P], pnorm[n % 2][:, k * P:(k + 1) * P], ident[:, :])
                ins.then_inc(t_full, 1)

            def weighted_values(n):
                hd, q = unit(n)
                bank = bO[n % 2]
                pe.wait_ge(t_evac, t_p[n] + 1)
                if n >= 2:
                    pe.wait_ge(o_evac, n - 1)
                if n == 0:
                    pe.wait_ge(*g_place[2 * CT + TT - 1])
                if hd is None:
                    pe.wait_ge(ld_cv[q % 4], 16 * (q // 4 + 1))
                    for c in range(CT):
                        cs = slice(c * 2 * NQ, (c + 1) * 2 * NQ)
                        mm(bank[:, cs], cv[q % 4][:, c * P:(c + 1) * P], pT[n % 2][:, cs], True, False)
                        ins = mm(bank[:, cs], V[:, QT, c * P:(c + 1) * P], pT[n % 2][:, P + c * 2 * NQ:P + (c + 1) * 2 * NQ], False, True)
                else:
                    rows = slice((hd % 2) * HD, (hd % 2 + 1) * HD)
                    for k in range(q + 1):
                        ins = mm(bank[rows, 0:P], V[:, k, hd * HD:(hd + 1) * HD], pT[n % 2][:, k * P:(k + 1) * P], k == 0, k == q)
                ins.then_inc(pv_full, 1)

            for n in range(UNITS + 3):
                if 2 * H <= n + 1 < UNITS:
                    b = n + 1 - 2 * H
                    bank = t_bank(t_kc[b])
                    pe.wait_ge(ld_ck[b % 4], 16 * (b // 4 + 1))
                    for c in range(CT):
                        ins = te.transpose(bank[:, c * P:(c + 1) * P], ck[b % 4][:, c * P:(c + 1) * P], ident[:, :])
                    ins.then_inc(t_full, 1)
                if n < UNITS:
                    scores_of(n)
                for j in fill_at.get(n, []):
                    project(j)
                if 0 <= n - 1 < UNITS:
                    probs_transpose(n - 1)
                if 0 <= n - 2 < UNITS:
                    weighted_values(n - 2)

            bank = t_bank(T_LAST)
            pe.wait_ge(last_done, CT)
            for ct in range(CT):
                ins = te.transpose(bank[0:2 + 2 * NB, ct * P:(ct + 1) * P], last[:, ct, :], ident[:, :])
            ins.then_inc(t_full, 1)
            pe.wait_ge(t_evac, T_LAST + 1)
            pe.wait_ge(sq_done, 2)
            for half, sq in enumerate((sqA, sqB)):
                for t in range(TT):
                    for ct in range(CT):
                        ins = mm(bT[0][:, half * TT + t:half * TT + t + 1], sq[:, ct, t * P:(t + 1) * P], ones[:, 0:1],
                                 ct == 0, ct == CT - 1)
            ins.then_inc(ssab_full, 1)

            def out_project(t):
                bB = bG if t % 2 == 0 else bO
                if t == 0:
                    pe.wait_ge(*g_place[-1])
                    pe.wait_ge(o_evac, UNITS)
                    pe.wait_ge(gain_done, 2 * CT)
                    pe.wait_ge(ld_wo[0], 16)
                    pe.wait_ge(ld_wo[1], 16)
                if t >= 2:
                    pe.wait_ge(x1_done, t - 1)
                for j in range(2):
                    for ct in range(CT):
                        mm(bB[j][:, :], oB[:, ct, t * P:(t + 1) * P], wo[1][:, ct, j * 512:(j + 1) * 512], ct == 0, ct == CT - 1)
                if t >= 1:
                    pe.wait_ge(outa_evac, t)
                for j in range(2):
                    for ct in range(CT):
                        ins = mm(bS[j][:, :], oT[:, ct, t * P:(t + 1) * P], wo[0][:, ct, j * 512:(j + 1) * 512], ct == 0, ct == CT - 1)
                ins.then_inc(out_full, 1)

            def router(t):
                pe.wait_ge(xn2_done, t + 1)
                if t == 0:
                    pe.wait_ge(nvab_done, 1)
                    pe.wait_ge(ld_rt, 7 * 16)
                for half in range(2):
                    if t >= 1:
                        pe.wait_ge(x2t_evac, 2 * t)
                        pe.wait_ge(lg_evac, t)
                    for k in range(4):
                        kk = half * 4 + k
                        ins = te.transpose(bT[half][:, k * P:(k + 1) * P], xn2[:, t, kk * P:(kk + 1) * P], ident[:, :])
                    ins.then_inc(x2t_full, 1)
                pe.wait_ge(x2t_evac, 2 * t + 2)
                for k in range(KT):
                    ins = mm(bT[0][:, 0:G + E], x2T[:, t, k, :], wr[:, k, :], k == 0, k == KT - 1)
                ins.then_inc(lg_full, 1)

            out_project(0)
            out_project(1)
            router(0)
            out_project(2)
            router(1)
            router(2)
            pe.wait_ge(lg_evac, TT)
            pe.wait_ge(oh_done, 1)
            for t in range(TT):
                for tp in range(t + 1):
                    mm(bT[0][:, t * E:(t + 1) * E], (t_lt if tp == t else ones)[:, :], ohs[:, tp, :], tp == 0, tp == t)
            for t in range(TT):
                ins = mm(bT[0][:, TT * E:(TT + 1) * E], ones[:, :], ohs[:, t, :], t == 0, t == TT - 1)
            ins.then_inc(rk_full, 1)
            pe.wait_ge(ovr_done, 1)
            for c in range(3):
                ins = mm(bG[0][0:1, c * OVROWS:(c + 1) * OVROWS], ovr[0:OVROWS, c:c + 1], ident[0:OVROWS, 0:OVROWS])
            ins.then_inc(ovr_full, 1)
            pe.wait_ge(tabf_done, 1)
            te.transpose(bT[1][0:SLOTS, 0:E], tabf[:, :], ident[0:E, 0:E]).then_inc(slot_full, 1)

            def rows_transpose(buf, done):
                pe.sem_inc(pe_paced, 1)
                for k in range(KT):
                    ins = te.transpose(bT[buf][:, k * SLOTS:(k + 1) * SLOTS], xg[buf][:, k * P:(k + 1) * P],
                                       ident[0:SLOTS, 0:SLOTS])
                ins.then_inc(done, 1)

            def gate_up(buf, r, k0, k1, done=None):
                for k in range(k0, k1):
                    ins = mm(bG[buf][0:SLOTS, :], xgT[buf][:, k, :], gu_ring[:, r, k * 2 * F:(k + 1) * 2 * F], k == 0, k == KT - 1)
                if done is not None:
                    ins.then_inc(done, 1)

            def hidden_transpose(buf, done):
                pe.sem_inc(pe_paced, 1)
                for j in range(FT):
                    ins = te.transpose(bS[0][:, j * SLOTS:(j + 1) * SLOTS], glu[buf][:, F + j * P:F + (j + 1) * P],
                                       ident[0:SLOTS, 0:SLOTS])
                ins.then_inc(done, 1)

            def down(r, done):
                for half in range(2):
                    for j in range(FT):
                        ins = mm(bO[half][0:SLOTS, :], hT[:, j, :], dn_ring[:, r, j * D + half * 512:j * D + half * 512 + 512],
                                 j == 0, j == FT - 1)
                ins.then_inc(done, 1)

            def begin(e, buf, r, turn, half_turn, first):
                pe.wait_ge(gathered[buf], half_turn * 16 + 16)
                if not first:
                    pe.wait_ge(xgt_evac, e - 1)
                rows_transpose(buf, xgt_full)
                pe.wait_ge(xgt_evac, e + 1)
                pe.wait_ge(ld_gu[r], turn * 16 + 16)
                if not first:
                    pe.wait_ge(glu_done, e - 1)
                gate_up(buf, r, 0, KT - 2)

            def step(e, u, i, first, has_next):
                if has_next:
                    r = (u + 1) % RING
                    begin(e + 1, (u + 1) % 2, r, i + (u + 1) // RING, i * (RING // 2) + (u + 1) // 2, first and u == 0)
                pe.wait_ge(glu_done, e + 1)
                if not (first and u == 0):
                    pe.wait_ge(ht_evac, e)
                hidden_transpose(u % 2, ht_full)
                if has_next:
                    gate_up((u + 1) % 2, r, KT - 2, KT, gu_full)
                pe.wait_ge(ht_evac, e + 1)
                pe.wait_ge(ld_dn[u], i * 16 + 16)
                if not (first and u == 0):
                    pe.wait_ge(y_evac_a, e)
                    pe.wait_ge(y_evac_d, e)
                down(u, y_full)

            pe.wait_ge(idx_done, 1)
            pe.wait_ge(ovr_regs, 1)
            begin(0, 0, 0, 0, 0, True)
            gate_up(0, 0, KT - 2, KT, gu_full)
            for u in range(RING):
                step(u, u, 0, True, True)
            with pe.Fori(1, LAST) as i:
                for u in range(RING):
                    step(i * RING + u, u, i, False, True)
            for u in range(RING):
                step(LAST * RING + u, u, LAST, False, u < RING - 1)
            pe.wait_ge(y_evac_a, E)
            pe.wait_ge(y_evac_d, E)
            n_ov = pe.value_load(ov_regs[0:1, 2 * OVROWS:2 * OVROWS + 1], min_val=0, max_val=MAXOV)
            with pe.If(n_ov > 0):
                with pe.Fori(0, n_ov) as i:
                    pe.wait_ge(ov_gat, i * 16 + 16)
                    rows_transpose(0, ov_xt)
                    pe.wait_ge(ov_xe, i + 1)
                    pe.wait_ge(ov_w, i * 32 + 32)
                    gate_up(0, 0, 0, KT, ov_gu)
                    pe.wait_ge(ov_glu, i + 1)
                    hidden_transpose(0, ov_ht)
                    pe.wait_ge(ov_he, i + 1)
                    pe.wait_ge(y_evac_a, i + E)
                    pe.wait_ge(y_evac_d, i + E)
                    down(0, y_full)


SHAPES = {
    "cache_k": (NB, PAST, A), "cache_v": (NB, PAST, A), "cache_logf": (NB, PAST, H), "state_conv": (2 * NB, C),
    "norm_mix_g": (D,), "w_in": (D, 3 * A + H + 3 * C), "b_forget": (H,), "conv_w": (3, C), "norm_attn_g": (A,),
    "norm_conv_g": (C,), "w_out": (A + C, D), "norm_ffn_g": (D,), "w_router_group": (D, G), "b_router_group": (G,),
    "w_router_expert": (G, D, EG), "b_router_expert": (E,), "w_expert_gate_up": (E, D, 2 * F),
    "w_expert_down": (E, F, D), "norm_final_g": (D,),
}
OUTPUTS = {
    "y_p": ((SEQ, D), (1, SEQ, D)), "y_s": ((NB * NQ, D), (NB, NQ, D)),
    "k_p": ((SEQ, A), (1, 1, SEQ, H, HD)), "v_p": ((SEQ, A), (1, 1, SEQ, H, HD)), "lf_p": ((SEQ, H), (1, 1, SEQ, H)),
    "conv_p": ((2, C), (1, 1, 2, C)), "k_s": ((NB * NQ, A), (1, NB, NQ, H, HD)), "v_s": ((NB * NQ, A), (1, NB, NQ, H, HD)),
    "lf_s": ((NB * NQ, H), (1, NB, NQ, H)), "conv_s": ((2 * NB, C), (1, NB, 2, C)),
}


def kernel(**inputs):
    import numpy as np
    import concourse.bacc as bacc
    from concourse.bass_utils import run_bass_kernel_spmd

    nc = bacc.Bacc("TRN2", target_bir_lowering=False, num_devices=1)
    arrays, a, o = {}, {}, {}
    rows = [np.asarray(inputs["x_prompt"]).reshape(SEQ, D), np.asarray(inputs["x_sample"]).reshape(NB * NQ, D)]
    laid = {"x": np.concatenate(rows)}
    for name, shape in SHAPES.items():
        laid[name] = np.asarray(inputs[name]).reshape(shape)
    for name, x in laid.items():
        x = np.ascontiguousarray(x)
        arrays[f"in_{name}"] = x
        a[name] = nc.dram_tensor(f"in_{name}", x.shape, mybir.dt.from_np(x.dtype), kind="ExternalInput").ap()
    for name, (shape, _) in OUTPUTS.items():
        o[name] = nc.dram_tensor(f"out_{name}", shape, mybir.dt.float32, kind="ExternalOutput").ap()
    build(nc, a, o)
    got = run_bass_kernel_spmd(nc, [arrays], core_ids=[0]).results[0]
    return tuple(got[f"out_{name}"].reshape(shape) for name, (_, shape) in OUTPUTS.items())
```

```python
import concourse.bass as bass
from concourse import mybir
from contextlib import ExitStack

P = 128
D = 1024
KT = D // P
SEQ = 256
NB = 8
NQ = 16
PAST = 128
H = 8
HD = 64
A = H * HD
C = D - A
CT = C // P
NTOK = SEQ + NB * NQ
TT = NTOK // P
QT = SEQ // P
G = 4
EG = 8
E = G * EG
F = 256
FT = F // P
EPS = 1e-6
NEG = -1.0e30
SLOTS = 64
LIST = NTOK
PAIRS = 2 * NTOK
DUOS = E // 2
EMPTY = 3 * NTOK
FAR = 1.0e6
RING = 4
MAXOV = PAIRS // SLOTS
OVROWS = 16 * -(-(MAXOV + 1) // 16)
LAST = E // RING - 1
CONSTS = 20
UNITS = 2 * H + NB


def build(nc, a, o):
    f32 = mybir.dt.float32
    i32 = mybir.dt.int32
    u32 = mybir.dt.uint32
    ALU = mybir.AluOpType
    ACT = mybir.ActivationFunctionType
    AX = mybir.AxisListType.X

    pair_dram = nc.dram_tensor("pair_rows", [PAIRS, D], f32, kind="Internal").ap()

    w_in = a["w_in"].rearrange("(p k) n -> p k n", k=KT)
    w_gu = a["w_expert_gate_up"].rearrange("e (p k) n -> e p (k n)", k=KT)
    w_dn = a["w_expert_down"].rearrange("e (j p) n -> e p j n", p=P)
    cols = {"q": 0, "k": A, "v": 2 * A, "f": 3 * A, "B": 3 * A + H, "C": 3 * A + H + C, "h": 3 * A + H + 2 * C}

    ctx = ExitStack()
    with ctx:
        def sb(name, shape, dt=f32):
            return ctx.enter_context(nc.sbuf_tensor(name, shape, dt))

        def sem(name):
            return ctx.enter_context(nc.semaphore(name))

        gu_ring = sb("gu_ring", [P, RING, KT * 2 * F])
        dn_ring = sb("dn_ring", [P, RING, FT * D])
        chunk = {
            "q": gu_ring[:, 0, :].rearrange("p (k n) -> p k n", k=KT),
            "k": gu_ring[:, 1, :].rearrange("p (k n) -> p k n", k=KT),
            "v": gu_ring[:, 2, :].rearrange("p (k n) -> p k n", k=KT),
            "B": gu_ring[:, 3, :].rearrange("p (k n) -> p k n", k=KT),
            "C": dn_ring[:, 0:2, :].rearrange("p r (k n) -> p (r k) n", n=C),
            "h": dn_ring[:, 2:4, :].rearrange("p r (k n) -> p (r k) n", n=C),
        }
        wo = [gu_ring[:, 0, :].rearrange("p (c n) -> p c n", c=CT),
              gu_ring[:, 1, :].rearrange("p (c n) -> p c n", c=CT)]

        X = sb("X", [P, TT, D])
        r_xs = sb("r_xs", [P, 4096])
        xs = r_xs[:, 0:TT * D].rearrange("p (t k q) -> p t k q", t=TT, k=KT)
        ck = [r_xs[:, 512 * i:512 * i + 512] for i in range(4)]
        cv = [r_xs[:, 2048 + 512 * i:2048 + 512 * i + 512] for i in range(4)]
        y_rows = [r_xs[:, D * i:D * (i + 1)] for i in range(2)]
        r_xT = sb("r_xT", [P, KT * NTOK])
        xT = r_xT[:, :].rearrange("p (k t) -> p k t", k=KT)
        x2T = r_xT[:, 0:TT * D].rearrange("p (t k q) -> p t k q", t=TT, k=KT)
        xgT = [r_xT[:, D * i:D * (i + 1)].rearrange("p (k s) -> p k s", k=KT) for i in range(2)]
        yo = [r_xT[:, D * t:D * (t + 1)] for t in range(TT)]
        r_qz = sb("r_qz", [P, H * NTOK])
        qz = r_qz[:, 0:H * SEQ].rearrange("p (h t) -> p h t", h=H)
        qs = r_qz[:, H * SEQ:].rearrange("p (c b s q) -> p c b s q", c=CT, b=NB, s=2)
        xn2 = r_qz[:, 0:TT * D].rearrange("p (t d) -> p t d", t=TT)
        r_kT = sb("r_kT", [P, CT, NTOK])
        kT = r_kT
        glu = [r_kT[:, :, :].rearrange("p c t -> p (c t)")[:, 2 * F * i:2 * F * (i + 1)] for i in range(2)]
        V = sb("V", [P, TT, A])
        BT = sb("BT", [P, CT, NTOK])
        oB = sb("oB", [P, CT, NTOK])
        r_U = sb("r_U", [P, CT * (SEQ + 2 + NB * (NQ + 2))])
        Up = r_U[:, 0:CT * (SEQ + 2)].rearrange("p (c t) -> p c t", c=CT)
        Us = r_U[:, CT * (SEQ + 2):].rearrange("p (c b t) -> p c b t", c=CT, b=NB)
        sqB = r_U[:, 0:CT * NTOK].rearrange("p (c t) -> p c t", c=CT)
        sqA = BT
        oT = sb("oT", [P, CT, NTOK])
        r_kc = sb("r_kc", [P, 2, 512])
        krow = [r_kc[:, i, :] for i in range(2)]
        kc = [r_kc[:, i, :].rearrange("p (c s) -> p c s", c=CT) for i in range(2)]
        r_sc = sb("r_sc", [P, 512])
        scores = [r_sc[:, 256 * i:256 * (i + 1)] for i in range(2)]
        last_row = r_sc[0:2 + 2 * NB, :]
        r_pr = sb("r_pr", [P, 512])
        probs = [r_pr[:, 256 * i:256 * (i + 1)] for i in range(2)]
        small = r_pr[0:5 * CT, 0:P]
        pnorm = [sb(f"pnorm{i}", [P, 256]) for i in range(2)]
        pT = [sb(f"pT{i}", [P, 256]) for i in range(2)]
        BT_flat = BT[:, :, :].rearrange("p c t -> p (c t)")
        pick = [BT_flat[:, NTOK * i:NTOK * (i + 1)].rearrange("p (t s) -> p t s", t=TT) for i in range(2)]
        pick0 = BT_flat[:, 2 * NTOK:3 * NTOK].rearrange("p (t s) -> p t s", t=TT)
        ranked = BT_flat[:, 3 * NTOK:4 * NTOK].rearrange("p (c t s) -> p c t s", c=2, t=TT)
        slot_no = r_U[:, 0:P]
        flat = [r_xs[:, 0:D], r_xs[:, D:2 * D], r_xs[:, 2 * D:3 * D], r_xs[:, 3 * D:4 * D],
                oB[:, :, :].rearrange("p c t -> p (c t)")[:, 0:D], oT[:, :, :].rearrange("p c t -> p (c t)")[:, 0:D]]
        yp = [flat[2 * t:2 * t + 2] for t in range(TT)]
        tmpc = sb("tmpc", [P, NTOK])
        gbc = r_kc[:, :, :].rearrange("p i n -> p (i n)")

        ident = sb("ident", [P, P])
        ones = sb("ones", [P, P])
        t_le = sb("t_le", [P, P])
        t_lt = sb("t_lt", [P, P])
        t_gt = sb("t_gt", [P, P])
        t_str = sb("t_str", [P, P])
        causal = sb("causal", [P, P])
        causal_s = sb("causal_s", [P, NQ])
        iota_q = sb("iota_q", [P, NQ])
        iota_e = sb("iota_e", [P, E])
        tok_id = sb("tok_id", [P, TT])
        pid = sb("pid", [P, 1], i32)
        pmod_i = sb("pmod_i", [P, 1], i32)
        pmod = sb("pmod", [P, 1])
        same_q = sb("same_q", [P, NQ])
        of_stream = sb("of_stream", [P, NB])

        gmix = sb("gmix", [P, KT])
        smallT = sb("smallT", [P, 5 * CT])
        gA = smallT[:, 0:CT]
        gB = smallT[:, CT:2 * CT]
        cw = smallT[:, 2 * CT:5 * CT].rearrange("p (i c) -> p i c", i=3)
        state = krow[0][0:2 * NB, :]
        last = sb("last", [P, CT, 2 + 2 * NB])
        wf = sb("wf", [P, KT, H])
        bf = sb("bf", [P, H])
        wr = sb("wr", [P, KT, G + E])
        br = sb("br", [P, G + E])
        lfc = sb("lfc", [P, NB, H])
        lf = sb("lf", [P, TT, H])
        fa = sb("fa", [P, TT, H])
        fb = sb("fb", [P, TT, H])
        fz = sb("fz", [P, TT, H])
        cum = sb("cum", [P, TT, H])
        nc_p = sb("nc_p", [P, SEQ])
        lfn = sb("lfn", [P, H, NQ])
        lfx = [sb(f"lfx{i}", [P, H, NQ]) for i in range(2)]
        cmul = pT[0][:, 0:H * NQ].rearrange("p (h q) -> p h q", h=H)
        cq_s = sb("cq_s", [P, NB])
        nmax = sb("nmax", [P, 2])
        psum_ = sb("rowsum", [P, 2])
        rrec = sb("rrec", [P, 2])
        ss = sb("ss", [P, 6])
        nv = sb("nv", [P, 6])
        nln = sb("nln", [P, 6])
        nr0 = sb("nr0", [P, 6])
        nt = sb("nt", [P, 6])
        rs1 = sb("rs1", [P, TT])
        rs_ab = sb("rs_ab", [P, 6])
        rs2 = sb("rs2", [P, TT])
        rs3 = sb("rs3", [P, TT])
        taken = [0]

        def over_v(shape, dt=f32):
            n = 1
            for m in shape[1:]:
                n *= m
            ap = V_flat[0:shape[0], taken[0]:taken[0] + n]
            taken[0] += n + n % 2
            assert taken[0] <= TT * A
            if dt != f32:
                ap = ap.bitcast(dt)
            if len(shape) == 3:
                ap = ap.rearrange("p (a b) -> p a b", a=shape[1])
            if len(shape) == 4:
                ap = ap.rearrange("p (a b c) -> p a b c", a=shape[1], b=shape[2])
            return ap

        V_flat = V[:, :, :].rearrange("p t a -> p (t a)")
        lg = over_v([P, TT, 8 + E])
        top = over_v([P, TT, 8])
        topi = over_v([P, TT, 8], u32)
        gidx = over_v([P, TT])
        goh = over_v([P, TT, G])
        ge = over_v([P, TT, G])
        gs = over_v([P, TT])
        etop = over_v([P, TT, 8])
        etopi = over_v([P, TT, 8], u32)
        eid = over_v([P, TT, 2])
        oh = over_v([P, 2, TT, E])
        ohs = over_v([P, TT, E])
        rk = over_v([P, TT, E])
        cnt = over_v([P, E])
        ohr = over_v([P, TT, E])
        pos = over_v([P, 2, TT])
        pair_no = sb("pair_no", [P, 2 * TT])
        key = over_v([P, 2, TT])
        okey = over_v([P, 2, TT])
        wt = over_v([P, 2, TT])
        wd = over_v([P, TT])
        sca_i = over_v([P, DUOS], u32)
        sidx_now = [sb(f"sidx_now{i}", [P, 1], u32) for i in range(2)]
        ovc = over_v([P, E])
        ovt = over_v([P, E])
        ovi = over_v([P, E])
        ovx = over_v([P, E])
        ovr = over_v([P, 4])
        ov_base = over_v([P, OVROWS])
        base_now = sb("base_now", [P, 1])
        ov_regs = sb("ov_regs", [1, 3 * OVROWS], i32)
        hT = over_v([P, FT, P])

        banks = [ctx.enter_context(nc.psum_tensor(f"bank{i}", [P, 512], f32)) for i in range(8)]
        bT, bG, bS, bO = banks[0:2], banks[2:4], banks[4:6], banks[6:8]

        ld_x = [sem(f"ld_x{t}") for t in range(TT)]
        ld_chunk = {c: sem(f"ld_{c}") for c in "qkvBCh"}
        ld_wo = [sem("ld_woA"), sem("ld_woB")]
        ld_gmix = sem("ld_gmix")
        ld_small = sem("ld_small")
        ld_rt = sem("ld_rt")
        ld_gain = sem("ld_gain")
        ld_ck = [sem(f"ld_ck{i}") for i in range(4)]
        ld_cv = [sem(f"ld_cv{i}") for i in range(4)]
        consts = sem("consts")
        act_chain = sem("act_chain")
        dve_chain = sem("dve_chain")
        ss1_done = sem("ss1_done")
        nv1_done = sem("nv1_done")
        nr1_done = sem("nr1_done")
        xs_done = sem("xs_done")
        t_full = sem("t_full")
        t_evac = sem("t_evac")
        g_full = sem("g_full")
        g_evac_act = sem("g_evac_act")
        g_evac_dve = sem("g_evac_dve")
        qz_zero = sem("qz_zero")
        f_full = sem("f_full")
        fz_done = sem("fz_done")
        sp_done = sem("sp_done")
        lf_done = sem("lf_done")
        lfx_done = sem("lfx_done")
        decay_full = sem("decay_full")
        decay_done = sem("decay_done")
        cmul_done = sem("cmul_done")
        cq_full = sem("cq_full")
        s_full = sem("s_full")
        s_evac = sem("s_evac")
        nmax_done = sem("nmax_done")
        exp_done = sem("exp_done")
        pn_done = sem("pn_done")
        pv_full = sem("pv_full")
        o_evac = sem("o_evac")
        conv_done = sem("conv_done")
        last_done = sem("last_done")
        sq_done = sem("sq_done")
        ssab_full = sem("ssab_full")
        nvab_done = sem("nvab_done")
        nrab_done = sem("nrab_done")
        gain_done = sem("gain_done")
        out_full = sem("out_full")
        outa_evac = sem("outa_evac")
        lg_evac = sem("lg_evac")
        x1_done = sem("x1_done")
        ss2_done = sem("ss2_done")
        nv2_done = sem("nv2_done")
        nr2_done = sem("nr2_done")
        xn2_done = sem("xn2_done")
        x2t_full = sem("x2t_full")
        x2t_evac = sem("x2t_evac")
        lg_full = sem("lg_full")
        gmax_done = sem("gmax_done")
        gexp_done = sem("gexp_done")
        oh_done = sem("oh_done")
        rk_full = sem("rk_full")
        ovr_done = sem("ovr_done")
        ovr_full = sem("ovr_full")
        ovr_regs = sem("ovr_regs")
        st_out = sem("st_out")
        st_v = sem("st_v")
        st_krow = [sem(f"st_krow{i}") for i in range(2)]
        ld_gu = [sem(f"ld_gu{i}") for i in range(RING)]
        ld_dn = [sem(f"ld_dn{i}") for i in range(RING)]
        sidx_set = sem("sidx_set")
        scattered = [sem(f"scattered{i}") for i in range(2)]
        slot_zero = sem("slot_no_done")
        key_done = sem("key_done")
        sca_full = sem("sca_full")
        sca_done = sem("sca_done")
        key_c = sem("key_chain")
        pick_c = sem("pick_chain")
        pick_done = sem("pick_done")
        xgt_full = sem("xgt_full")
        xgt_evac = sem("xgt_evac")
        gu_full = sem("gu_full")
        gexp = sem("gexp")
        glu_c = sem("glu_chain")
        glu_done = sem("glu_done")
        ht_full = sem("ht_full")
        ht_evac = sem("ht_evac")
        y_half = sem("y_half")
        y_full = sem("y_full")
        y_evac_a = sem("y_evac_a")
        y_evac_d = sem("y_evac_d")
        pe_paced = sem("pe_paced")
        pool_paced = sem("pool_paced")
        ov_w = sem("ov_w")
        ov_base_set = sem("ov_base_set")
        ov_pick = sem("ov_pick")
        ov_no = sem("ov_no")
        ov_idx = sem("ov_idx")
        ov_xt = sem("ov_xt")
        ov_xe = sem("ov_xe")
        ov_gu = sem("ov_gu")
        ov_ex = sem("ov_ex")
        ov_c = sem("ov_chain")
        ov_glu = sem("ov_glu")
        ov_ht = sem("ov_ht")
        ov_he = sem("ov_he")
        rows_done = sem("rows_done")
        ld_pair = [sem(f"ld_pair{i}") for i in range(2 * TT)]
        ss3_done = sem("ss3_done")
        y2_done = sem("y2_done")
        nv3_done = sem("nv3_done")
        nr3_done = sem("nr3_done")
        out_done = sem("out_done")
        st_y = sem("st_y")

        T_X, T_SMALL, T_STATE, T_K = 0, KT, KT + 1, KT + 2
        t_jobs = T_K + TT
        t_kc, t_p = {}, {}
        for n in range(UNITS + 3):
            if 2 * H <= n + 1 < UNITS:
                t_kc[n + 1 - 2 * H] = t_jobs
                t_jobs += 1
            if 0 <= n - 1 < UNITS:
                t_p[n - 1] = t_jobs
                t_jobs += 1
        T_LAST = t_jobs
        t_jobs += 1
        g_kinds = ["q"] * CT + ["k"] * CT + ["v"] * TT + ["C", "h", "B"] * CT
        G_FILL = 2 * CT + TT
        g_place = []
        na = nd = 0
        for kind in g_kinds:
            if kind == "h":
                nd += 1
                g_place.append((g_evac_dve, nd))
            else:
                na += 1
                g_place.append((g_evac_act, na))
        fill_at = {}
        for f in range(3 * CT):
            fill_at.setdefault(1 + (f * 20) // (3 * CT), []).append(G_FILL + f)

        def unit(n):
            return (n // QT, n % QT) if n < 2 * H else (None, n - 2 * H)

        block = ctx.enter_context(nc.Block())

        @block.sync
        def _(sp):
            for t in range(TT):
                sp.dma_start(X[:, t, :], a["x"][t * P:(t + 1) * P, :]).then_inc(ld_x[t], 16)
                if t == 0:
                    sp.dma_start(gmix[:, :], a["norm_mix_g"].rearrange("(p k) -> p k", k=KT)).then_inc(ld_gmix, 16)
            sp.dma_start(wf[:, :, :], w_in[:, :, cols["f"]:cols["f"] + H]).then_inc(ld_small, 16)
            for c in "qkvChB":
                sp.dma_start(chunk[c], w_in[:, :, cols[c]:cols[c] + 512]).then_inc(ld_chunk[c], 16)
                if c == "q":
                    sp.dma_start(bf[:, :], a["b_forget"].partition_broadcast(P)).then_inc(ld_small, 16)
                    sp.dma_start(small[0:CT, :], a["norm_attn_g"].rearrange("(c p) -> c p", p=P)).then_inc(ld_small, 16)
                    sp.dma_start(small[CT:2 * CT, :], a["norm_conv_g"].rearrange("(c p) -> c p", p=P)).then_inc(ld_small, 16)
                    sp.dma_start(small[2 * CT:5 * CT, :], a["conv_w"].rearrange("i (c p) -> (i c) p", p=P)).then_inc(ld_small, 16)
                    sp.dma_start(state, a["state_conv"]).then_inc(ld_small, 16)
                    sp.dma_start(lfc[:, :, :], a["cache_logf"].rearrange("b s h -> s b h")).then_inc(ld_small, 16)
            sp.wait_ge(t_full, T_X + KT)
            for b in range(4):
                sp.dma_start(ck[b], a["cache_k"][b]).then_inc(ld_ck[b], 16)
                sp.dma_start(cv[b], a["cache_v"][b]).then_inc(ld_cv[b], 16)
            sp.dma_start(wr[:, :, 0:G], a["w_router_group"].rearrange("(p k) g -> p k g", k=KT)).then_inc(ld_rt, 16)
            for gi in range(G):
                sp.dma_start(wr[:, :, G + gi * EG:G + (gi + 1) * EG],
                             a["w_router_expert"][gi].rearrange("(p k) e -> p k e", k=KT)).then_inc(ld_rt, 16)
            sp.dma_start(br[:, 0:G], a["b_router_group"].partition_broadcast(P)).then_inc(ld_rt, 16)
            sp.dma_start(br[:, G:G + E], a["b_router_expert"].partition_broadcast(P)).then_inc(ld_rt, 16)
            for half, job in ((0, CT), (1, 2 * CT)):
                sp.wait_ge(g_full, job)
                sp.dma_start(wo[half], a["w_out"][half * A:(half + 1) * A, :].rearrange("(c p) n -> p c n", p=P)).then_inc(ld_wo[half], 16)
            for b in range(4, NB):
                sp.wait_ge(t_full, t_kc[b - 4] + 1)
                sp.dma_start(ck[b - 4], a["cache_k"][b]).then_inc(ld_ck[b - 4], 16)
                sp.wait_ge(pv_full, 2 * H + b - 4 + 1)
                sp.dma_start(cv[b - 4], a["cache_v"][b]).then_inc(ld_cv[b - 4], 16)
            sp.wait_ge(g_full, G_FILL + 3 * CT)
            for e in (2, 3):
                sp.dma_start(gu_ring[:, e, :], w_gu[e]).then_inc(ld_gu[e], 16)
            for e in range(RING):
                sp.dma_start(dn_ring[:, e, :].rearrange("p (j n) -> p j n", j=FT), w_dn[e]).then_inc(ld_dn[e], 16)
            sp.wait_ge(out_full, TT)
            for e in (0, 1):
                sp.dma_start(gu_ring[:, e, :], w_gu[e]).then_inc(ld_gu[e], 16)
            with sp.Fori(1, E // RING) as i:
                for u in range(2):
                    sp.wait_ge(gu_full, i * 2 + (u - 1))
                    for r in (2 * u, 2 * u + 1):
                        sp.dma_start(gu_ring[:, r, :], w_gu[i * RING + r]).then_inc(ld_gu[r], 16)
                    sp.wait_ge(y_full, i * 2 + (u - 1))
                    for r in (2 * u, 2 * u + 1):
                        sp.dma_start(dn_ring[:, r, :].rearrange("p (j n) -> p j n", j=FT), w_dn[i * RING + r]).then_inc(ld_dn[r], 16)
            sp.wait_ge(ovr_regs, 1)
            sp.wait_ge(y_full, DUOS)
            n_ov = sp.value_load(ov_regs[0:1, 2 * OVROWS:2 * OVROWS + 1], min_val=0, max_val=MAXOV)
            with sp.If(n_ov > 0):
                with sp.Fori(0, n_ov) as i:
                    sp.wait_ge(y_full, i + DUOS)
                    e = sp.value_load(ov_regs[0:1, bass.ds(i, 1)], min_val=0, max_val=E - 1)
                    sp.dma_start(gu_ring[:, 0, :], w_gu[e]).then_inc(ov_w, 16)
                    sp.dma_start(dn_ring[:, 0, :].rearrange("p (j n) -> p j n", j=FT), w_dn[e]).then_inc(ov_w, 16)
            sp.wait_ge(rows_done, 1)
            for t in range(TT):
                for c in range(2):
                    sp.dma_start(yp[t][c], pair_dram[c * NTOK + t * P:c * NTOK + (t + 1) * P, :]).then_inc(ld_pair[2 * t + c], 16)

        @block.gpsimd
        def _(pool):
            g = nc.gpsimd
            g.memset(ident[:, :], 0.0).then_inc(consts, 1)
            g.memset(ones[:, :], 1.0).then_inc(consts, 1)
            pool.wait_ge(consts, 2)
            g.affine_select(out=ident[:, :], in_=ident[:, :], compare_op=ALU.not_equal, fill=1.0, base=0,
                            pattern=[[-1, P]], channel_multiplier=1).then_inc(consts, 1)
            g.affine_select(out=t_le[:, :], in_=ones[:, :], compare_op=ALU.is_ge, fill=0.0, base=0,
                            pattern=[[1, P]], channel_multiplier=-1).then_inc(consts, 1)
            g.affine_select(out=t_lt[:, :], in_=ones[:, :], compare_op=ALU.is_ge, fill=0.0, base=-1,
                            pattern=[[1, P]], channel_multiplier=-1).then_inc(consts, 1)
            g.affine_select(out=t_gt[:, :], in_=ones[:, :], compare_op=ALU.is_ge, fill=0.0, base=-1,
                            pattern=[[-1, P]], channel_multiplier=1).then_inc(consts, 1)
            g.memset(causal[:, :], 0.0).then_inc(consts, 1)
            pool.wait_ge(consts, 7)
            g.affine_select(out=t_str[:, :].rearrange("p (b q) -> p b q", b=NB),
                            in_=t_le[:, :].rearrange("p (b q) -> p b q", b=NB), compare_op=ALU.is_ge, fill=0.0,
                            base=0, pattern=[[-NQ, NB], [0, NQ]], channel_multiplier=1).then_inc(consts, 1)
            g.affine_select(out=causal[:, :], in_=causal[:, :], compare_op=ALU.is_ge, fill=NEG, base=0,
                            pattern=[[-1, P]], channel_multiplier=1).then_inc(consts, 1)
            g.affine_select(out=of_stream[:, :], in_=ones[:, 0:NB], compare_op=ALU.is_ge, fill=0.0, base=0,
                            pattern=[[-NQ, NB]], channel_multiplier=1).then_inc(consts, 1)
            pool.wait_ge(consts, 10)
            g.affine_select(out=of_stream[:, :], in_=of_stream[:, :], compare_op=ALU.is_ge, fill=0.0, base=NQ - 1,
                            pattern=[[NQ, NB]], channel_multiplier=-1).then_inc(consts, 1)
            g.iota(iota_q[:, :], [[1, NQ]], base=0, channel_multiplier=0,
                   allow_small_or_imprecise_dtypes=True).then_inc(consts, 1)
            g.iota(iota_e[:, :], [[1, E]], base=0, channel_multiplier=0,
                   allow_small_or_imprecise_dtypes=True).then_inc(consts, 1)
            g.iota(tok_id[:, :], [[P, TT]], base=0, channel_multiplier=1,
                   allow_small_or_imprecise_dtypes=True).then_inc(consts, 1)
            g.iota(pid[:, :], [[0, 1]], base=0, channel_multiplier=1).then_inc(consts, 1)
            g.iota(pair_no[:, :], [[P, 2 * TT]], base=-EMPTY, channel_multiplier=1,
                   allow_small_or_imprecise_dtypes=True).then_inc(consts, 1)
            g.memset(nc_p[:, :], 0.0).then_inc(consts, 1)
            g.memset(r_qz[:, :], 0.0).then_inc(qz_zero, 1)
            g.memset(pnorm[0][:, :], 0.0).then_inc(consts, 1)
            g.memset(pnorm[1][:, :], 0.0).then_inc(consts, 1)
            g.memset(Up[:, :, 0:2], 0.0).then_inc(consts, 1)
            for t in range(TT):
                kdst = o["k_p"][t * P:(t + 1) * P, :] if t < QT else o["k_s"]
                pool.wait_ge(t_evac, T_K + t + 1)
                pool.dma_start(kdst, krow[t % 2]).then_inc(st_krow[t % 2], 16)
            pool.wait_ge(lf_done, 1)
            pool.dma_start(o["lf_p"].rearrange("(t p) h -> p t h", p=P), lf[:, 0:QT, :]).then_inc(st_out, 16)
            pool.dma_start(o["lf_s"], lf[:, QT, :]).then_inc(st_out, 16)
            for t in range(TT):
                vdst = o["v_p"][t * P:(t + 1) * P, :] if t < QT else o["v_s"]
                pool.wait_ge(*g_place[2 * CT + t])
                pool.dma_start(vdst, V[:, t, :]).then_inc(st_v, 16)
            for b in range(NB):
                if b == 0:
                    pool.wait_ge(ld_small, 7 * 16)
                if b >= 2:
                    pool.wait_ge(s_full, 2 * H + b - 1)
                g.tensor_copy(lfx[b % 2][:, :, :], lfc[:, b, :].unsqueeze(2).to_broadcast([P, H, NQ])).then_inc(lfx_done, 1)
            pool.wait_ge(t_evac, T_LAST + 1)
            pool.dma_start(o["conv_p"], last_row[0:2, :]).then_inc(st_out, 16)
            pool.dma_start(o["conv_s"], last_row[2:2 + 2 * NB, :]).then_inc(st_out, 16)
            pool.wait_ge(ssab_full, 1)
            g.iota(slot_no, [[1, P]], base=0, channel_multiplier=0, allow_small_or_imprecise_dtypes=True).then_inc(slot_zero, 1)
            pool.wait_ge(sca_done, 1)

            def step(n, u, i, first):
                if not first:
                    pool.wait_ge(scattered[u], i * 16)
                g.tensor_copy(sidx_now[u][:, :], sca_i[:, bass.ds(n, 1)]).then_inc(sidx_set, 1)
                pool.wait_ge(sidx_set, n + 1)
                pool.wait_ge(y_evac_a, n + 1)
                pool.wait_ge(y_evac_d, n + 1)
                pool.sem_inc(pool_paced, 1)
                pool.indirect_dma_start(pair_dram, bass.IndirectOffsetOnAxis(sidx_now[u][:, 0:1], 0),
                                        y_rows[u], None,
                                        bounds_check=PAIRS - 1, oob_is_err=False).then_inc(scattered[u], 16)

            for u in range(2):
                step(u, u, 0, True)
            with pool.Fori(1, LAST + 1) as i:
                for u in range(2):
                    step(i * 2 + u, u, i, False)
            pool.wait_ge(scattered[0], DUOS // 2 * 16)
            pool.wait_ge(scattered[1], DUOS // 2 * 16)
            n_ov = pool.value_load(ov_regs[0:1, 2 * OVROWS:2 * OVROWS + 1], min_val=0, max_val=MAXOV)
            with pool.If(n_ov > 0):
                with pool.Fori(0, n_ov) as i:
                    g.tensor_copy(base_now[:, :], ov_base[:, bass.ds(i, 1)]).then_inc(ov_base_set, 1)
                    pool.wait_ge(ov_idx, i + 1)
                    pool.wait_ge(y_evac_a, i + (DUOS + 1))
                    pool.wait_ge(y_evac_d, i + (DUOS + 1))
                    pool.sem_inc(pool_paced, 1)
                    pool.indirect_dma_start(pair_dram, bass.IndirectOffsetOnAxis(sidx_now[0][0:SLOTS, 0:1], 0),
                                            y_rows[0][0:SLOTS, :], None,
                                            bounds_check=PAIRS - 1, oob_is_err=False).then_inc(scattered[0], 16)
                    pool.wait_ge(scattered[0], i * 16 + (DUOS // 2 * 16 + 16))
            pool.sem_inc(rows_done, 1)
            pool.wait_ge(st_krow[0], 32)
            pool.wait_ge(st_krow[1], 16)
            pool.wait_ge(st_out, 16 * 4)

        @block.scalar
        def _(act):
            s = nc.scalar
            chain = [0]

            def link(ins):
                chain[0] += 1
                ins.then_inc(act_chain, 1)
                act.wait_ge(act_chain, chain[0])

            for t in range(TT):
                act.wait_ge(ld_x[t], 16)
                s.activation(xs[:, t, :, :].rearrange("p k q -> p (k q)"), X[:, t, :], ACT.Square,
                             accum_out=ss[:, t:t + 1]).then_inc(ss1_done, 1)
            act.wait_ge(nv1_done, 1)
            link(s.activation(nln[:, 0:TT], nv[:, 0:TT], ACT.Ln))
            s.activation(nr0[:, 0:TT], nln[:, 0:TT], ACT.Exp, scale=-0.5).then_inc(nr1_done, 1)

            act.wait_ge(ld_gmix, 16)
            for k in range(KT):
                act.wait_ge(t_full, T_X + k + 1)
                s.activation(xT[:, k, :], bT[(T_X + k) % 2][:, 0:NTOK], ACT.Copy, scale=gmix[:, k:k + 1]).then_inc(t_evac, 1)
            act.wait_ge(t_full, T_SMALL + 1)
            s.activation(smallT[:, :], bT[T_SMALL % 2][:, 0:5 * CT], ACT.Copy).then_inc(t_evac, 1)
            act.wait_ge(t_full, T_STATE + 1)
            s.activation(Us[:, :, :, 0:2], bT[T_STATE % 2][:, 0:CT * 2 * NB].rearrange("p (c b i) -> p c b i", c=CT, b=NB),
                         ACT.Copy).then_inc(t_evac, 1)

            act.wait_ge(fz_done, 1)
            link(s.activation(fb[:, :, :], fa[:, :, :], ACT.Exp, scale=-1.0))
            s.activation(fa[:, :, :], fb[:, :, :], ACT.Ln, bias=1.0).then_inc(sp_done, 1)

            def g_copy(j):
                kind, bank = g_kinds[j], bG[j % 2]
                act.wait_ge(g_full, j + 1)
                if kind == "q":
                    if j == 0:
                        act.wait_ge(qz_zero, 1)
                    for half in range(2):
                        rows = slice(half * HD, (half + 1) * HD)
                        s.activation(qz[rows, 2 * j + half, :], bank[rows, 0:SEQ], ACT.Copy, scale=HD ** -0.5)
                        ins = s.activation(qs[rows, j, :, half, :], bank[rows, SEQ:NTOK].rearrange("p (b q) -> p b q", b=NB),
                                           ACT.Copy, scale=HD ** -0.5)
                elif kind == "k":
                    ins = s.activation(kT[:, j - CT, :], bank[:, 0:NTOK], ACT.Copy)
                elif kind == "v":
                    ins = s.activation(V[:, j - 2 * CT, :], bank[:, :], ACT.Copy)
                else:
                    ct = (j - G_FILL) // 3
                    dst = oB if kind == "C" else BT
                    ins = s.activation(dst[:, ct, :], bank[:, 0:NTOK], ACT.Copy)
                ins.then_inc(g_evac_act, 1)

            for j in range(2 * CT):
                g_copy(j)
            for t in range(TT):
                act.wait_ge(t_full, T_K + t + 1)
                if t >= 2:
                    act.wait_ge(st_krow[t % 2], 16)
                s.activation(krow[t % 2], bT[(T_K + t) % 2][:, :], ACT.Copy).then_inc(t_evac, 1)
            for t in range(TT):
                g_copy(2 * CT + t)

            for n in range(UNITS + 3):
                if 2 * H <= n + 1 < UNITS:
                    b = n + 1 - 2 * H
                    j = t_kc[b]
                    act.wait_ge(t_full, j + 1)
                    if b < 2:
                        act.wait_ge(st_krow[b], 32 if b == 0 else 16)
                    if b >= 2:
                        act.wait_ge(s_full, 2 * H + b - 2 + 1)
                    s.activation(kc[b % 2], bT[j % 2][:, :].rearrange("p (c s) -> p c s", c=CT), ACT.Copy).then_inc(t_evac, 1)
                if n < UNITS:
                    hd, q = unit(n)
                    w = PAST + NQ if hd is None else (q + 1) * P
                    act.wait_ge(nmax_done, n + 1)
                    if n >= 2:
                        act.wait_ge(pn_done, n - 1)
                    s.activation(probs[n % 2][:, 0:w], scores[n % 2][:, 0:w], ACT.Exp, bias=nmax[:, n % 2:n % 2 + 1],
                                 accum_out=psum_[:, n % 2:n % 2 + 1]).then_inc(exp_done, 1)
                for j in fill_at.get(n, []):
                    if g_kinds[j] != "h":
                        g_copy(j)
                if 0 <= n - 1 < UNITS:
                    m = n - 1
                    hd, q = unit(m)
                    w = 256 if hd is None else (q + 1) * P
                    act.wait_ge(t_full, t_p[m] + 1)
                    if m >= 2:
                        act.wait_ge(pv_full, m - 1)
                    s.activation(pT[m % 2][:, 0:w], bT[t_p[m] % 2][:, 0:w], ACT.Copy).then_inc(t_evac, 1)

            act.wait_ge(s_full, UNITS)
            act.dma_start(gbc, a["norm_ffn_g"].partition_broadcast(P)).then_inc(ld_gain, 16)
            act.wait_ge(conv_done, CT)
            s.activation(sqB[:, :, :], oB[:, :, :], ACT.Square).then_inc(sq_done, 1)
            act.wait_ge(o_evac, UNITS)
            s.activation(sqA[:, :, :], oT[:, :, :], ACT.Square).then_inc(sq_done, 1)
            act.wait_ge(sq_done, 2)
            for ct in range(CT):
                s.activation(oB[:, ct, :], oB[:, ct, :], ACT.Copy, scale=gB[:, ct:ct + 1]).then_inc(gain_done, 1)
            for ct in range(CT):
                s.activation(oT[:, ct, :], oT[:, ct, :], ACT.Copy, scale=gA[:, ct:ct + 1]).then_inc(gain_done, 1)
            act.wait_ge(t_full, T_LAST + 1)
            s.activation(last_row, bT[T_LAST % 2][0:2 + 2 * NB, :], ACT.Copy).then_inc(t_evac, 1)
            act.wait_ge(nvab_done, 1)
            link(s.activation(nln[:, 0:6], nv[:, 0:6], ACT.Ln))
            s.activation(nr0[:, 0:6], nln[:, 0:6], ACT.Exp, scale=-0.5).then_inc(nrab_done, 1)

            for t in range(TT):
                act.wait_ge(x1_done, t + 1)
                s.activation(xn2[:, t, :], X[:, t, :], ACT.Square, accum_out=ss[:, t:t + 1]).then_inc(ss2_done, 1)
                act.wait_ge(nv2_done, t + 1)
                link(s.activation(nln[:, t:t + 1], nv[:, t:t + 1], ACT.Ln))
                s.activation(nr0[:, t:t + 1], nln[:, t:t + 1], ACT.Exp, scale=-0.5).then_inc(nr2_done, 1)
                for half in range(2):
                    act.wait_ge(x2t_full, 2 * t + half + 1)
                    s.activation(x2T[:, t, 4 * half:4 * half + 4, :], bT[half][:, :].rearrange("p (k q) -> p k q", k=4),
                                 ACT.Copy).then_inc(x2t_evac, 1)
            act.wait_ge(xn2_done, TT)
            act.dma_start(gbc, a["norm_final_g"].partition_broadcast(P)).then_inc(ld_gain, 16)
            act.wait_ge(gmax_done, 1)
            s.activation(ge[:, :, :], ge[:, :, :], ACT.Exp).then_inc(gexp_done, 1)
            act.wait_ge(gmax_done, 2)
            s.activation(wd[:, :], wd[:, :], ACT.Exp).then_inc(gexp_done, 1)

            def rows_evac(n, buf, first):
                for half in range(2):
                    act.wait_ge(xgt_full, n * 2 + (half + 1))
                    if half == 0 and not first:
                        act.wait_ge(gu_full, n - 1)
                    s.activation(xgT[buf][:, 4 * half:4 * half + 4, :], bT[half][:, :].rearrange("p (k q) -> p k q", k=4),
                                 ACT.Copy).then_inc(xgt_evac, 1)

            def gate_exp(n, buf, first):
                act.wait_ge(gu_full, n + 1)
                if not first:
                    act.wait_ge(glu_done, n - 1)
                s.activation(glu[buf][:, 0:F], bG[buf][:, 0:F], ACT.Exp, scale=-1.0).then_inc(gexp, 1)

            def step(n, u, i, first, has_next):
                other = 1 - u
                if has_next:
                    rows_evac(n + 1, other, first and u == 0)
                act.wait_ge(ht_full, n + 1)
                if not (first and u == 0):
                    act.wait_ge(y_full, n)
                s.activation(hT[:, :, :], bS[0][:, 0:FT * P].rearrange("p (j q) -> p j q", j=FT), ACT.Copy).then_inc(ht_evac, 1)
                act.wait_ge(y_half, n + 1)
                if not first:
                    act.wait_ge(scattered[u], i * 16)
                s.activation(y_rows[u][:, 0:512], bO[0][:, :], ACT.Copy).then_inc(y_evac_a, 1)
                if has_next:
                    gate_exp(n + 1, other, first and u == 0)

            rows_evac(0, 0, True)
            gate_exp(0, 0, True)
            for u in range(2):
                step(u, u, 0, True, True)
            with act.Fori(1, LAST) as i:
                for u in range(2):
                    step(i * 2 + u, u, i, False, True)
            for u in range(2):
                step(LAST * 2 + u, u, LAST, False, u == 0)
            n_ov = act.value_load(ov_regs[0:1, 2 * OVROWS:2 * OVROWS + 1], min_val=0, max_val=MAXOV)
            with act.If(n_ov > 0):
                with act.Fori(0, n_ov) as i:
                    act.wait_ge(ov_xt, i + 1)
                    for half in range(2):
                        ins = s.activation(xgT[0][:, 4 * half:4 * half + 4, 0:SLOTS],
                                           bT[half][:, 0:4 * SLOTS].rearrange("p (k q) -> p k q", k=4), ACT.Copy)
                    ins.then_inc(ov_xe, 1)
                    act.wait_ge(ov_gu, i + 1)
                    s.activation(glu[0][0:SLOTS, 0:F], bG[0][0:SLOTS, 0:F], ACT.Exp, scale=-1.0).then_inc(ov_ex, 1)
                    act.wait_ge(ov_ht, i + 1)
                    s.activation(hT[:, :, 0:SLOTS], bS[0][:, 0:FT * SLOTS].rearrange("p (j q) -> p j q", j=FT), ACT.Copy).then_inc(ov_he, 1)
                    act.wait_ge(y_full, i + (DUOS + 1))
                    act.wait_ge(scattered[0], i * 16 + DUOS // 2 * 16)
                    s.activation(y_rows[0][0:SLOTS, 0:512], bO[0][0:SLOTS, :], ACT.Copy).then_inc(y_evac_a, 1)
            for t in range(TT):
                act.wait_ge(y2_done, t + 1)
                s.activation(yo[t], X[:, t, :], ACT.Square, accum_out=ss[:, t:t + 1]).then_inc(ss3_done, 1)
                act.wait_ge(nv3_done, t + 1)
                link(s.activation(nln[:, t:t + 1], nv[:, t:t + 1], ACT.Ln))
                s.activation(nr0[:, t:t + 1], nln[:, t:t + 1], ACT.Exp, scale=-0.5).then_inc(nr3_done, 1)
                act.wait_ge(out_done, t + 1)
                act.dma_start(o["y_p"][t * P:(t + 1) * P, :] if t < QT else o["y_s"], yo[t]).then_inc(st_y, 16)
            act.wait_ge(st_y, 16 * TT)

        @block.vector
        def _(dve):
            v = nc.vector
            chain = [0]

            def link(ins):
                chain[0] += 1
                ins.then_inc(dve_chain, 1)
                dve.wait_ge(dve_chain, chain[0])

            def inv_sqrt(out, n0, n1, done, count):
                dve.wait_ge(done, count)
                link(v.tensor_tensor(nt[:, n0:n1], nr0[:, n0:n1], nr0[:, n0:n1], ALU.mult))
                link(v.tensor_tensor(nt[:, n0:n1], nt[:, n0:n1], nv[:, n0:n1], ALU.mult))
                link(v.tensor_scalar(nt[:, n0:n1], nt[:, n0:n1], -0.5, 1.5, ALU.mult, ALU.add))
                link(v.tensor_tensor(out, nt[:, n0:n1], nr0[:, n0:n1], ALU.mult))

            dve.wait_ge(consts, CONSTS)
            link(v.tensor_single_scalar(pmod_i[:, :], pid[:, :], NQ - 1, ALU.bitwise_and))
            link(v.tensor_copy(pmod[:, :], pmod_i[:, :]))
            link(v.tensor_scalar(causal_s[:, :], iota_q[:, :], pmod[:, 0:1], NEG, ALU.is_gt, ALU.mult))
            link(v.tensor_scalar(same_q[:, :], iota_q[:, :], pmod[:, 0:1], None, ALU.is_equal))

            dve.wait_ge(ss1_done, TT)
            v.tensor_scalar(nv[:, 0:TT], ss[:, 0:TT], 1.0 / D, EPS, ALU.mult, ALU.add).then_inc(nv1_done, 1)
            inv_sqrt(rs1[:, :], 0, TT, nr1_done, 1)
            for t in range(TT):
                v.tensor_scalar(xs[:, t, :, :], X[:, t, :].rearrange("p (q k) -> p k q", k=KT), rs1[:, t:t + 1], None,
                                ALU.mult).then_inc(xs_done, 1)

            dve.wait_ge(ld_small, 7 * 16)
            dve.wait_ge(f_full, 1)
            link(v.tensor_tensor(fz[:, :, :], bS[0][:, 0:TT * H].rearrange("p (t h) -> p t h", t=TT),
                                 bf[:, :].unsqueeze(1).to_broadcast([P, TT, H]), ALU.add))
            v.scalar_tensor_tensor(fa[:, :, :], fz[:, :, :], -1.0, fz[:, :, :], ALU.mult, ALU.max).then_inc(fz_done, 1)
            dve.wait_ge(sp_done, 1)
            v.scalar_tensor_tensor(lf[:, :, :], fz[:, :, :], 0.0, fa[:, :, :], ALU.min, ALU.subtract).then_inc(lf_done, 1)
            dve.wait_ge(decay_full, 1)
            link(v.tensor_copy(cum[:, :, :], bS[1][:, 0:TT * H].rearrange("p (t h) -> p t h", t=TT)))
            v.tensor_single_scalar(nc_p[0:H, :], bS[1][0:H, 32:32 + SEQ], -1.0, ALU.mult)
            v.tensor_single_scalar(lfn[:, :, :], lf[:, QT, :].unsqueeze(2).to_broadcast([P, H, NQ]), -1.0, ALU.mult)
            v.tensor_tensor(cmul[:, :, :], same_q[:, :].unsqueeze(1).to_broadcast([P, H, NQ]),
                            cum[:, QT, :].unsqueeze(2).to_broadcast([P, H, NQ]), ALU.mult).then_inc(cmul_done, 1)
            dve.wait_ge(cq_full, 1)
            v.tensor_copy(cq_s[:, :], bS[0][:, 0:NB]).then_inc(decay_done, 1)
            dve.wait_ge(decay_done, 1)

            def softmax_max(n):
                hd, q = unit(n)
                sc, bank = scores[n % 2], bS[n % 2]
                dve.wait_ge(s_full, n + 1)
                if n >= 2:
                    dve.wait_ge(exp_done, n - 1)
                if hd is None:
                    cq = cq_s[:, q:q + 1]
                    v.tensor_scalar(sc[:, 0:PAST], bank[:, 0:PAST], cq, None, ALU.add)
                    ins = v.scalar_tensor_tensor(sc[:, PAST:PAST + NQ], bank[:, PAST:PAST + NQ], cq, causal_s[:, :], ALU.add, ALU.add)
                    w = PAST + NQ
                else:
                    cq = cum[:, q, hd:hd + 1]
                    if q:
                        v.tensor_scalar(sc[:, 0:P], bank[:, 0:P], cq, None, ALU.add)
                    ins = v.scalar_tensor_tensor(sc[:, q * P:(q + 1) * P], bank[:, q * P:(q + 1) * P], cq, causal[:, :], ALU.add, ALU.add)
                    w = (q + 1) * P
                ins.then_inc(s_evac, 1)
                dve.wait_ge(s_evac, n + 1)
                v.reduce_max(nmax[:, n % 2:n % 2 + 1], sc[:, 0:w], AX, negate=True).then_inc(nmax_done, 1)

            def softmax_norm(n):
                hd, q = unit(n)
                r = rrec[:, n % 2:n % 2 + 1]
                dve.wait_ge(exp_done, n + 1)
                link(v.reciprocal(r, psum_[:, n % 2:n % 2 + 1]))
                if n >= 2:
                    dve.wait_ge(t_full, t_p[n - 2] + 1)
                if hd is None:
                    link(v.memset(pnorm[n % 2][:, PAST:PAST + P], 0.0))
                    v.tensor_scalar(pnorm[n % 2][:, 0:PAST], probs[n % 2][:, 0:PAST], r, None, ALU.mult)
                    v.tensor_scalar(pnorm[n % 2][:, PAST + NQ * q:PAST + NQ * (q + 1)], probs[n % 2][:, PAST:PAST + NQ],
                                    r, None, ALU.mult).then_inc(pn_done, 1)
                else:
                    w = (q + 1) * P
                    v.tensor_scalar(pnorm[n % 2][:, 0:w], probs[n % 2][:, 0:w], r, None, ALU.mult).then_inc(pn_done, 1)

            def out_evac_unit(n):
                hd, q = unit(n)
                bank = bO[n % 2]
                dve.wait_ge(pv_full, n + 1)
                if hd is None:
                    for half in range(2):
                        rows = slice(half * HD, (half + 1) * HD)
                        src = bank[rows, 0:CT * 2 * NQ].rearrange("p (c s q) -> p c s q", c=CT, s=2)[:, :, half, :]
                        ins = v.tensor_copy(oT[rows, :, SEQ + q * NQ:SEQ + (q + 1) * NQ], src)
                else:
                    rows = slice((hd % 2) * HD, (hd % 2 + 1) * HD)
                    ins = v.tensor_copy(oT[rows, hd // 2, q * P:(q + 1) * P], bank[rows, 0:P])
                ins.then_inc(o_evac, 1)

            def conv_in(j):
                ct = (j - G_FILL) // 3
                bank = bG[j % 2]
                dve.wait_ge(*g_place[j - 1])
                dve.wait_ge(g_full, j + 1)
                v.tensor_tensor(Up[:, ct, 2:2 + SEQ], bank[:, 0:SEQ], oB[:, ct, 0:SEQ], ALU.mult)
                v.tensor_tensor(Us[:, ct, :, 2:2 + NQ], bank[:, SEQ:NTOK].rearrange("p (b q) -> p b q", b=NB),
                                oB[:, ct, SEQ:NTOK].rearrange("p (b q) -> p b q", b=NB), ALU.mult).then_inc(g_evac_dve, 1)
                dve.wait_ge(g_evac_dve, ct + 1)
                v.tensor_copy(last[:, ct, 0:2], Up[:, ct, SEQ:SEQ + 2])
                v.tensor_copy(last[:, ct, 2:2 + 2 * NB].rearrange("p (b i) -> p b i", b=NB), Us[:, ct, :, NQ:NQ + 2])\
                    .then_inc(last_done, 1)

            def conv(ct):
                dve.wait_ge(*g_place[G_FILL + 3 * ct + 2])
                tp = tmpc[:, 0:SEQ]
                ts = tmpc[:, SEQ:NTOK].rearrange("p (b q) -> p b q", b=NB)
                w = [cw[:, i, ct:ct + 1] for i in range(3)]
                v.tensor_scalar(tp, Up[:, ct, 0:SEQ], w[0], None, ALU.mult)
                link(v.tensor_scalar(ts, Us[:, ct, :, 0:NQ], w[0], None, ALU.mult))
                for i in (1, 2):
                    v.scalar_tensor_tensor(tp, Up[:, ct, i:i + SEQ], w[i], tp, ALU.mult, ALU.add)
                    link(v.scalar_tensor_tensor(ts, Us[:, ct, :, i:i + NQ], w[i], ts, ALU.mult, ALU.add))
                v.tensor_tensor(oB[:, ct, :], tmpc[:, :], BT[:, ct, :], ALU.mult).then_inc(conv_done, 1)

            ready = []
            for n in range(UNITS + 3):
                if 0 <= n - 1 < UNITS:
                    softmax_norm(n - 1)
                if n < UNITS:
                    softmax_max(n)
                for ct in ready:
                    conv(ct)
                ready = []
                for j in fill_at.get(n, []):
                    if g_kinds[j] == "h":
                        conv_in(j)
                    if g_kinds[j] == "B":
                        ready.append((j - G_FILL) // 3)
                if 0 <= n - 3 < UNITS:
                    out_evac_unit(n - 3)

            dve.wait_ge(ssab_full, 1)
            v.tensor_scalar(nv[:, 0:6], bT[0][:, 0:6], 1.0 / A, EPS, ALU.mult, ALU.add).then_inc(nvab_done, 1)
            inv_sqrt(rs_ab[:, :], 0, 6, nrab_done, 1)
            dve.wait_ge(st_v, 16 * TT)
            link(v.memset(lg[:, :, 0:8], NEG))
            for t in range(TT):
                bB = bG if t % 2 == 0 else bO
                dve.wait_ge(out_full, t + 1)
                for j in range(2):
                    cs = slice(512 * j, 512 * j + 512)
                    ins = v.scalar_tensor_tensor(X[:, t, cs], bS[j][:, :], rs_ab[:, t:t + 1], X[:, t, cs], ALU.mult, ALU.add)
                ins.then_inc(outa_evac, 1)
                dve.wait_ge(outa_evac, t + 1)
                for j in range(2):
                    cs = slice(512 * j, 512 * j + 512)
                    ins = v.scalar_tensor_tensor(X[:, t, cs], bB[j][:, :], rs_ab[:, TT + t:TT + t + 1], X[:, t, cs], ALU.mult, ALU.add)
                ins.then_inc(x1_done, 1)
                dve.wait_ge(ss2_done, t + 1)
                v.tensor_scalar(nv[:, t:t + 1], ss[:, t:t + 1], 1.0 / D, EPS, ALU.mult, ALU.add).then_inc(nv2_done, 1)
                inv_sqrt(rs2[:, t:t + 1], t, t + 1, nr2_done, t + 1)
                if t == 0:
                    dve.wait_ge(ld_gain, 16)
                v.scalar_tensor_tensor(xn2[:, t, :].rearrange("p (k q) -> p k q", k=KT),
                                       X[:, t, :].rearrange("p (q k) -> p k q", k=KT), rs2[:, t:t + 1],
                                       gbc.rearrange("p (q k) -> p k q", k=KT), ALU.mult, ALU.mult).then_inc(xn2_done, 1)
                if t == 0:
                    dve.wait_ge(ld_rt, 7 * 16)
                dve.wait_ge(lg_full, t + 1)
                v.tensor_tensor(lg[:, t, 0:G], bT[0][:, 0:G], br[:, 0:G], ALU.add)
                v.tensor_tensor(lg[:, t, 8:8 + E], bT[0][:, G:G + E], br[:, G:G + E], ALU.add).then_inc(lg_evac, 1)
            dve.wait_ge(lg_evac, TT)

            for t in range(TT):
                link(v.max(top[:, t, :], lg[:, t, 0:8]))
                v.max_index(topi[:, t, :], top[:, t, :], lg[:, t, 0:8])
            v.tensor_tensor(ge[:, :, :], lg[:, :, 0:G], top[:, :, 0:1].to_broadcast([P, TT, G]), ALU.subtract).then_inc(gmax_done, 1)
            dve.wait_ge(gmax_done, 1)
            link(v.tensor_copy(gidx[:, :], topi[:, :, 0]))
            for t in range(TT):
                ins = v.tensor_scalar(goh[:, t, :], iota_e[:, 0:G], gidx[:, t:t + 1], None, ALU.is_equal)
            link(ins)
            link(v.tensor_scalar(goh[:, :, :], goh[:, :, :], -NEG, NEG, ALU.mult, ALU.add))
            for t in range(TT):
                el = lg[:, t, 8:8 + E]
                link(v.tensor_tensor(el.rearrange("p (g e) -> p g e", g=G), el.rearrange("p (g e) -> p g e", g=G),
                                     goh[:, t, :].unsqueeze(2).to_broadcast([P, G, EG]), ALU.add))
                link(v.max(etop[:, t, :], el))
                link(v.max_index(etopi[:, t, :], etop[:, t, :], el))
            v.tensor_tensor(wd[:, :], etop[:, :, 1], etop[:, :, 0], ALU.subtract).then_inc(gmax_done, 1)
            link(v.tensor_copy(eid[:, :, :], etopi[:, :, 0:2]))
            for c in range(2):
                for t in range(TT):
                    ins = v.tensor_scalar(oh[:, c, t, :], iota_e[:, :], eid[:, t, c:c + 1], None, ALU.is_equal)
            link(ins)
            v.tensor_tensor(ohs[:, :, :], oh[:, 0, :, :], oh[:, 1, :, :], ALU.add).then_inc(oh_done, 1)
            dve.wait_ge(gexp_done, 2)
            link(v.reduce_sum(gs[:, :], ge[:, :, :], AX))
            link(v.tensor_scalar_add(wt[:, 1, :], wd[:, :], 1.0))
            link(v.tensor_tensor(gs[:, :], gs[:, :], wt[:, 1, :], ALU.mult))
            link(v.reciprocal(wt[:, 0, :], gs[:, :]))
            v.tensor_tensor(wt[:, 1, :], wt[:, 0, :], wd[:, :], ALU.mult)
            dve.wait_ge(rk_full, 1)
            v.tensor_copy(rk[:, :, :], bT[0][:, 0:TT * E].rearrange("p (t e) -> p t e", t=TT))
            link(v.tensor_copy(cnt[:, :], bT[0][:, TT * E:(TT + 1) * E]))
            for c in range(2):
                link(v.tensor_tensor(ohr[:, :, :], oh[:, c, :, :], rk[:, :, :], ALU.mult))
                link(v.reduce_sum(pos[:, c, :], ohr[:, :, :], AX))
            dve.wait_ge(slot_zero, 1)
            for c in range(2):
                for t in range(TT):
                    ins = v.tensor_scalar(ranked[:, c, t, :], slot_no[:, 0:SLOTS], pos[:, c, t:t + 1],
                                          pair_no[:, c * TT + t:c * TT + t + 1], ALU.is_equal, ALU.mult)
            ins.then_inc(key_done, 1)
            link(v.tensor_scalar(key[:, :, :], pos[:, :, :], float(SLOTS), FAR, ALU.is_ge, ALU.mult))
            link(v.tensor_tensor(key[:, :, :], key[:, :, :], pos[:, :, :], ALU.add))
            for c in range(2):
                v.scalar_tensor_tensor(okey[:, c, :], eid[:, :, c], float(LIST), pos[:, c, :], ALU.mult, ALU.add)
                ins = v.scalar_tensor_tensor(key[:, c, :], eid[:, :, c], float(SLOTS), key[:, c, :], ALU.mult, ALU.add)
            link(ins)

            def pick_step(n, buf, first, step_keys=True):
                if step_keys:
                    dve.wait_ge(pick_done, n)
                    v.tensor_scalar_add(key[:, :, :], key[:, :, :], -float(P)).then_inc(key_c, 1)
                    dve.wait_ge(key_c, n)
                if not first:
                    dve.wait_ge(xgt_full, n * 2 - 2)
                for t in range(TT):
                    ins = v.tensor_scalar(pick0[:, t, :], slot_no, key[:, 0, t:t + 1], None, ALU.is_equal)
                ins.then_inc(pick_c, 1)
                dve.wait_ge(pick_c, n + 1)
                for t in range(TT):
                    ins = v.scalar_tensor_tensor(pick[buf][:, t, :], slot_no, key[:, 1, t:t + 1], pick0[:, t, :], ALU.is_equal, ALU.add)
                ins.then_inc(pick_done, 1)

            pick_step(0, 0, True, False)
            pick_step(1, 1, True)
            dve.wait_ge(sca_full, 1)
            v.tensor_scalar_add(sca_i[:, :], bT[1][:, 0:DUOS], float(EMPTY)).then_inc(sca_done, 1)
            link(v.tensor_scalar(ovc[:, :], cnt[:, :], float(SLOTS), None, ALU.is_gt))
            for j in range(2, (LIST + SLOTS - 1) // SLOTS):
                link(v.scalar_tensor_tensor(ovc[:, :], cnt[:, :], float(SLOTS * j), ovc[:, :], ALU.is_gt, ALU.add))
            link(v.tensor_tensor_scan(ovi[:, :], ovc[:, :], ovc[:, :], 0.0, ALU.add, ALU.max))
            link(v.tensor_scalar(ovt[:, :], ovi[:, :], tok_id[:, 0:1], None, ALU.is_le))
            link(v.reduce_sum(ovr[:, 0:1], ovt[:, :], AX))
            link(v.tensor_tensor(ovx[:, :], ovt[:, :], ovc[:, :], ALU.mult))
            link(v.reduce_sum(ovr[:, 3:4], ovx[:, :], AX))
            link(v.tensor_tensor(ovr[:, 3:4], tok_id[:, 0:1], ovr[:, 3:4], ALU.subtract))
            link(v.tensor_scalar(ovr[:, 3:4], ovr[:, 3:4], 1.0, float(SLOTS), ALU.add, ALU.mult))
            link(v.scalar_tensor_tensor(ovr[:, 1:2], ovr[:, 0:1], float(LIST), ovr[:, 3:4], ALU.mult, ALU.add))
            v.tensor_copy(ovr[:, 2:3], ovi[:, E - 1:E]).then_inc(ovr_done, 1)
            dve.wait_ge(ovr_full, 1)
            v.tensor_copy(ov_base[:, :], bG[1][:, 0:OVROWS])
            v.tensor_copy(ov_regs[:, :], bG[0][0:1, 0:3 * OVROWS]).then_inc(ovr_regs, 1)

            def swiglu(n, buf, first):
                gl, bank = glu[buf], bG[buf]
                dve.wait_ge(gexp, n + 1)
                v.tensor_scalar_add(gl[:, 0:F], gl[:, 0:F], 1.0).then_inc(glu_c, 1)
                dve.wait_ge(glu_c, n * 3 + 1)
                v.reciprocal(gl[:, 0:F], gl[:, 0:F]).then_inc(glu_c, 1)
                dve.wait_ge(glu_c, n * 3 + 2)
                v.tensor_tensor(gl[:, 0:F], gl[:, 0:F], bank[:, 0:F], ALU.mult).then_inc(glu_c, 1)
                dve.wait_ge(glu_c, n * 3 + 3)
                if not first:
                    dve.wait_ge(ht_full, n - 1)
                v.tensor_tensor(gl[:, F:2 * F], gl[:, 0:F], bank[:, F:2 * F], ALU.mult).then_inc(glu_done, 1)

            def step(n, u, i, first, has_next, has_two_more):
                if has_two_more:
                    pick_step(n + 2, u, False)
                dve.wait_ge(y_full, n + 1)
                if not first:
                    dve.wait_ge(scattered[u], i * 16)
                v.tensor_copy(y_rows[u][:, 512:D], bO[1][:, :]).then_inc(y_evac_d, 1)
                if has_next:
                    swiglu(n + 1, 1 - u, first and u == 0)

            swiglu(0, 0, True)
            for u in range(2):
                step(u, u, 0, True, True, True)
            with dve.Fori(1, LAST) as i:
                for u in range(2):
                    step(i * 2 + u, u, i, False, True, True)
            for u in range(2):
                step(LAST * 2 + u, u, LAST, False, u == 0, False)
            dve.wait_ge(xgt_full, 2 * DUOS)
            n_ov = dve.value_load(ov_regs[0:1, 2 * OVROWS:2 * OVROWS + 1], min_val=0, max_val=MAXOV)
            with dve.If(n_ov > 0):
                with dve.Fori(0, n_ov) as i:
                    dve.wait_ge(ov_base_set, i + 1)
                    for c in range(2):
                        for t in range(TT):
                            ins = v.tensor_scalar(ranked[:, c, t, :], slot_no[:, 0:SLOTS], base_now[:, 0:1],
                                                  okey[:, c, t:t + 1], ALU.add, ALU.is_equal)
                    ins.then_inc(ov_c, 1)
                    dve.wait_ge(ov_c, i * 4 + 1)
                    v.tensor_tensor(pick[0][:, :, 0:SLOTS], ranked[:, 0, :, :], ranked[:, 1, :, :], ALU.add).then_inc(ov_pick, 1)
                    dve.wait_ge(ov_no, i + 1)
                    v.tensor_scalar_add(sidx_now[0][0:SLOTS, :], bS[1][0:SLOTS, 0:1], float(EMPTY)).then_inc(ov_idx, 1)
                    gl, bank = glu[0][0:SLOTS, :], bG[0][0:SLOTS, :]
                    dve.wait_ge(ov_ex, i + 1)
                    v.tensor_scalar_add(gl[:, 0:F], gl[:, 0:F], 1.0).then_inc(ov_c, 1)
                    dve.wait_ge(ov_c, i * 4 + 2)
                    v.reciprocal(gl[:, 0:F], gl[:, 0:F]).then_inc(ov_c, 1)
                    dve.wait_ge(ov_c, i * 4 + 3)
                    v.tensor_tensor(gl[:, 0:F], gl[:, 0:F], bank[:, 0:F], ALU.mult).then_inc(ov_c, 1)
                    dve.wait_ge(ov_c, i * 4 + 4)
                    v.tensor_tensor(gl[:, F:2 * F], gl[:, 0:F], bank[:, F:2 * F], ALU.mult).then_inc(ov_glu, 1)
                    dve.wait_ge(y_full, i + (DUOS + 1))
                    dve.wait_ge(scattered[0], i * 16 + DUOS // 2 * 16)
                    v.tensor_copy(y_rows[0][0:SLOTS, 512:D], bO[1][0:SLOTS, :]).then_inc(y_evac_d, 1)

            dve.wait_ge(ld_gain, 32)
            for t in range(TT):
                for c in range(2):
                    dve.wait_ge(ld_pair[2 * t + c], 16)
                    ins = v.scalar_tensor_tensor(X[:, t, :], yp[t][c], wt[:, c, t:t + 1], X[:, t, :], ALU.mult, ALU.add)
                    if c == 0:
                        link(ins)
                ins.then_inc(y2_done, 1)
            for t in range(TT):
                dve.wait_ge(ss3_done, t + 1)
                v.tensor_scalar(nv[:, t:t + 1], ss[:, t:t + 1], 1.0 / D, EPS, ALU.mult, ALU.add).then_inc(nv3_done, 1)
                inv_sqrt(rs3[:, t:t + 1], t, t + 1, nr3_done, t + 1)
                v.scalar_tensor_tensor(yo[t], X[:, t, :], rs3[:, t:t + 1], gbc, ALU.mult, ALU.mult).then_inc(out_done, 1)

        @block.tensor
        def _(pe):
            te = nc.tensor

            def mm(out, lhsT, rhs, start=True, stop=True, **kw):
                return te.matmul(out, lhsT, rhs, start=start, stop=stop, **kw)

            def t_bank(j):
                if j >= 2:
                    pe.wait_ge(t_evac, j - 1)
                return bT[j % 2]

            def project(j):
                kind = g_kinds[j]
                if j >= 2:
                    pe.wait_ge(*g_place[j - 2])
                bank = bG[j % 2]
                first_of = {"q": 0, "k": CT, "v": 2 * CT}
                n = j - first_of[kind] if kind in first_of else (j - G_FILL) // 3
                if n == 0:
                    pe.wait_ge(ld_chunk[kind], 16)
                w = chunk[kind]
                for k in range(KT):
                    if kind == "v":
                        ins = mm(bank[:, :], xT[:, k, n * P:(n + 1) * P], w[:, k, :], k == 0, k == KT - 1)
                    else:
                        ins = mm(bank[:, 0:NTOK], w[:, k, n * P:(n + 1) * P], xT[:, k, :], k == 0, k == KT - 1)
                ins.then_inc(g_full, 1)

            pe.wait_ge(consts, 3)
            pe.wait_ge(xs_done, TT)
            for k in range(KT):
                bank = t_bank(T_X + k)
                for t in range(TT):
                    ins = te.transpose(bank[:, t * P:(t + 1) * P], xs[:, t, k, :], ident[:, :])
                ins.then_inc(t_full, 1)
            pe.wait_ge(ld_small, 7 * 16)
            te.transpose(t_bank(T_SMALL)[:, 0:5 * CT], small, ident[0:5 * CT, 0:5 * CT]).then_inc(t_full, 1)
            bank = t_bank(T_STATE)
            for ct in range(CT):
                ins = te.transpose(bank[:, ct * 2 * NB:(ct + 1) * 2 * NB], state[:, ct * P:(ct + 1) * P],
                                   ident[0:2 * NB, 0:2 * NB])
            ins.then_inc(t_full, 1)
            pe.wait_ge(t_evac, T_X + KT)
            for t in range(TT):
                for k in range(KT):
                    ins = mm(bS[0][:, t * H:(t + 1) * H], xT[:, k, t * P:(t + 1) * P], wf[:, k, :], k == 0, k == KT - 1)
            ins.then_inc(f_full, 1)
            for j in range(2 * CT):
                project(j)
            for t in range(TT):
                bank = t_bank(T_K + t)
                if t == 0:
                    pe.wait_ge(*g_place[2 * CT - 1])
                for ct in range(CT):
                    ins = te.transpose(bank[:, ct * P:(ct + 1) * P], kT[:, ct, t * P:(t + 1) * P], ident[:, :])
                ins.then_inc(t_full, 1)
            pe.wait_ge(consts, CONSTS)
            pe.wait_ge(lf_done, 1)
            tri = [t_le, t_le, t_str]
            for t in range(TT):
                mm(bS[1][:, t * H:(t + 1) * H], tri[t][:, :], lf[:, t, :], True, t != 1)
                if t == 1:
                    mm(bS[1][:, H:2 * H], ones[:, :], lf[:, 0, :], False, True)
            for t in range(QT):
                dst = bS[1][0:H, 32 + t * P:32 + (t + 1) * P]
                mm(dst, lf[:, t, :], tri[t][:, :], True, t != 1)
                if t == 1:
                    ins = mm(dst, lf[:, 0, :], ones[:, :], False, True)
            ins.then_inc(decay_full, 1)
            for t in range(TT):
                project(2 * CT + t)
            pe.wait_ge(cmul_done, 1)
            mm(bS[0][:, 0:NB], cmul[:, :, :].rearrange("p h q -> p (h q)"), of_stream[:, :]).then_inc(cq_full, 1)

            def scores_of(n):
                hd, q = unit(n)
                bank = bS[n % 2]
                if n == 0:
                    pe.wait_ge(decay_done, 1)
                if n >= 2:
                    pe.wait_ge(s_evac, n - 1)
                if hd is None:
                    b = q
                    new = slice(SEQ + b * NQ, SEQ + (b + 1) * NQ)
                    pe.wait_ge(t_evac, t_kc[b] + 1)
                    pe.wait_ge(lfx_done, b + 1)
                    mm(bank[:, 0:PAST], lfx[b % 2][:, :, :].rearrange("p h q -> p (h q)"), t_gt[:, :],
                       True, False, skip_group_check=True)
                    mm(bank[:, PAST:PAST + NQ], lfn[:, :, :].rearrange("p h q -> p (h q)"), t_str[:, b * NQ:(b + 1) * NQ],
                       False, False, skip_group_check=True)
                    for c in range(CT):
                        rows = slice(2 * NQ * c, 2 * NQ * (c + 1))
                        lhsT = qs[:, c, b, :, :].rearrange("p s q -> p (s q)")
                        mm(bank[rows, 0:PAST], lhsT, kc[b % 2][:, c, :], False, True, skip_group_check=True)
                        ins = mm(bank[rows, PAST:PAST + NQ], lhsT, kT[:, c, new], False, True, skip_group_check=True)
                else:
                    w = (q + 1) * P
                    mm(bank[:, 0:w], ident[:, hd:hd + 1].to_broadcast([P, P]), nc_p[:, 0:w], True, False)
                    ins = mm(bank[:, 0:w], qz[:, hd, q * P:(q + 1) * P], kT[:, hd // 2, 0:w], False, True)
                ins.then_inc(s_full, 1)

            def probs_transpose(n):
                hd, q = unit(n)
                blocks = 2 if hd is None else q + 1
                bank = t_bank(t_p[n])
                pe.wait_ge(pn_done, n + 1)
                for k in range(blocks):
                    ins = te.transpose(bank[:, k * P:(k + 1) * P], pnorm[n % 2][:, k * P:(k + 1) * P], ident[:, :])
                ins.then_inc(t_full, 1)

            def weighted_values(n):
                hd, q = unit(n)
                bank = bO[n % 2]
                pe.wait_ge(t_evac, t_p[n] + 1)
                if n >= 2:
                    pe.wait_ge(o_evac, n - 1)
                if n == 0:
                    pe.wait_ge(*g_place[2 * CT + TT - 1])
                if hd is None:
                    pe.wait_ge(ld_cv[q % 4], 16 * (q // 4 + 1))
                    for c in range(CT):
                        cs = slice(c * 2 * NQ, (c + 1) * 2 * NQ)
                        mm(bank[:, cs], cv[q % 4][:, c * P:(c + 1) * P], pT[n % 2][:, cs], True, False)
                        ins = mm(bank[:, cs], V[:, QT, c * P:(c + 1) * P], pT[n % 2][:, P + c * 2 * NQ:P + (c + 1) * 2 * NQ], False, True)
                else:
                    rows = slice((hd % 2) * HD, (hd % 2 + 1) * HD)
                    for k in range(q + 1):
                        ins = mm(bank[rows, 0:P], V[:, k, hd * HD:(hd + 1) * HD], pT[n % 2][:, k * P:(k + 1) * P], k == 0, k == q)
                ins.then_inc(pv_full, 1)

            for n in range(UNITS + 3):
                if 2 * H <= n + 1 < UNITS:
                    b = n + 1 - 2 * H
                    bank = t_bank(t_kc[b])
                    pe.wait_ge(ld_ck[b % 4], 16 * (b // 4 + 1))
                    for c in range(CT):
                        ins = te.transpose(bank[:, c * P:(c + 1) * P], ck[b % 4][:, c * P:(c + 1) * P], ident[:, :])
                    ins.then_inc(t_full, 1)
                if n < UNITS:
                    scores_of(n)
                for j in fill_at.get(n, []):
                    project(j)
                if 0 <= n - 1 < UNITS:
                    probs_transpose(n - 1)
                if 0 <= n - 2 < UNITS:
                    weighted_values(n - 2)

            bank = t_bank(T_LAST)
            pe.wait_ge(last_done, CT)
            for ct in range(CT):
                ins = te.transpose(bank[0:2 + 2 * NB, ct * P:(ct + 1) * P], last[:, ct, :], ident[:, :])
            ins.then_inc(t_full, 1)
            pe.wait_ge(t_evac, T_LAST + 1)
            pe.wait_ge(sq_done, 2)
            for half, sq in enumerate((sqA, sqB)):
                for t in range(TT):
                    for ct in range(CT):
                        ins = mm(bT[0][:, half * TT + t:half * TT + t + 1], sq[:, ct, t * P:(t + 1) * P], ones[:, 0:1],
                                 ct == 0, ct == CT - 1)
            ins.then_inc(ssab_full, 1)

            def out_project(t):
                bB = bG if t % 2 == 0 else bO
                if t == 0:
                    pe.wait_ge(*g_place[-1])
                    pe.wait_ge(o_evac, UNITS)
                    pe.wait_ge(gain_done, 2 * CT)
                    pe.wait_ge(ld_wo[0], 16)
                    pe.wait_ge(ld_wo[1], 16)
                if t >= 2:
                    pe.wait_ge(x1_done, t - 1)
                for j in range(2):
                    for ct in range(CT):
                        mm(bB[j][:, :], oB[:, ct, t * P:(t + 1) * P], wo[1][:, ct, j * 512:(j + 1) * 512], ct == 0, ct == CT - 1)
                if t >= 1:
                    pe.wait_ge(outa_evac, t)
                for j in range(2):
                    for ct in range(CT):
                        ins = mm(bS[j][:, :], oT[:, ct, t * P:(t + 1) * P], wo[0][:, ct, j * 512:(j + 1) * 512], ct == 0, ct == CT - 1)
                ins.then_inc(out_full, 1)

            def router(t):
                pe.wait_ge(xn2_done, t + 1)
                if t == 0:
                    pe.wait_ge(nvab_done, 1)
                    pe.wait_ge(ld_rt, 7 * 16)
                for half in range(2):
                    if t >= 1:
                        pe.wait_ge(x2t_evac, 2 * t)
                        pe.wait_ge(lg_evac, t)
                    for k in range(4):
                        kk = half * 4 + k
                        ins = te.transpose(bT[half][:, k * P:(k + 1) * P], xn2[:, t, kk * P:(kk + 1) * P], ident[:, :])
                    ins.then_inc(x2t_full, 1)
                pe.wait_ge(x2t_evac, 2 * t + 2)
                for k in range(KT):
                    ins = mm(bT[0][:, 0:G + E], x2T[:, t, k, :], wr[:, k, :], k == 0, k == KT - 1)
                ins.then_inc(lg_full, 1)

            out_project(0)
            out_project(1)
            router(0)
            out_project(2)
            router(1)
            router(2)
            pe.wait_ge(lg_evac, TT)
            pe.wait_ge(oh_done, 1)
            for t in range(TT):
                for tp in range(t + 1):
                    mm(bT[0][:, t * E:(t + 1) * E], (t_lt if tp == t else ones)[:, :], ohs[:, tp, :], tp == 0, tp == t)
            for t in range(TT):
                ins = mm(bT[0][:, TT * E:(TT + 1) * E], ones[:, :], ohs[:, t, :], t == 0, t == TT - 1)
            ins.then_inc(rk_full, 1)
            pe.wait_ge(key_done, 1)
            for half in range(2):
                rows = slice(half * SLOTS, (half + 1) * SLOTS)
                for j in range(2 * TT):
                    ins = mm(bT[1][rows, 0:DUOS], ranked[:, j // TT, j % TT, :], oh[:, j // TT, j % TT, half::2], j == 0, j == 2 * TT - 1)
            ins.then_inc(sca_full, 1)

            def pick_rows(n, buf, k0, k1, first):
                if k0 == 0:
                    pe.wait_ge(pick_done, n + 1)
                for k in range(k0, k1):
                    if k % 4 == 0 and not first:
                        pe.wait_ge(xgt_evac, n * 2 + (k // 4 - 1))
                    for t in range(TT):
                        ins = mm(bT[k // 4][:, (k % 4) * P:(k % 4 + 1) * P], xn2[:, t, k * P:(k + 1) * P], pick[buf][:, t, :],
                                 t == 0, t == TT - 1)
                    if k % 4 == 3:
                        ins.then_inc(xgt_full, 1)

            def gate_up(n, buf, turn, first):
                for r in (2 * buf, 2 * buf + 1):
                    pe.wait_ge(ld_gu[r], turn * 16 + 16)
                if not first:
                    pe.wait_ge(glu_done, n - 1)
                for k in range(KT):
                    if k % 4 == 0:
                        pe.wait_ge(xgt_evac, n * 2 + (k // 4 + 1))
                    for h in range(2):
                        rows = slice(h * SLOTS, (h + 1) * SLOTS)
                        ins = mm(bG[buf][rows, :], xgT[buf][:, k, rows], gu_ring[:, 2 * buf + h, k * 2 * F:(k + 1) * 2 * F], k == 0, k == KT - 1)
                ins.then_inc(gu_full, 1)

            def hidden_transpose(n, buf, first):
                pe.wait_ge(glu_done, n + 1)
                if not first:
                    pe.wait_ge(ht_evac, n)
                for j in range(FT):
                    ins = te.transpose(bS[0][:, j * P:(j + 1) * P], glu[buf][:, F + j * P:F + (j + 1) * P], ident[:, :])
                ins.then_inc(ht_full, 1)

            def down(n, buf, turn, first):
                pe.wait_ge(ht_evac, n + 1)
                for r in (2 * buf, 2 * buf + 1):
                    pe.wait_ge(ld_dn[r], turn * 16 + 16)
                for half, evac, done in ((0, y_evac_a, y_half), (1, y_evac_d, y_full)):
                    if not first:
                        pe.wait_ge(evac, n)
                    for j in range(FT):
                        for h in range(2):
                            rows = slice(h * SLOTS, (h + 1) * SLOTS)
                            ins = mm(bO[half][rows, :], hT[:, j, rows],
                                     dn_ring[:, 2 * buf + h, j * D + half * 512:j * D + half * 512 + 512], j == 0, j == FT - 1)
                    ins.then_inc(done, 1)

            def step(n, u, i, first, has_next):
                if has_next:
                    pick_rows(n + 1, 1 - u, 0, KT, False)
                hidden_transpose(n, u, first and u == 0)
                down(n, u, i, first and u == 0)
                if has_next:
                    gate_up(n + 1, 1 - u, i + u, first and u == 0)

            pe.wait_ge(sca_done, 1)
            pick_rows(0, 0, 0, KT, True)
            pe.wait_ge(ovr_done, 1)
            for c in range(3):
                mm(bG[0][0:1, c * OVROWS:(c + 1) * OVROWS], ovr[0:OVROWS, c:c + 1], ident[0:OVROWS, 0:OVROWS])
            mm(bG[1][:, 0:OVROWS], ovr[0:OVROWS, 1:2].to_broadcast([OVROWS, P]), ident[0:OVROWS, 0:OVROWS]).then_inc(ovr_full, 1)
            pe.wait_ge(ovr_regs, 1)
            gate_up(0, 0, 0, True)
            for u in range(2):
                step(u, u, 0, True, True)
            with pe.Fori(1, LAST) as i:
                for u in range(2):
                    step(i * 2 + u, u, i, False, True)
            for u in range(2):
                step(LAST * 2 + u, u, LAST, False, u == 0)
            pe.wait_ge(y_evac_a, DUOS)
            pe.wait_ge(y_evac_d, DUOS)
            n_ov = pe.value_load(ov_regs[0:1, 2 * OVROWS:2 * OVROWS + 1], min_val=0, max_val=MAXOV)
            with pe.If(n_ov > 0):
                with pe.Fori(0, n_ov) as i:
                    pe.wait_ge(ov_pick, i + 1)
                    for k in range(KT):
                        for t in range(TT):
                            ins = mm(bT[k // 4][:, (k % 4) * SLOTS:(k % 4 + 1) * SLOTS], xn2[:, t, k * P:(k + 1) * P],
                                     pick[0][:, t, 0:SLOTS], t == 0, t == TT - 1)
                    ins.then_inc(ov_xt, 1)
                    for j in range(2 * TT):
                        ins = mm(bS[1][0:SLOTS, 0:1], ranked[:, j // TT, j % TT, :], pair_no[:, j:j + 1], j == 0, j == 2 * TT - 1)
                    ins.then_inc(ov_no, 1)
                    pe.wait_ge(ov_xe, i + 1)
                    pe.wait_ge(ov_w, i * 32 + 32)
                    for k in range(KT):
                        ins = mm(bG[0][0:SLOTS, :], xgT[0][:, k, 0:SLOTS], gu_ring[:, 0, k * 2 * F:(k + 1) * 2 * F], k == 0, k == KT - 1)
                    ins.then_inc(ov_gu, 1)
                    pe.wait_ge(ov_glu, i + 1)
                    pe.sem_inc(pe_paced, 1)
                    for j in range(FT):
                        ins = te.transpose(bS[0][:, j * SLOTS:(j + 1) * SLOTS], glu[0][0:SLOTS, F + j * P:F + (j + 1) * P],
                                           ident[0:SLOTS, 0:SLOTS])
                    ins.then_inc(ov_ht, 1)
                    pe.wait_ge(ov_he, i + 1)
                    pe.wait_ge(y_evac_a, i + DUOS)
                    pe.wait_ge(y_evac_d, i + DUOS)
                    for half in range(2):
                        for j in range(FT):
                            ins = mm(bO[half][0:SLOTS, :], hT[:, j, 0:SLOTS],
                                     dn_ring[:, 0, j * D + half * 512:j * D + half * 512 + 512], j == 0, j == FT - 1)
                    ins.then_inc(y_full, 1)


SHAPES = {
    "cache_k": (NB, PAST, A), "cache_v": (NB, PAST, A), "cache_logf": (NB, PAST, H), "state_conv": (2 * NB, C),
    "norm_mix_g": (D,), "w_in": (D, 3 * A + H + 3 * C), "b_forget": (H,), "conv_w": (3, C), "norm_attn_g": (A,),
    "norm_conv_g": (C,), "w_out": (A + C, D), "norm_ffn_g": (D,), "w_router_group": (D, G), "b_router_group": (G,),
    "w_router_expert": (G, D, EG), "b_router_expert": (E,), "w_expert_gate_up": (E, D, 2 * F),
    "w_expert_down": (E, F, D), "norm_final_g": (D,),
}
OUTPUTS = {
    "y_p": ((SEQ, D), (1, SEQ, D)), "y_s": ((NB * NQ, D), (NB, NQ, D)),
    "k_p": ((SEQ, A), (1, 1, SEQ, H, HD)), "v_p": ((SEQ, A), (1, 1, SEQ, H, HD)), "lf_p": ((SEQ, H), (1, 1, SEQ, H)),
    "conv_p": ((2, C), (1, 1, 2, C)), "k_s": ((NB * NQ, A), (1, NB, NQ, H, HD)), "v_s": ((NB * NQ, A), (1, NB, NQ, H, HD)),
    "lf_s": ((NB * NQ, H), (1, NB, NQ, H)), "conv_s": ((2 * NB, C), (1, NB, 2, C)),
}


def kernel(**inputs):
    import numpy as np
    import concourse.bacc as bacc
    from concourse.bass_utils import run_bass_kernel_spmd

    nc = bacc.Bacc("TRN2", target_bir_lowering=False, num_devices=1)
    arrays, a, o = {}, {}, {}
    rows = [np.asarray(inputs["x_prompt"]).reshape(SEQ, D), np.asarray(inputs["x_sample"]).reshape(NB * NQ, D)]
    laid = {"x": np.concatenate(rows)}
    for name, shape in SHAPES.items():
        laid[name] = np.asarray(inputs[name]).reshape(shape)
    for name, x in laid.items():
        x = np.ascontiguousarray(x)
        arrays[f"in_{name}"] = x
        a[name] = nc.dram_tensor(f"in_{name}", x.shape, mybir.dt.from_np(x.dtype), kind="ExternalInput").ap()
    for name, (shape, _) in OUTPUTS.items():
        o[name] = nc.dram_tensor(f"out_{name}", shape, mybir.dt.float32, kind="ExternalOutput").ap()
    build(nc, a, o)
    got = run_bass_kernel_spmd(nc, [arrays], core_ids=[0]).results[0]
    return tuple(got[f"out_{name}"].reshape(shape) for name, (_, shape) in OUTPUTS.items())
```

```python
import concourse.bass as bass
from concourse import mybir
from contextlib import ExitStack

P = 128
D = 1024
KT = D // P
SEQ = 256
NB = 8
NQ = 16
PAST = 128
H = 8
HD = 64
A = H * HD
C = D - A
CT = C // P
NTOK = SEQ + NB * NQ
TT = NTOK // P
QT = SEQ // P
G = 4
EG = 8
E = G * EG
F = 256
FT = F // P
EPS = 1e-6
NEG = -1.0e30
SLOTS = 64
LIST = NTOK
PAIRS = 2 * NTOK
DUOS = E // 2
EMPTY = 3 * NTOK
FAR = 1.0e6
RING = 4
MAXOV = PAIRS // SLOTS
OVROWS = 16 * -(-(MAXOV + 1) // 16)
LAST = E // RING - 1
CONSTS = 20
UNITS = 2 * H + NB


def build(nc, a, o):
    f32 = mybir.dt.float32
    i32 = mybir.dt.int32
    u32 = mybir.dt.uint32
    ALU = mybir.AluOpType
    ACT = mybir.ActivationFunctionType
    AX = mybir.AxisListType.X

    pair_dram = nc.dram_tensor("pair_rows", [PAIRS, D], f32, kind="Internal").ap()

    w_in = a["w_in"].rearrange("(p k) n -> p k n", k=KT)
    w_gu = a["w_expert_gate_up"].rearrange("e (p k) n -> e p (k n)", k=KT)
    w_dn = a["w_expert_down"].rearrange("e (j p) n -> e p j n", p=P)
    cols = {"q": 0, "k": A, "v": 2 * A, "f": 3 * A, "B": 3 * A + H, "C": 3 * A + H + C, "h": 3 * A + H + 2 * C}

    ctx = ExitStack()
    with ctx:
        def sb(name, shape, dt=f32):
            return ctx.enter_context(nc.sbuf_tensor(name, shape, dt))

        def sem(name):
            return ctx.enter_context(nc.semaphore(name))

        gu_ring = sb("gu_ring", [P, RING, KT * 2 * F])
        dn_ring = sb("dn_ring", [P, RING, FT * D])
        chunk = {
            "q": gu_ring[:, 0, :].rearrange("p (k n) -> p k n", k=KT),
            "k": gu_ring[:, 1, :].rearrange("p (k n) -> p k n", k=KT),
            "v": gu_ring[:, 2, :].rearrange("p (k n) -> p k n", k=KT),
            "B": gu_ring[:, 3, :].rearrange("p (k n) -> p k n", k=KT),
            "C": dn_ring[:, 0:2, :].rearrange("p r (k n) -> p (r k) n", n=C),
            "h": dn_ring[:, 2:4, :].rearrange("p r (k n) -> p (r k) n", n=C),
        }
        wo = [gu_ring[:, 0, :].rearrange("p (c n) -> p c n", c=CT),
              gu_ring[:, 1, :].rearrange("p (c n) -> p c n", c=CT)]

        X = sb("X", [P, TT, D])
        r_xs = sb("r_xs", [P, 4096])
        xs = r_xs[:, 0:TT * D].rearrange("p (t k q) -> p t k q", t=TT, k=KT)
        ck = [r_xs[:, 512 * i:512 * i + 512] for i in range(4)]
        cv = [r_xs[:, 2048 + 512 * i:2048 + 512 * i + 512] for i in range(4)]
        y_rows = [r_xs[:, D * i:D * (i + 1)] for i in range(2)]
        r_xT = sb("r_xT", [P, KT * NTOK])
        xT = r_xT[:, :].rearrange("p (k t) -> p k t", k=KT)
        x2T = r_xT[:, 0:TT * D].rearrange("p (t k q) -> p t k q", t=TT, k=KT)
        xgT = [r_xT[:, D * i:D * (i + 1)].rearrange("p (k s) -> p k s", k=KT) for i in range(2)]
        yo = [r_xT[:, D * t:D * (t + 1)] for t in range(TT)]
        r_qz = sb("r_qz", [P, H * NTOK])
        qz = r_qz[:, 0:H * SEQ].rearrange("p (h t) -> p h t", h=H)
        qs = r_qz[:, H * SEQ:].rearrange("p (c b s q) -> p c b s q", c=CT, b=NB, s=2)
        xn2 = r_qz[:, 0:TT * D].rearrange("p (t d) -> p t d", t=TT)
        r_kT = sb("r_kT", [P, CT, NTOK])
        kT = r_kT
        glu = [r_kT[:, :, :].rearrange("p c t -> p (c t)")[:, 2 * F * i:2 * F * (i + 1)] for i in range(2)]
        V = sb("V", [P, TT, A])
        BT = sb("BT", [P, CT, NTOK])
        oB = sb("oB", [P, CT, NTOK])
        r_U = sb("r_U", [P, CT * (SEQ + 2 + NB * (NQ + 2))])
        Up = r_U[:, 0:CT * (SEQ + 2)].rearrange("p (c t) -> p c t", c=CT)
        Us = r_U[:, CT * (SEQ + 2):].rearrange("p (c b t) -> p c b t", c=CT, b=NB)
        sqB = r_U[:, 0:CT * NTOK].rearrange("p (c t) -> p c t", c=CT)
        sqA = BT
        oT = sb("oT", [P, CT, NTOK])
        r_kc = sb("r_kc", [P, 2, 512])
        krow = [r_kc[:, i, :] for i in range(2)]
        kc = [r_kc[:, i, :].rearrange("p (c s) -> p c s", c=CT) for i in range(2)]
        r_sc = sb("r_sc", [P, 512])
        scores = [r_sc[:, 256 * i:256 * (i + 1)] for i in range(2)]
        last_row = r_sc[0:2 + 2 * NB, :]
        r_pr = sb("r_pr", [P, 512])
        probs = [r_pr[:, 256 * i:256 * (i + 1)] for i in range(2)]
        small = r_pr[0:5 * CT, 0:P]
        pnorm = [sb(f"pnorm{i}", [P, 256]) for i in range(2)]
        pT = [sb(f"pT{i}", [P, 256]) for i in range(2)]
        BT_flat = BT[:, :, :].rearrange("p c t -> p (c t)")
        pick = [BT_flat[:, NTOK * i:NTOK * (i + 1)].rearrange("p (t s) -> p t s", t=TT) for i in range(2)]
        pick0 = BT_flat[:, 2 * NTOK:3 * NTOK].rearrange("p (t s) -> p t s", t=TT)
        ranked = BT_flat[:, 3 * NTOK:4 * NTOK].rearrange("p (c t s) -> p c t s", c=2, t=TT)
        slot_no = r_U[:, D:D + P]
        flat = [r_xs[:, 0:D], r_xs[:, D:2 * D], r_xs[:, 2 * D:3 * D], r_xs[:, 3 * D:4 * D],
                oB[:, :, :].rearrange("p c t -> p (c t)")[:, 0:D], oT[:, :, :].rearrange("p c t -> p (c t)")[:, 0:D]]
        yp = [flat[2 * t:2 * t + 2] for t in range(TT)]
        tmpc = sb("tmpc", [P, NTOK])
        gbc = r_U[:, 0:D]

        ident = sb("ident", [P, P])
        ones = sb("ones", [P, P])
        t_le = sb("t_le", [P, P])
        t_lt = sb("t_lt", [P, P])
        t_gt = sb("t_gt", [P, P])
        t_str = sb("t_str", [P, P])
        causal = sb("causal", [P, P])
        causal_s = sb("causal_s", [P, NQ])
        iota_q = sb("iota_q", [P, NQ])
        iota_e = sb("iota_e", [P, E])
        tok_id = sb("tok_id", [P, TT])
        pid = sb("pid", [P, 1], i32)
        pmod_i = sb("pmod_i", [P, 1], i32)
        pmod = sb("pmod", [P, 1])
        same_q = sb("same_q", [P, NQ])
        of_stream = sb("of_stream", [P, NB])

        gmix = sb("gmix", [P, KT])
        smallT = sb("smallT", [P, 5 * CT])
        gA = smallT[:, 0:CT]
        gB = smallT[:, CT:2 * CT]
        cw = smallT[:, 2 * CT:5 * CT].rearrange("p (i c) -> p i c", i=3)
        state = krow[0][0:2 * NB, :]
        last = sb("last", [P, CT, 2 + 2 * NB])
        wf = sb("wf", [P, KT, H])
        bf = sb("bf", [P, H])
        wr = sb("wr", [P, KT, G + E])
        br = sb("br", [P, G + E])
        lfc = sb("lfc", [P, NB, H])
        lf = sb("lf", [P, TT, H])
        fa = sb("fa", [P, TT, H])
        fb = sb("fb", [P, TT, H])
        fz = sb("fz", [P, TT, H])
        cum = sb("cum", [P, TT, H])
        nc_p = sb("nc_p", [P, SEQ])
        lfn = sb("lfn", [P, H, NQ])
        lfx = [sb(f"lfx{i}", [P, H, NQ]) for i in range(2)]
        cmul = pT[0][:, 0:H * NQ].rearrange("p (h q) -> p h q", h=H)
        cq_s = sb("cq_s", [P, NB])
        nmax = sb("nmax", [P, 2])
        psum_ = sb("rowsum", [P, 2])
        rrec = sb("rrec", [P, 2])
        ss = sb("ss", [P, 6])
        nv = sb("nv", [P, 9])
        nln = sb("nln", [P, 9])
        nr0 = sb("nr0", [P, 9])
        nt = sb("nt", [P, 9])
        rs1 = sb("rs1", [P, TT])
        rs_ab = sb("rs_ab", [P, 2 * TT])
        rs2 = sb("rs2", [P, TT])
        rs3 = sb("rs3", [P, TT])
        taken = [0]

        def over_v(shape, dt=f32):
            n = 1
            for m in shape[1:]:
                n *= m
            ap = V_flat[0:shape[0], taken[0]:taken[0] + n]
            taken[0] += n + n % 2
            assert taken[0] <= TT * A
            if dt != f32:
                ap = ap.bitcast(dt)
            if len(shape) == 3:
                ap = ap.rearrange("p (a b) -> p a b", a=shape[1])
            if len(shape) == 4:
                ap = ap.rearrange("p (a b c) -> p a b c", a=shape[1], b=shape[2])
            return ap

        V_flat = V[:, :, :].rearrange("p t a -> p (t a)")
        lg = over_v([P, TT, 8 + E])
        top = over_v([P, TT, 8])
        topi = over_v([P, TT, 8], u32)
        gidx = over_v([P, TT])
        goh = over_v([P, TT, G])
        ge = over_v([P, TT, G])
        gs = over_v([P, TT])
        etop = over_v([P, TT, 8])
        etopi = over_v([P, TT, 8], u32)
        eid = over_v([P, TT, 2])
        oh = over_v([P, 2, TT, E])
        ohs = over_v([P, TT, E])
        rk = over_v([P, TT, E])
        cnt = over_v([P, E])
        ohr = over_v([P, TT, E])
        pos = over_v([P, 2, TT])
        pair_no = sb("pair_no", [P, 2 * TT])
        slot_key = over_v([P, 2, TT])
        okey = over_v([P, 2, TT])
        wt = over_v([P, 2, TT])
        wd = over_v([P, TT])
        sca_i = over_v([P, DUOS], u32)
        sidx_now = [sb(f"sidx_now{i}", [P, 1], u32) for i in range(2)]
        ovc = over_v([P, E])
        ovt = over_v([P, E])
        ovi = over_v([P, E])
        ovx = over_v([P, E])
        ovr = over_v([P, 4])
        ov_base = over_v([P, OVROWS])
        base_now = sb("base_now", [P, 1])
        ov_regs = sb("ov_regs", [1, 3 * OVROWS], i32)
        hT = over_v([P, FT, P])

        banks = [ctx.enter_context(nc.psum_tensor(f"bank{i}", [P, 512], f32)) for i in range(8)]
        bT, bG, bS, bO = banks[0:2], banks[2:4], banks[4:6], banks[6:8]

        ld_x = [sem(f"ld_x{t}") for t in range(TT)]
        ld_chunk = {c: sem(f"ld_{c}") for c in "qkvBCh"}
        ld_wo = [sem("ld_woA"), sem("ld_woB")]
        ld_gmix = sem("ld_gmix")
        ld_small = sem("ld_small")
        ld_rt = sem("ld_rt")
        ld_gain = sem("ld_gain")
        ld_ck = [sem(f"ld_ck{i}") for i in range(4)]
        ld_cv = [sem(f"ld_cv{i}") for i in range(4)]
        consts = sem("consts")
        act_chain = sem("act_chain")
        dve_chain = sem("dve_chain")
        ss1_done = sem("ss1_done")
        nv1_done = sem("nv1_done")
        nr1_done = sem("nr1_done")
        xs_done = sem("xs_done")
        t_full = sem("t_full")
        t_evac = sem("t_evac")
        g_full = sem("g_full")
        g_evac_act = sem("g_evac_act")
        g_evac_dve = sem("g_evac_dve")
        qz_zero = sem("qz_zero")
        f_full = sem("f_full")
        fz_done = sem("fz_done")
        sp_done = sem("sp_done")
        lf_done = sem("lf_done")
        lfx_done = sem("lfx_done")
        decay_full = sem("decay_full")
        decay_done = sem("decay_done")
        cmul_done = sem("cmul_done")
        cq_full = sem("cq_full")
        s_full = sem("s_full")
        s_evac = sem("s_evac")
        nmax_done = sem("nmax_done")
        exp_done = sem("exp_done")
        pn_done = sem("pn_done")
        pv_full = sem("pv_full")
        o_evac = sem("o_evac")
        conv_done = sem("conv_done")
        last_done = sem("last_done")
        sq_done = sem("sq_done")
        gain_done = sem("gain_done")
        nr_done = sem("nr_done")
        ss2_done = sem("ss2_done")
        rs2_done = sem("rs2_done")
        xn2_scaled = sem("xn2_scaled")
        nv2_done = sem("nv2_done")
        xn2_done = sem("xn2_done")
        gexp_done = sem("gexp_done")
        oh_done = sem("oh_done")
        rk_full = sem("rk_full")
        cnt_full = sem("cnt_full")
        ovr_done = sem("ovr_done")
        ovr_full = sem("ovr_full")
        ovr_regs = sem("ovr_regs")
        st_out = sem("st_out")
        st_v = sem("st_v")
        st_krow = [sem(f"st_krow{i}") for i in range(2)]
        ld_gu = [sem(f"ld_gu{i}") for i in range(RING)]
        ld_dn = [sem(f"ld_dn{i}") for i in range(RING)]
        sidx_set = sem("sidx_set")
        scattered = [sem(f"scattered{i}") for i in range(2)]
        slot_no_done = sem("slot_no_done")
        key_done = sem("key_done")
        sca_full = sem("sca_full")
        sca_done = sem("sca_done")
        key_c = sem("key_chain")
        pick_c = sem("pick_chain")
        pick_done = sem("pick_done")
        xgt_full = sem("xgt_full")
        xgt_evac = sem("xgt_evac")
        gu_full = sem("gu_full")
        gexp = sem("gexp")
        glu_c = sem("glu_chain")
        glu_done = sem("glu_done")
        ht_full = sem("ht_full")
        ht_evac = sem("ht_evac")
        y_half = sem("y_half")
        y_full = sem("y_full")
        y_evac_a = sem("y_evac_a")
        y_evac_d = sem("y_evac_d")
        pe_paced = sem("pe_paced")
        pool_paced = sem("pool_paced")
        ov_w = sem("ov_w")
        ov_base_set = sem("ov_base_set")
        ov_pick = sem("ov_pick")
        ov_no = sem("ov_no")
        ov_idx = sem("ov_idx")
        ov_xt = sem("ov_xt")
        ov_xe = sem("ov_xe")
        ov_gu = sem("ov_gu")
        ov_ex = sem("ov_ex")
        ov_c = sem("ov_chain")
        ov_glu = sem("ov_glu")
        ov_ht = sem("ov_ht")
        ov_he = sem("ov_he")
        rows_done = sem("rows_done")
        ld_pair = [sem(f"ld_pair{i}") for i in range(2 * TT)]
        ss3_done = sem("ss3_done")
        y2_done = sem("y2_done")
        nv3_done = sem("nv3_done")
        nr3_done = sem("nr3_done")
        out_done = sem("out_done")
        y3_done = sem("y3_done")
        st_y = sem("st_y")

        T_X, T_SMALL, T_STATE, T_K = 0, KT, KT + 1, KT + 2
        jobs_at = {}
        for f in range(3 * CT):
            jobs_at.setdefault(1 + f, []).append(("ChB"[f % 3], f // 3))
        first_oB = 3 * CT + 4
        jobs_at[first_oB - 1] = [("ssB",), ("ssA", 0)]
        for i, keys in enumerate((
                [("oB", 0, 0)], [("oB", 0, 1)], [("oA", 0, 0)], [("oA", 0, 1)],
                [("ssA", 1), ("oB", 1, 0)], [("oB", 1, 1)], [("x2", 0), ("oA", 1, 0)], [("lg", 0), ("oA", 1, 1)],
                [("oB", 2, 0)], [("oB", 2, 1)], [("x2", 1)])):
            jobs_at[first_oB + i] = keys
        AFTER = [("lg", 1), ("ssA", 2), ("oA", 2, 0), ("oA", 2, 1), ("x2", 2), ("lg", 2)]
        jobs_at[UNITS + 3] = AFTER
        at = {key: n for n in jobs_at for key in jobs_at[n]}
        assert max(n for n in at.values() if n < UNITS + 3) < UNITS + 3
        late, early = {}, {}
        for ct in range(CT):
            late.setdefault(at["B", ct] + 1, []).append(("conv", ct))
        for key in (("ssB",), ("ssA", 0), ("ssA", 1)):
            early.setdefault(at[key] + 1, []).append(key)
            late.setdefault(at[key] + 1, []).append(key)
        late.setdefault(2 * H + 3, []).append(("lg pad",))
        for t in range(TT - 1):
            done = at["oA", t, 1]
            early.setdefault(done + 1, []).append(("square", t))
            late.setdefault(done + 1, []).append(("rows", t))
            late.setdefault(done + 1, []).append(("nv2", t))
            early.setdefault(done + 2, []).insert(0, ("nr2", t))
            late.setdefault(done + 2, []).insert(0, ("rs2", t))
            assert done + 2 < at["x2", t] < at["lg", t]
        late.setdefault(at["lg", 0] + 1, []).append(("route", 0))
        nr_order = [("ssB",), ("ssA", 0), ("nr2", 0), ("ssA", 1), ("nr2", 1), ("ssA", 2), ("nr2", 2)]
        assert [k for n in sorted(early) for k in early[n] if k[0] != "square"] == nr_order[:5]
        nr_count = {key: i + 1 for i, key in enumerate(nr_order)}

        t_jobs = T_K + TT
        t_kc, t_p, t_x2 = {}, {}, {}
        for n in range(UNITS + 3):
            if 2 * H <= n + 1 < UNITS:
                t_kc[n + 1 - 2 * H] = t_jobs
                t_jobs += 1
            for key in jobs_at.get(n, []):
                if key[0] == "x2":
                    t_x2[key[1]] = t_jobs
                    t_jobs += 2
            if 0 <= n - 1 < UNITS:
                t_p[n - 1] = t_jobs
                t_jobs += 1
        T_LAST = t_jobs
        t_x2[TT - 1] = t_jobs + 1
        t_jobs += 3
        g_kinds = [("q", ct) for ct in range(CT)] + [("k", ct) for ct in range(CT)] + [("v", t) for t in range(TT)]
        g_kinds += [key for n in sorted(jobs_at) for key in jobs_at[n] if key[0] != "x2"]
        g_of = {key: j for j, key in enumerate(g_kinds)}
        g_place = []
        na = nd = 0
        for key in g_kinds:
            if key[0] in "qkvCB":
                na += 1
                g_place.append((g_evac_act, na))
            else:
                nd += 1
                g_place.append((g_evac_dve, nd))

        def unit(n):
            return (n % H, n // H) if n < 2 * H else (None, n - 2 * H)

        block = ctx.enter_context(nc.Block())

        @block.sync
        def _(sp):
            for t in range(TT):
                sp.dma_start(X[:, t, :], a["x"][t * P:(t + 1) * P, :]).then_inc(ld_x[t], 16)
                if t == 0:
                    sp.dma_start(gmix[:, :], a["norm_mix_g"].rearrange("(p k) -> p k", k=KT)).then_inc(ld_gmix, 16)
            sp.dma_start(wf[:, :, :], w_in[:, :, cols["f"]:cols["f"] + H]).then_inc(ld_small, 16)
            for c in "qkvChB":
                sp.dma_start(chunk[c], w_in[:, :, cols[c]:cols[c] + 512]).then_inc(ld_chunk[c], 16)
                if c == "q":
                    sp.dma_start(bf[:, :], a["b_forget"].partition_broadcast(P)).then_inc(ld_small, 16)
                    sp.dma_start(small[0:CT, :], a["norm_attn_g"].rearrange("(c p) -> c p", p=P)).then_inc(ld_small, 16)
                    sp.dma_start(small[CT:2 * CT, :], a["norm_conv_g"].rearrange("(c p) -> c p", p=P)).then_inc(ld_small, 16)
                    sp.dma_start(small[2 * CT:5 * CT, :], a["conv_w"].rearrange("i (c p) -> (i c) p", p=P)).then_inc(ld_small, 16)
                    sp.dma_start(state, a["state_conv"]).then_inc(ld_small, 16)
                    sp.dma_start(lfc[:, :, :], a["cache_logf"].rearrange("b s h -> s b h")).then_inc(ld_small, 16)
            sp.wait_ge(t_full, T_X + KT)
            for b in range(4):
                sp.dma_start(ck[b], a["cache_k"][b]).then_inc(ld_ck[b], 16)
                sp.dma_start(cv[b], a["cache_v"][b]).then_inc(ld_cv[b], 16)
            sp.dma_start(wr[:, :, 0:G], a["w_router_group"].rearrange("(p k) g -> p k g", k=KT)).then_inc(ld_rt, 16)
            for gi in range(G):
                sp.dma_start(wr[:, :, G + gi * EG:G + (gi + 1) * EG],
                             a["w_router_expert"][gi].rearrange("(p k) e -> p k e", k=KT)).then_inc(ld_rt, 16)
            sp.dma_start(br[:, 0:G], a["b_router_group"].partition_broadcast(P)).then_inc(ld_rt, 16)
            sp.dma_start(br[:, G:G + E], a["b_router_expert"].partition_broadcast(P)).then_inc(ld_rt, 16)
            for half, job in ((0, CT), (1, 2 * CT)):
                sp.wait_ge(g_full, job)
                sp.dma_start(wo[half], a["w_out"][half * A:(half + 1) * A, :].rearrange("(c p) n -> p c n", p=P)).then_inc(ld_wo[half], 16)
            sp.wait_ge(g_full, g_of["B", CT - 1] + 1)
            for e in (2, 3):
                sp.dma_start(gu_ring[:, e, :], w_gu[e]).then_inc(ld_gu[e], 16)
            for e in range(RING):
                sp.dma_start(dn_ring[:, e, :].rearrange("p (j n) -> p j n", j=FT), w_dn[e]).then_inc(ld_dn[e], 16)
            sp.wait_ge(g_full, g_of["ssB",] + 1)
            sp.dma_start(gbc, a["norm_ffn_g"].partition_broadcast(P)).then_inc(ld_gain, 16)
            for b in range(4, NB):
                sp.wait_ge(t_full, t_kc[b - 4] + 1)
                sp.dma_start(ck[b - 4], a["cache_k"][b]).then_inc(ld_ck[b - 4], 16)
                sp.wait_ge(pv_full, 2 * H + b - 4 + 1)
                sp.dma_start(cv[b - 4], a["cache_v"][b]).then_inc(ld_cv[b - 4], 16)
            sp.wait_ge(g_full, g_of["oA", TT - 1, 1] + 1)
            for e in (0, 1):
                sp.dma_start(gu_ring[:, e, :], w_gu[e]).then_inc(ld_gu[e], 16)
            with sp.Fori(1, E // RING) as i:
                for u in range(2):
                    sp.wait_ge(gu_full, i * 2 + (u - 1))
                    for r in (2 * u, 2 * u + 1):
                        sp.dma_start(gu_ring[:, r, :], w_gu[i * RING + r]).then_inc(ld_gu[r], 16)
                    sp.wait_ge(y_full, i * 2 + (u - 1))
                    for r in (2 * u, 2 * u + 1):
                        sp.dma_start(dn_ring[:, r, :].rearrange("p (j n) -> p j n", j=FT), w_dn[i * RING + r]).then_inc(ld_dn[r], 16)
            sp.wait_ge(ovr_regs, 1)
            sp.wait_ge(y_full, DUOS)
            n_ov = sp.value_load(ov_regs[0:1, 2 * OVROWS:2 * OVROWS + 1], min_val=0, max_val=MAXOV)
            with sp.If(n_ov > 0):
                with sp.Fori(0, n_ov) as i:
                    sp.wait_ge(y_full, i + DUOS)
                    e = sp.value_load(ov_regs[0:1, bass.ds(i, 1)], min_val=0, max_val=E - 1)
                    sp.dma_start(gu_ring[:, 0, :], w_gu[e]).then_inc(ov_w, 16)
                    sp.dma_start(dn_ring[:, 0, :].rearrange("p (j n) -> p j n", j=FT), w_dn[e]).then_inc(ov_w, 16)
            sp.wait_ge(rows_done, 1)
            for t in range(TT):
                for c in range(2):
                    sp.dma_start(yp[t][c], pair_dram[c * NTOK + t * P:c * NTOK + (t + 1) * P, :]).then_inc(ld_pair[2 * t + c], 16)

        @block.gpsimd
        def _(pool):
            g = nc.gpsimd
            g.memset(ident[:, :], 0.0).then_inc(consts, 1)
            g.memset(ones[:, :], 1.0).then_inc(consts, 1)
            pool.wait_ge(consts, 2)
            g.affine_select(out=ident[:, :], in_=ident[:, :], compare_op=ALU.not_equal, fill=1.0, base=0,
                            pattern=[[-1, P]], channel_multiplier=1).then_inc(consts, 1)
            g.affine_select(out=t_le[:, :], in_=ones[:, :], compare_op=ALU.is_ge, fill=0.0, base=0,
                            pattern=[[1, P]], channel_multiplier=-1).then_inc(consts, 1)
            g.affine_select(out=t_lt[:, :], in_=ones[:, :], compare_op=ALU.is_ge, fill=0.0, base=-1,
                            pattern=[[1, P]], channel_multiplier=-1).then_inc(consts, 1)
            g.affine_select(out=t_gt[:, :], in_=ones[:, :], compare_op=ALU.is_ge, fill=0.0, base=-1,
                            pattern=[[-1, P]], channel_multiplier=1).then_inc(consts, 1)
            g.memset(causal[:, :], 0.0).then_inc(consts, 1)
            pool.wait_ge(consts, 7)
            g.affine_select(out=t_str[:, :].rearrange("p (b q) -> p b q", b=NB),
                            in_=t_le[:, :].rearrange("p (b q) -> p b q", b=NB), compare_op=ALU.is_ge, fill=0.0,
                            base=0, pattern=[[-NQ, NB], [0, NQ]], channel_multiplier=1).then_inc(consts, 1)
            g.affine_select(out=causal[:, :], in_=causal[:, :], compare_op=ALU.is_ge, fill=NEG, base=0,
                            pattern=[[-1, P]], channel_multiplier=1).then_inc(consts, 1)
            g.affine_select(out=of_stream[:, :], in_=ones[:, 0:NB], compare_op=ALU.is_ge, fill=0.0, base=0,
                            pattern=[[-NQ, NB]], channel_multiplier=1).then_inc(consts, 1)
            pool.wait_ge(consts, 10)
            g.affine_select(out=of_stream[:, :], in_=of_stream[:, :], compare_op=ALU.is_ge, fill=0.0, base=NQ - 1,
                            pattern=[[NQ, NB]], channel_multiplier=-1).then_inc(consts, 1)
            g.iota(iota_q[:, :], [[1, NQ]], base=0, channel_multiplier=0,
                   allow_small_or_imprecise_dtypes=True).then_inc(consts, 1)
            g.iota(iota_e[:, :], [[1, E]], base=0, channel_multiplier=0,
                   allow_small_or_imprecise_dtypes=True).then_inc(consts, 1)
            g.iota(tok_id[:, :], [[P, TT]], base=0, channel_multiplier=1,
                   allow_small_or_imprecise_dtypes=True).then_inc(consts, 1)
            g.iota(pid[:, :], [[0, 1]], base=0, channel_multiplier=1).then_inc(consts, 1)
            g.iota(pair_no[:, :], [[P, 2 * TT]], base=-EMPTY, channel_multiplier=1,
                   allow_small_or_imprecise_dtypes=True).then_inc(consts, 1)
            g.memset(nc_p[:, :], 0.0).then_inc(consts, 1)
            g.memset(r_qz[:, :], 0.0).then_inc(qz_zero, 1)
            g.memset(pnorm[0][:, :], 0.0).then_inc(consts, 1)
            g.memset(pnorm[1][:, :], 0.0).then_inc(consts, 1)
            g.memset(Up[:, :, 0:2], 0.0).then_inc(consts, 1)
            for t in range(TT):
                kdst = o["k_p"][t * P:(t + 1) * P, :] if t < QT else o["k_s"]
                pool.wait_ge(t_evac, T_K + t + 1)
                pool.dma_start(kdst, krow[t % 2]).then_inc(st_krow[t % 2], 16)
            pool.wait_ge(lf_done, 1)
            pool.dma_start(o["lf_p"].rearrange("(t p) h -> p t h", p=P), lf[:, 0:QT, :]).then_inc(st_out, 16)
            pool.dma_start(o["lf_s"], lf[:, QT, :]).then_inc(st_out, 16)
            for t in range(TT):
                vdst = o["v_p"][t * P:(t + 1) * P, :] if t < QT else o["v_s"]
                pool.wait_ge(*g_place[2 * CT + t])
                pool.dma_start(vdst, V[:, t, :]).then_inc(st_v, 16)
            def gains(o_part, sq, gain, k):
                w = o_part.shape[2]
                g.tensor_tensor(sq, o_part, o_part, ALU.mult).then_inc(sq_done, 1)
                pool.wait_ge(sq_done, k)
                g.tensor_tensor(o_part, o_part, gain.unsqueeze(2).to_broadcast([P, CT, w]), ALU.mult).then_inc(gain_done, 1)

            def gains_a(t):
                pool.wait_ge(o_evac, UNITS if t == TT - 1 else (t + 1) * H)
                ts = slice(t * P, (t + 1) * P)
                gains(oT[:, :, ts], sqA[:, :, ts], gA, t + 2)

            def spread_lf(b):
                if b >= 2:
                    pool.wait_ge(s_full, 2 * H + b - 1)
                g.tensor_copy(lfx[b % 2][:, :, :], lfc[:, b, :].unsqueeze(2).to_broadcast([P, H, NQ])).then_inc(lfx_done, 1)

            pool.wait_ge(ld_small, 7 * 16)
            spread_lf(0)
            spread_lf(1)
            pool.wait_ge(t_evac, T_SMALL + 1)
            pool.wait_ge(conv_done, CT)
            gains(oB[:, :, :], sqB[:, :, :], gB, 1)
            gains_a(0)
            spread_lf(2)
            spread_lf(3)
            gains_a(1)
            for b in range(4, NB):
                spread_lf(b)
            pool.wait_ge(g_full, g_of["ssB",] + 1)
            g.iota(slot_no, [[1, P]], base=0, channel_multiplier=0, allow_small_or_imprecise_dtypes=True).then_inc(slot_no_done, 1)
            gains_a(2)
            pool.wait_ge(t_evac, T_LAST + 1)
            pool.dma_start(o["conv_p"], last_row[0:2, :]).then_inc(st_out, 16)
            pool.dma_start(o["conv_s"], last_row[2:2 + 2 * NB, :]).then_inc(st_out, 16)
            pool.wait_ge(sca_done, 1)

            def step(n, u, i, first):
                if not first:
                    pool.wait_ge(scattered[u], i * 16)
                g.tensor_copy(sidx_now[u][:, :], sca_i[:, bass.ds(n, 1)]).then_inc(sidx_set, 1)
                pool.wait_ge(sidx_set, n + 1)
                pool.wait_ge(y_evac_a, n + 1)
                pool.wait_ge(y_evac_d, n + 1)
                pool.sem_inc(pool_paced, 1)
                pool.indirect_dma_start(pair_dram, bass.IndirectOffsetOnAxis(sidx_now[u][:, 0:1], 0),
                                        y_rows[u], None,
                                        bounds_check=PAIRS - 1, oob_is_err=False).then_inc(scattered[u], 16)

            for u in range(2):
                step(u, u, 0, True)
            with pool.Fori(1, LAST + 1) as i:
                for u in range(2):
                    step(i * 2 + u, u, i, False)
            pool.wait_ge(scattered[0], DUOS // 2 * 16)
            pool.wait_ge(scattered[1], DUOS // 2 * 16)
            n_ov = pool.value_load(ov_regs[0:1, 2 * OVROWS:2 * OVROWS + 1], min_val=0, max_val=MAXOV)
            with pool.If(n_ov > 0):
                with pool.Fori(0, n_ov) as i:
                    g.tensor_copy(base_now[:, :], ov_base[:, bass.ds(i, 1)]).then_inc(ov_base_set, 1)
                    pool.wait_ge(ov_idx, i + 1)
                    pool.wait_ge(y_evac_a, i + (DUOS + 1))
                    pool.wait_ge(y_evac_d, i + (DUOS + 1))
                    pool.sem_inc(pool_paced, 1)
                    pool.indirect_dma_start(pair_dram, bass.IndirectOffsetOnAxis(sidx_now[0][0:SLOTS, 0:1], 0),
                                            y_rows[0][0:SLOTS, :], None,
                                            bounds_check=PAIRS - 1, oob_is_err=False).then_inc(scattered[0], 16)
                    pool.wait_ge(scattered[0], i * 16 + (DUOS // 2 * 16 + 16))
            pool.sem_inc(rows_done, 1)
            pool.wait_ge(st_krow[0], 32)
            pool.wait_ge(st_krow[1], 16)
            pool.wait_ge(st_out, 16 * 4)

        @block.scalar
        def _(act):
            s = nc.scalar
            chain = [0]

            def link(ins):
                chain[0] += 1
                ins.then_inc(act_chain, 1)
                act.wait_ge(act_chain, chain[0])

            for t in range(TT):
                act.wait_ge(ld_x[t], 16)
                s.activation(xs[:, t, :, :].rearrange("p k q -> p (k q)"), X[:, t, :], ACT.Square,
                             accum_out=ss[:, t:t + 1]).then_inc(ss1_done, 1)
            act.wait_ge(nv1_done, 1)
            link(s.activation(nln[:, 0:TT], nv[:, 0:TT], ACT.Ln))
            s.activation(nr0[:, 0:TT], nln[:, 0:TT], ACT.Exp, scale=-0.5).then_inc(nr1_done, 1)

            act.wait_ge(ld_gmix, 16)
            for k in range(KT):
                act.wait_ge(t_full, T_X + k + 1)
                s.activation(xT[:, k, :], bT[(T_X + k) % 2][:, 0:NTOK], ACT.Copy, scale=gmix[:, k:k + 1]).then_inc(t_evac, 1)
            act.wait_ge(t_full, T_SMALL + 1)
            s.activation(smallT[:, :], bT[T_SMALL % 2][:, 0:5 * CT], ACT.Copy).then_inc(t_evac, 1)
            act.wait_ge(t_full, T_STATE + 1)
            s.activation(Us[:, :, :, 0:2], bT[T_STATE % 2][:, 0:CT * 2 * NB].rearrange("p (c b i) -> p c b i", c=CT, b=NB),
                         ACT.Copy).then_inc(t_evac, 1)

            act.wait_ge(fz_done, 1)
            link(s.activation(fb[:, :, :], fa[:, :, :], ACT.Exp, scale=-1.0))
            s.activation(fa[:, :, :], fb[:, :, :], ACT.Ln, bias=1.0).then_inc(sp_done, 1)

            def g_copy(j):
                (kind, n), bank = g_kinds[j], bG[j % 2]
                act.wait_ge(g_full, j + 1)
                if kind == "q":
                    if n == 0:
                        act.wait_ge(qz_zero, 1)
                    for half in range(2):
                        rows = slice(half * HD, (half + 1) * HD)
                        s.activation(qz[rows, 2 * n + half, :], bank[rows, 0:SEQ], ACT.Copy, scale=HD ** -0.5)
                        ins = s.activation(qs[rows, n, :, half, :], bank[rows, SEQ:NTOK].rearrange("p (b q) -> p b q", b=NB),
                                           ACT.Copy, scale=HD ** -0.5)
                elif kind == "v":
                    ins = s.activation(V[:, n, :], bank[:, :], ACT.Copy)
                else:
                    dst = {"k": kT, "C": oB, "B": BT}[kind]
                    ins = s.activation(dst[:, n, :], bank[:, 0:NTOK], ACT.Copy)
                ins.then_inc(g_evac_act, 1)

            for j in range(2 * CT):
                g_copy(j)
            for t in range(TT):
                act.wait_ge(t_full, T_K + t + 1)
                if t >= 2:
                    act.wait_ge(st_krow[t % 2], 16)
                s.activation(krow[t % 2], bT[(T_K + t) % 2][:, :], ACT.Copy).then_inc(t_evac, 1)
            for t in range(TT):
                g_copy(2 * CT + t)

            def estimate(key):
                if key[0] == "nr2":
                    act.wait_ge(nv2_done, key[1] + 1)
                    cs = slice(6 + key[1], 7 + key[1])
                else:
                    act.wait_ge(*g_place[g_of[key]])
                    cs = slice(TT, 2 * TT) if key == ("ssB",) else slice(key[1], key[1] + 1)
                link(s.activation(nln[:, cs], nv[:, cs], ACT.Ln))
                s.activation(nr0[:, cs], nln[:, cs], ACT.Exp, scale=-0.5).then_inc(nr_done, 1)

            def square(t):
                act.wait_ge(*g_place[g_of["oA", t, 1]])
                s.activation(x2T[:, t, :, :].rearrange("p k q -> p (k q)"), X[:, t, :], ACT.Square, accum_out=ss[:, TT + t:TT + t + 1]).then_inc(ss2_done, 1)

            def x2_evac(t):
                act.wait_ge(ss2_done, t + 1)
                for half in range(2):
                    j = t_x2[t] + half
                    act.wait_ge(t_full, j + 1)
                    s.activation(x2T[:, t, 4 * half:4 * half + 4, :], bT[j % 2][:, :].rearrange("p (k q) -> p k q", k=4),
                                 ACT.Copy).then_inc(t_evac, 1)

            def scale_rows(t):
                act.wait_ge(rs2_done, t + 1)
                act.wait_ge(t_full, t_x2[t] + 2)
                s.activation(xn2[:, t, :], xn2[:, t, :], ACT.Copy, scale=rs2[:, t:t + 1]).then_inc(xn2_scaled, 1)

            for n in range(UNITS + 3):
                for key in early.get(n, []):
                    if key[0] == "square":
                        square(key[1])
                    else:
                        estimate(key)
                if 2 * H <= n + 1 < UNITS:
                    b = n + 1 - 2 * H
                    j = t_kc[b]
                    act.wait_ge(t_full, j + 1)
                    if b < 2:
                        act.wait_ge(st_krow[b], 32 if b == 0 else 16)
                    if b >= 2:
                        act.wait_ge(s_full, 2 * H + b - 2 + 1)
                    s.activation(kc[b % 2], bT[j % 2][:, :].rearrange("p (c s) -> p c s", c=CT), ACT.Copy).then_inc(t_evac, 1)
                if n < UNITS:
                    hd, q = unit(n)
                    w = PAST + NQ if hd is None else (q + 1) * P
                    act.wait_ge(nmax_done, n + 1)
                    if n >= 2:
                        act.wait_ge(pn_done, n - 1)
                    s.activation(probs[n % 2][:, 0:w], scores[n % 2][:, 0:w], ACT.Exp, bias=nmax[:, n % 2:n % 2 + 1],
                                 accum_out=psum_[:, n % 2:n % 2 + 1]).then_inc(exp_done, 1)
                for key in jobs_at.get(n, []):
                    if key[0] in "CB":
                        g_copy(g_of[key])
                    if key[0] == "x2":
                        x2_evac(key[1])
                        scale_rows(key[1])
                if 0 <= n - 1 < UNITS:
                    m = n - 1
                    hd, q = unit(m)
                    w = 256 if hd is None else (q + 1) * P
                    act.wait_ge(t_full, t_p[m] + 1)
                    if m >= 2:
                        act.wait_ge(pv_full, m - 1)
                    s.activation(pT[m % 2][:, 0:w], bT[t_p[m] % 2][:, 0:w], ACT.Copy).then_inc(t_evac, 1)

            act.wait_ge(t_full, T_LAST + 1)
            s.activation(last_row, bT[T_LAST % 2][0:2 + 2 * NB, :], ACT.Copy).then_inc(t_evac, 1)
            estimate(("ssA", TT - 1))
            square(TT - 1)
            x2_evac(TT - 1)
            estimate(("nr2", TT - 1))
            scale_rows(TT - 1)
            act.wait_ge(xn2_done, TT)
            act.dma_start(gbc, a["norm_final_g"].partition_broadcast(P)).then_inc(ld_gain, 16)
            act.wait_ge(oh_done, TT)
            s.activation(ge[:, :, :], ge[:, :, :], ACT.Exp).then_inc(gexp_done, 1)
            s.activation(wd[:, :], wd[:, :], ACT.Exp).then_inc(gexp_done, 1)

            def rows_evac(n, buf, first):
                for half in range(2):
                    act.wait_ge(xgt_full, n * 2 + (half + 1))
                    if half == 0 and not first:
                        act.wait_ge(gu_full, n - 1)
                    s.activation(xgT[buf][:, 4 * half:4 * half + 4, :], bT[half][:, :].rearrange("p (k q) -> p k q", k=4),
                                 ACT.Copy).then_inc(xgt_evac, 1)

            def gate_exp(n, buf, first):
                act.wait_ge(gu_full, n + 1)
                if not first:
                    act.wait_ge(glu_done, n - 1)
                s.activation(glu[buf][:, 0:F], bG[buf][:, 0:F], ACT.Exp, scale=-1.0).then_inc(gexp, 1)

            def step(n, u, i, first, has_next):
                other = 1 - u
                if has_next:
                    rows_evac(n + 1, other, first and u == 0)
                act.wait_ge(ht_full, n + 1)
                if not (first and u == 0):
                    act.wait_ge(y_full, n)
                s.activation(hT[:, :, :], bS[0][:, 0:FT * P].rearrange("p (j q) -> p j q", j=FT), ACT.Copy).then_inc(ht_evac, 1)
                act.wait_ge(y_half, n + 1)
                if not first:
                    act.wait_ge(scattered[u], i * 16)
                s.activation(y_rows[u][:, 0:512], bO[0][:, :], ACT.Copy).then_inc(y_evac_a, 1)
                if has_next:
                    gate_exp(n + 1, other, first and u == 0)

            rows_evac(0, 0, True)
            gate_exp(0, 0, True)
            for u in range(2):
                step(u, u, 0, True, True)
            with act.Fori(1, LAST) as i:
                for u in range(2):
                    step(i * 2 + u, u, i, False, True)
            for u in range(2):
                step(LAST * 2 + u, u, LAST, False, u == 0)
            n_ov = act.value_load(ov_regs[0:1, 2 * OVROWS:2 * OVROWS + 1], min_val=0, max_val=MAXOV)
            with act.If(n_ov > 0):
                with act.Fori(0, n_ov) as i:
                    act.wait_ge(ov_xt, i + 1)
                    for half in range(2):
                        ins = s.activation(xgT[0][:, 4 * half:4 * half + 4, 0:SLOTS],
                                           bT[half][:, 0:4 * SLOTS].rearrange("p (k q) -> p k q", k=4), ACT.Copy)
                    ins.then_inc(ov_xe, 1)
                    act.wait_ge(ov_gu, i + 1)
                    s.activation(glu[0][0:SLOTS, 0:F], bG[0][0:SLOTS, 0:F], ACT.Exp, scale=-1.0).then_inc(ov_ex, 1)
                    act.wait_ge(ov_ht, i + 1)
                    s.activation(hT[:, :, 0:SLOTS], bS[0][:, 0:FT * SLOTS].rearrange("p (j q) -> p j q", j=FT), ACT.Copy).then_inc(ov_he, 1)
                    act.wait_ge(y_full, i + (DUOS + 1))
                    act.wait_ge(scattered[0], i * 16 + DUOS // 2 * 16)
                    s.activation(y_rows[0][0:SLOTS, 0:512], bO[0][0:SLOTS, :], ACT.Copy).then_inc(y_evac_a, 1)
            for t in range(TT):
                act.wait_ge(y2_done, t + 1)
                s.activation(yo[t], X[:, t, :], ACT.Square, accum_out=ss[:, t:t + 1]).then_inc(ss3_done, 1)
            act.wait_ge(nv3_done, 1)
            link(s.activation(nln[:, 0:TT], nv[:, 0:TT], ACT.Ln))
            s.activation(nr0[:, 0:TT], nln[:, 0:TT], ACT.Exp, scale=-0.5).then_inc(nr3_done, 1)
            for t in range(TT):
                act.wait_ge(out_done, t + 1)
                act.dma_start(o["y_p"][t * P:(t + 1) * P, :] if t < QT else o["y_s"], yo[t]).then_inc(st_y, 16)
            act.wait_ge(st_y, 16 * TT)

        @block.vector
        def _(dve):
            v = nc.vector
            chain = [0]

            def link(ins):
                chain[0] += 1
                ins.then_inc(dve_chain, 1)
                dve.wait_ge(dve_chain, chain[0])

            def inv_sqrt(out, n0, n1, done, count, ready=None):
                dve.wait_ge(done, count)
                link(v.tensor_tensor(nt[:, n0:n1], nr0[:, n0:n1], nr0[:, n0:n1], ALU.mult))
                link(v.tensor_tensor(nt[:, n0:n1], nt[:, n0:n1], nv[:, n0:n1], ALU.mult))
                link(v.tensor_scalar(nt[:, n0:n1], nt[:, n0:n1], -0.5, 1.5, ALU.mult, ALU.add))
                ins = v.tensor_tensor(out, nt[:, n0:n1], nr0[:, n0:n1], ALU.mult)
                if ready is None:
                    link(ins)
                else:
                    ins.then_inc(ready, 1)

            dve.wait_ge(consts, CONSTS)
            link(v.tensor_single_scalar(pmod_i[:, :], pid[:, :], NQ - 1, ALU.bitwise_and))
            link(v.tensor_copy(pmod[:, :], pmod_i[:, :]))
            link(v.tensor_scalar(causal_s[:, :], iota_q[:, :], pmod[:, 0:1], NEG, ALU.is_gt, ALU.mult))
            link(v.tensor_scalar(same_q[:, :], iota_q[:, :], pmod[:, 0:1], None, ALU.is_equal))

            dve.wait_ge(ss1_done, TT)
            v.tensor_scalar(nv[:, 0:TT], ss[:, 0:TT], 1.0 / D, EPS, ALU.mult, ALU.add).then_inc(nv1_done, 1)
            inv_sqrt(rs1[:, :], 0, TT, nr1_done, 1)
            for t in range(TT):
                v.tensor_scalar(xs[:, t, :, :], X[:, t, :].rearrange("p (q k) -> p k q", k=KT), rs1[:, t:t + 1], None,
                                ALU.mult).then_inc(xs_done, 1)

            dve.wait_ge(ld_small, 7 * 16)
            dve.wait_ge(f_full, 1)
            link(v.tensor_tensor(fz[:, :, :], bS[0][:, 0:TT * H].rearrange("p (t h) -> p t h", t=TT),
                                 bf[:, :].unsqueeze(1).to_broadcast([P, TT, H]), ALU.add))
            v.scalar_tensor_tensor(fa[:, :, :], fz[:, :, :], -1.0, fz[:, :, :], ALU.mult, ALU.max).then_inc(fz_done, 1)
            dve.wait_ge(sp_done, 1)
            v.scalar_tensor_tensor(lf[:, :, :], fz[:, :, :], 0.0, fa[:, :, :], ALU.min, ALU.subtract).then_inc(lf_done, 1)
            dve.wait_ge(decay_full, 1)
            link(v.tensor_copy(cum[:, :, :], bS[1][:, 0:TT * H].rearrange("p (t h) -> p t h", t=TT)))
            v.tensor_single_scalar(nc_p[0:H, :], bS[1][0:H, 32:32 + SEQ], -1.0, ALU.mult)
            v.tensor_single_scalar(lfn[:, :, :], lf[:, QT, :].unsqueeze(2).to_broadcast([P, H, NQ]), -1.0, ALU.mult)
            v.tensor_tensor(cmul[:, :, :], same_q[:, :].unsqueeze(1).to_broadcast([P, H, NQ]),
                            cum[:, QT, :].unsqueeze(2).to_broadcast([P, H, NQ]), ALU.mult).then_inc(cmul_done, 1)
            dve.wait_ge(cq_full, 1)
            v.tensor_copy(cq_s[:, :], bS[0][:, 0:NB]).then_inc(decay_done, 1)
            dve.wait_ge(decay_done, 1)

            def softmax_max(n):
                hd, q = unit(n)
                sc, bank = scores[n % 2], bS[n % 2]
                dve.wait_ge(s_full, n + 1)
                if n >= 2:
                    dve.wait_ge(exp_done, n - 1)
                if hd is None:
                    cq = cq_s[:, q:q + 1]
                    v.tensor_scalar(sc[:, 0:PAST], bank[:, 0:PAST], cq, None, ALU.add)
                    ins = v.scalar_tensor_tensor(sc[:, PAST:PAST + NQ], bank[:, PAST:PAST + NQ], cq, causal_s[:, :], ALU.add, ALU.add)
                    w = PAST + NQ
                else:
                    cq = cum[:, q, hd:hd + 1]
                    if q:
                        v.tensor_scalar(sc[:, 0:P], bank[:, 0:P], cq, None, ALU.add)
                    ins = v.scalar_tensor_tensor(sc[:, q * P:(q + 1) * P], bank[:, q * P:(q + 1) * P], cq, causal[:, :], ALU.add, ALU.add)
                    w = (q + 1) * P
                ins.then_inc(s_evac, 1)
                dve.wait_ge(s_evac, n + 1)
                v.reduce_max(nmax[:, n % 2:n % 2 + 1], sc[:, 0:w], AX, negate=True).then_inc(nmax_done, 1)

            def softmax_norm(n):
                hd, q = unit(n)
                r = rrec[:, n % 2:n % 2 + 1]
                dve.wait_ge(exp_done, n + 1)
                link(v.reciprocal(r, psum_[:, n % 2:n % 2 + 1]))
                if n >= 2:
                    dve.wait_ge(t_full, t_p[n - 2] + 1)
                if hd is None:
                    link(v.memset(pnorm[n % 2][:, PAST:PAST + P], 0.0))
                    v.tensor_scalar(pnorm[n % 2][:, 0:PAST], probs[n % 2][:, 0:PAST], r, None, ALU.mult)
                    v.tensor_scalar(pnorm[n % 2][:, PAST + NQ * q:PAST + NQ * (q + 1)], probs[n % 2][:, PAST:PAST + NQ],
                                    r, None, ALU.mult).then_inc(pn_done, 1)
                else:
                    w = (q + 1) * P
                    v.tensor_scalar(pnorm[n % 2][:, 0:w], probs[n % 2][:, 0:w], r, None, ALU.mult).then_inc(pn_done, 1)

            def out_evac_unit(n):
                hd, q = unit(n)
                bank = bO[n % 2]
                dve.wait_ge(pv_full, n + 1)
                if hd is None:
                    for half in range(2):
                        rows = slice(half * HD, (half + 1) * HD)
                        src = bank[rows, 0:CT * 2 * NQ].rearrange("p (c s q) -> p c s q", c=CT, s=2)[:, :, half, :]
                        ins = v.tensor_copy(oT[rows, :, SEQ + q * NQ:SEQ + (q + 1) * NQ], src)
                else:
                    rows = slice((hd % 2) * HD, (hd % 2 + 1) * HD)
                    ins = v.tensor_copy(oT[rows, hd // 2, q * P:(q + 1) * P], bank[rows, 0:P])
                ins.then_inc(o_evac, 1)

            def conv_in(j):
                ct = g_kinds[j][1]
                bank = bG[j % 2]
                dve.wait_ge(*g_place[g_of["C", ct]])
                dve.wait_ge(g_full, j + 1)
                v.tensor_tensor(Up[:, ct, 2:2 + SEQ], bank[:, 0:SEQ], oB[:, ct, 0:SEQ], ALU.mult)
                v.tensor_tensor(Us[:, ct, :, 2:2 + NQ], bank[:, SEQ:NTOK].rearrange("p (b q) -> p b q", b=NB),
                                oB[:, ct, SEQ:NTOK].rearrange("p (b q) -> p b q", b=NB), ALU.mult).then_inc(g_evac_dve, 1)
                dve.wait_ge(*g_place[j])
                v.tensor_copy(last[:, ct, 0:2], Up[:, ct, SEQ:SEQ + 2])
                v.tensor_copy(last[:, ct, 2:2 + 2 * NB].rearrange("p (b i) -> p b i", b=NB), Us[:, ct, :, NQ:NQ + 2])\
                    .then_inc(last_done, 1)

            def conv(ct):
                dve.wait_ge(*g_place[g_of["B", ct]])
                tp = tmpc[:, 0:SEQ]
                ts = tmpc[:, SEQ:NTOK].rearrange("p (b q) -> p b q", b=NB)
                w = [cw[:, i, ct:ct + 1] for i in range(3)]
                v.tensor_scalar(tp, Up[:, ct, 0:SEQ], w[0], None, ALU.mult)
                link(v.tensor_scalar(ts, Us[:, ct, :, 0:NQ], w[0], None, ALU.mult))
                for i in (1, 2):
                    v.scalar_tensor_tensor(tp, Up[:, ct, i:i + SEQ], w[i], tp, ALU.mult, ALU.add)
                    link(v.scalar_tensor_tensor(ts, Us[:, ct, :, i:i + NQ], w[i], ts, ALU.mult, ALU.add))
                v.tensor_tensor(oB[:, ct, :], tmpc[:, :], BT[:, ct, :], ALU.mult).then_inc(conv_done, 1)

            def job_evac(key):
                j, kind = g_of[key], key[0]
                bank = bG[j % 2]
                if kind == "h":
                    return conv_in(j)
                dve.wait_ge(g_full, j + 1)
                if kind == "ssB":
                    ins = v.tensor_scalar(nv[:, TT:2 * TT], bank[:, 0:TT], 1.0 / C, EPS, ALU.mult, ALU.add)
                elif kind == "ssA":
                    t = key[1]
                    ins = v.tensor_scalar(nv[:, t:t + 1], bank[:, 0:1], 1.0 / A, EPS, ALU.mult, ALU.add)
                elif kind in ("oA", "oB"):
                    t, half = key[1:]
                    cs = slice(512 * half, 512 * half + 512)
                    rs = rs_ab[:, TT + t:TT + t + 1] if kind == "oB" else rs_ab[:, t:t + 1]
                    if kind == "oA":
                        dve.wait_ge(*g_place[g_of["oB", t, half]])
                    ins = v.scalar_tensor_tensor(X[:, t, cs], bank[:, :], rs, X[:, t, cs], ALU.mult, ALU.add)
                else:
                    t = key[1]
                    r = rs2[:, t:t + 1]
                    dve.wait_ge(rs2_done, t + 1)
                    v.scalar_tensor_tensor(lg[:, t, 0:G], bank[:, 0:G], r, br[:, 0:G], ALU.mult, ALU.add)
                    ins = v.scalar_tensor_tensor(lg[:, t, 8:8 + E], bank[:, G:G + E], r, br[:, G:G + E], ALU.mult, ALU.add)
                ins.then_inc(g_evac_dve, 1)

            def rstd(key):
                cs = slice(TT, 2 * TT) if key == ("ssB",) else slice(key[1], key[1] + 1)
                inv_sqrt(rs_ab[:, cs], cs.start, cs.stop, nr_done, nr_count[key])

            def nv2(t):
                dve.wait_ge(ss2_done, t + 1)
                v.tensor_scalar(nv[:, 6 + t:7 + t], ss[:, TT + t:TT + t + 1], 1.0 / D, EPS, ALU.mult, ALU.add).then_inc(nv2_done, 1)

            def gained_rows(t):
                dve.wait_ge(*g_place[g_of["oA", t, 0]])
                dve.wait_ge(*g_place[g_of["oA", t, 1]])
                if t == 0:
                    dve.wait_ge(ld_gain, 16)
                v.scalar_tensor_tensor(xn2[:, t, :].rearrange("p (k q) -> p k q", k=KT),
                                       X[:, t, :].rearrange("p (q k) -> p k q", k=KT), 1.0,
                                       gbc.rearrange("p (q k) -> p k q", k=KT), ALU.mult, ALU.mult).then_inc(xn2_done, 1)

            def rstd2(t):
                inv_sqrt(rs2[:, t:t + 1], 6 + t, 7 + t, nr_done, nr_count["nr2", t], rs2_done)

            def route(t):
                link(v.max(top[:, t, :], lg[:, t, 0:8]))
                link(v.max_index(topi[:, t, :], top[:, t, :], lg[:, t, 0:8]))
                v.tensor_tensor(ge[:, t, :], lg[:, t, 0:G], top[:, t, 0:1].to_broadcast([P, G]), ALU.subtract)
                link(v.tensor_copy(gidx[:, t:t + 1], topi[:, t, 0:1]))
                link(v.tensor_scalar(goh[:, t, :], iota_e[:, 0:G], gidx[:, t:t + 1], None, ALU.is_equal))
                link(v.tensor_scalar(goh[:, t, :], goh[:, t, :], -NEG, NEG, ALU.mult, ALU.add))
                el = lg[:, t, 8:8 + E]
                link(v.tensor_tensor(el.rearrange("p (g e) -> p g e", g=G), el.rearrange("p (g e) -> p g e", g=G),
                                     goh[:, t, :].unsqueeze(2).to_broadcast([P, G, EG]), ALU.add))
                link(v.max(etop[:, t, :], el))
                link(v.max_index(etopi[:, t, :], etop[:, t, :], el))
                v.tensor_tensor(wd[:, t:t + 1], etop[:, t, 1:2], etop[:, t, 0:1], ALU.subtract)
                link(v.tensor_copy(eid[:, t, :], etopi[:, t, 0:2]))
                for c in range(2):
                    ins = v.tensor_scalar(oh[:, c, t, :], iota_e[:, :], eid[:, t, c:c + 1], None, ALU.is_equal)
                link(ins)
                v.tensor_tensor(ohs[:, t, :], oh[:, 0, t, :], oh[:, 1, t, :], ALU.add).then_inc(oh_done, 1)

            for n in range(UNITS + 3):
                if 0 <= n - 1 < UNITS:
                    softmax_norm(n - 1)
                if n < UNITS:
                    softmax_max(n)
                for key in late.get(n, []):
                    if key[0] == "conv":
                        conv(key[1])
                    elif key[0] == "nv2":
                        nv2(key[1])
                    elif key[0] == "rows":
                        gained_rows(key[1])
                    elif key[0] == "route":
                        dve.wait_ge(*g_place[g_of["lg", key[1]]])
                        route(key[1])
                    elif key[0] == "rs2":
                        rstd2(key[1])
                    elif key[0] == "lg pad":
                        dve.wait_ge(pv_full, 2 * H)
                        dve.wait_ge(st_v, 16 * TT)
                        link(v.memset(lg[:, :, 0:8], NEG))
                        dve.wait_ge(ld_rt, 7 * 16)
                    else:
                        rstd(key)
                for key in jobs_at.get(n, []):
                    if key[0] not in ("C", "B", "x2"):
                        job_evac(key)
                if 0 <= n - 3 < UNITS:
                    out_evac_unit(n - 3)
            job_evac(("lg", 1))
            job_evac(("ssA", TT - 1))
            rstd(("ssA", TT - 1))
            job_evac(("oA", TT - 1, 0))
            job_evac(("oA", TT - 1, 1))
            gained_rows(TT - 1)
            nv2(TT - 1)
            dve.wait_ge(*g_place[g_of["lg", 1]])
            route(1)
            rstd2(TT - 1)
            job_evac(("lg", TT - 1))
            dve.wait_ge(*g_place[-1])
            route(TT - 1)

            dve.wait_ge(rk_full, 1)
            link(v.tensor_copy(rk[:, :, :], bT[0][:, 0:TT * E].rearrange("p (t e) -> p t e", t=TT)))
            for c in range(2):
                link(v.tensor_tensor(ohr[:, :, :], oh[:, c, :, :], rk[:, :, :], ALU.mult))
                link(v.reduce_sum(pos[:, c, :], ohr[:, :, :], AX))
            dve.wait_ge(slot_no_done, 1)
            link(v.tensor_scalar(slot_key[:, :, :], pos[:, :, :], float(SLOTS), FAR, ALU.is_ge, ALU.mult))
            link(v.tensor_tensor(slot_key[:, :, :], slot_key[:, :, :], pos[:, :, :], ALU.add))
            for c in range(2):
                v.scalar_tensor_tensor(okey[:, c, :], eid[:, :, c], float(LIST), pos[:, c, :], ALU.mult, ALU.add)
                ins = v.scalar_tensor_tensor(slot_key[:, c, :], eid[:, :, c], float(SLOTS), slot_key[:, c, :], ALU.mult, ALU.add)
            link(ins)

            def pick_step(n, buf, first, step_keys=True):
                if step_keys:
                    dve.wait_ge(pick_done, n)
                    v.tensor_scalar_add(slot_key[:, :, :], slot_key[:, :, :], -float(P)).then_inc(key_c, 1)
                    dve.wait_ge(key_c, n)
                if not first:
                    dve.wait_ge(xgt_full, n * 2 - 2)
                for t in range(TT):
                    ins = v.tensor_scalar(pick0[:, t, :], slot_no, slot_key[:, 0, t:t + 1], None, ALU.is_equal)
                ins.then_inc(pick_c, 1)
                dve.wait_ge(pick_c, n + 1)
                for t in range(TT):
                    ins = v.scalar_tensor_tensor(pick[buf][:, t, :], slot_no, slot_key[:, 1, t:t + 1], pick0[:, t, :], ALU.is_equal, ALU.add)
                ins.then_inc(pick_done, 1)

            pick_step(0, 0, True, False)
            for c in range(2):
                for t in range(TT):
                    ins = v.tensor_scalar(ranked[:, c, t, :], slot_no[:, 0:SLOTS], pos[:, c, t:t + 1],
                                          pair_no[:, c * TT + t:c * TT + t + 1], ALU.is_equal, ALU.mult)
            ins.then_inc(key_done, 1)
            pick_step(1, 1, True)
            dve.wait_ge(sca_full, 1)
            v.tensor_scalar_add(sca_i[:, :], bS[1][:, 0:DUOS], float(EMPTY)).then_inc(sca_done, 1)
            dve.wait_ge(gexp_done, 2)
            link(v.reduce_sum(gs[:, :], ge[:, :, :], AX))
            link(v.tensor_scalar_add(wt[:, 1, :], wd[:, :], 1.0))
            link(v.tensor_tensor(gs[:, :], gs[:, :], wt[:, 1, :], ALU.mult))
            link(v.reciprocal(wt[:, 0, :], gs[:, :]))
            v.tensor_tensor(wt[:, 1, :], wt[:, 0, :], wd[:, :], ALU.mult)
            dve.wait_ge(cnt_full, 1)
            link(v.tensor_copy(cnt[:, :], bS[0][:, 0:E]))
            link(v.tensor_scalar(ovc[:, :], cnt[:, :], float(SLOTS), None, ALU.is_gt))
            for j in range(2, (LIST + SLOTS - 1) // SLOTS):
                link(v.scalar_tensor_tensor(ovc[:, :], cnt[:, :], float(SLOTS * j), ovc[:, :], ALU.is_gt, ALU.add))
            link(v.tensor_tensor_scan(ovi[:, :], ovc[:, :], ovc[:, :], 0.0, ALU.add, ALU.max))
            link(v.tensor_scalar(ovt[:, :], ovi[:, :], tok_id[:, 0:1], None, ALU.is_le))
            link(v.reduce_sum(ovr[:, 0:1], ovt[:, :], AX))
            link(v.tensor_tensor(ovx[:, :], ovt[:, :], ovc[:, :], ALU.mult))
            link(v.reduce_sum(ovr[:, 3:4], ovx[:, :], AX))
            link(v.tensor_tensor(ovr[:, 3:4], tok_id[:, 0:1], ovr[:, 3:4], ALU.subtract))
            link(v.tensor_scalar(ovr[:, 3:4], ovr[:, 3:4], 1.0, float(SLOTS), ALU.add, ALU.mult))
            link(v.scalar_tensor_tensor(ovr[:, 1:2], ovr[:, 0:1], float(LIST), ovr[:, 3:4], ALU.mult, ALU.add))
            v.tensor_copy(ovr[:, 2:3], ovi[:, E - 1:E]).then_inc(ovr_done, 1)
            dve.wait_ge(ovr_full, 1)
            v.tensor_copy(ov_base[:, :], bO[1][:, 0:OVROWS])
            v.tensor_copy(ov_regs[:, :], bO[0][0:1, 0:3 * OVROWS]).then_inc(ovr_regs, 1)

            def swiglu(n, buf, first):
                gl, bank = glu[buf], bG[buf]
                dve.wait_ge(gexp, n + 1)
                v.tensor_scalar_add(gl[:, 0:F], gl[:, 0:F], 1.0).then_inc(glu_c, 1)
                dve.wait_ge(glu_c, n * 3 + 1)
                v.reciprocal(gl[:, 0:F], gl[:, 0:F]).then_inc(glu_c, 1)
                dve.wait_ge(glu_c, n * 3 + 2)
                v.tensor_tensor(gl[:, 0:F], gl[:, 0:F], bank[:, 0:F], ALU.mult).then_inc(glu_c, 1)
                dve.wait_ge(glu_c, n * 3 + 3)
                if not first:
                    dve.wait_ge(ht_full, n - 1)
                v.tensor_tensor(gl[:, F:2 * F], gl[:, 0:F], bank[:, F:2 * F], ALU.mult).then_inc(glu_done, 1)

            def step(n, u, i, first, has_next, has_two_more):
                if has_two_more:
                    pick_step(n + 2, u, False)
                dve.wait_ge(y_full, n + 1)
                if not first:
                    dve.wait_ge(scattered[u], i * 16)
                v.tensor_copy(y_rows[u][:, 512:D], bO[1][:, :]).then_inc(y_evac_d, 1)
                if has_next:
                    swiglu(n + 1, 1 - u, first and u == 0)

            swiglu(0, 0, True)
            for u in range(2):
                step(u, u, 0, True, True, True)
            with dve.Fori(1, LAST) as i:
                for u in range(2):
                    step(i * 2 + u, u, i, False, True, True)
            for u in range(2):
                step(LAST * 2 + u, u, LAST, False, u == 0, False)
            dve.wait_ge(xgt_full, 2 * DUOS)
            n_ov = dve.value_load(ov_regs[0:1, 2 * OVROWS:2 * OVROWS + 1], min_val=0, max_val=MAXOV)
            with dve.If(n_ov > 0):
                with dve.Fori(0, n_ov) as i:
                    dve.wait_ge(ov_base_set, i + 1)
                    for c in range(2):
                        for t in range(TT):
                            ins = v.tensor_scalar(ranked[:, c, t, :], slot_no[:, 0:SLOTS], base_now[:, 0:1],
                                                  okey[:, c, t:t + 1], ALU.add, ALU.is_equal)
                    ins.then_inc(ov_c, 1)
                    dve.wait_ge(ov_c, i * 4 + 1)
                    v.tensor_tensor(pick[0][:, :, 0:SLOTS], ranked[:, 0, :, :], ranked[:, 1, :, :], ALU.add).then_inc(ov_pick, 1)
                    dve.wait_ge(ov_no, i + 1)
                    v.tensor_scalar_add(sidx_now[0][0:SLOTS, :], bS[1][0:SLOTS, 0:1], float(EMPTY)).then_inc(ov_idx, 1)
                    gl, bank = glu[0][0:SLOTS, :], bG[0][0:SLOTS, :]
                    dve.wait_ge(ov_ex, i + 1)
                    v.tensor_scalar_add(gl[:, 0:F], gl[:, 0:F], 1.0).then_inc(ov_c, 1)
                    dve.wait_ge(ov_c, i * 4 + 2)
                    v.reciprocal(gl[:, 0:F], gl[:, 0:F]).then_inc(ov_c, 1)
                    dve.wait_ge(ov_c, i * 4 + 3)
                    v.tensor_tensor(gl[:, 0:F], gl[:, 0:F], bank[:, 0:F], ALU.mult).then_inc(ov_c, 1)
                    dve.wait_ge(ov_c, i * 4 + 4)
                    v.tensor_tensor(gl[:, F:2 * F], gl[:, 0:F], bank[:, F:2 * F], ALU.mult).then_inc(ov_glu, 1)
                    dve.wait_ge(y_full, i + (DUOS + 1))
                    dve.wait_ge(scattered[0], i * 16 + DUOS // 2 * 16)
                    v.tensor_copy(y_rows[0][0:SLOTS, 512:D], bO[1][0:SLOTS, :]).then_inc(y_evac_d, 1)

            dve.wait_ge(ld_gain, 32)
            for t in range(TT):
                for c in range(2):
                    dve.wait_ge(ld_pair[2 * t + c], 16)
                    ins = v.scalar_tensor_tensor(X[:, t, :], yp[t][c], wt[:, c, t:t + 1], X[:, t, :], ALU.mult, ALU.add)
                    if c == 0:
                        link(ins)
                ins.then_inc(y2_done, 1)
            dve.wait_ge(ss3_done, TT)
            v.tensor_scalar(nv[:, 0:TT], ss[:, 0:TT], 1.0 / D, EPS, ALU.mult, ALU.add).then_inc(nv3_done, 1)
            for t in range(TT):
                v.tensor_tensor(X[:, t, :], X[:, t, :], gbc, ALU.mult).then_inc(y3_done, 1)
            dve.wait_ge(y3_done, TT)
            inv_sqrt(rs3[:, :], 0, TT, nr3_done, 1)
            for t in range(TT):
                v.tensor_scalar(yo[t], X[:, t, :], rs3[:, t:t + 1], None, ALU.mult).then_inc(out_done, 1)

        @block.tensor
        def _(pe):
            te = nc.tensor

            def mm(out, lhsT, rhs, start=True, stop=True, **kw):
                return te.matmul(out, lhsT, rhs, start=start, stop=stop, **kw)

            def t_bank(j):
                if j >= 2:
                    pe.wait_ge(t_evac, j - 1)
                return bT[j % 2]

            def project(j):
                kind, n = g_kinds[j]
                if j >= 2:
                    pe.wait_ge(*g_place[j - 2])
                bank = bG[j % 2]
                if n == 0:
                    pe.wait_ge(ld_chunk[kind], 16)
                w = chunk[kind]
                for k in range(KT):
                    if kind == "v":
                        ins = mm(bank[:, :], xT[:, k, n * P:(n + 1) * P], w[:, k, :], k == 0, k == KT - 1)
                    else:
                        ins = mm(bank[:, 0:NTOK], w[:, k, n * P:(n + 1) * P], xT[:, k, :], k == 0, k == KT - 1)
                ins.then_inc(g_full, 1)

            pe.wait_ge(consts, 3)
            pe.wait_ge(xs_done, TT)
            for k in range(KT):
                bank = t_bank(T_X + k)
                for t in range(TT):
                    ins = te.transpose(bank[:, t * P:(t + 1) * P], xs[:, t, k, :], ident[:, :])
                ins.then_inc(t_full, 1)
            pe.wait_ge(ld_small, 7 * 16)
            te.transpose(t_bank(T_SMALL)[:, 0:5 * CT], small, ident[0:5 * CT, 0:5 * CT]).then_inc(t_full, 1)
            bank = t_bank(T_STATE)
            for ct in range(CT):
                ins = te.transpose(bank[:, ct * 2 * NB:(ct + 1) * 2 * NB], state[:, ct * P:(ct + 1) * P],
                                   ident[0:2 * NB, 0:2 * NB])
            ins.then_inc(t_full, 1)
            pe.wait_ge(t_evac, T_X + KT)
            for t in range(TT):
                for k in range(KT):
                    ins = mm(bS[0][:, t * H:(t + 1) * H], xT[:, k, t * P:(t + 1) * P], wf[:, k, :], k == 0, k == KT - 1)
            ins.then_inc(f_full, 1)
            for j in range(2 * CT):
                project(j)
            for t in range(TT):
                bank = t_bank(T_K + t)
                if t == 0:
                    pe.wait_ge(*g_place[2 * CT - 1])
                for ct in range(CT):
                    ins = te.transpose(bank[:, ct * P:(ct + 1) * P], kT[:, ct, t * P:(t + 1) * P], ident[:, :])
                ins.then_inc(t_full, 1)
            pe.wait_ge(consts, CONSTS)
            pe.wait_ge(lf_done, 1)
            tri = [t_le, t_le, t_str]
            for t in range(TT):
                mm(bS[1][:, t * H:(t + 1) * H], tri[t][:, :], lf[:, t, :], True, t != 1)
                if t == 1:
                    mm(bS[1][:, H:2 * H], ones[:, :], lf[:, 0, :], False, True)
            for t in range(QT):
                dst = bS[1][0:H, 32 + t * P:32 + (t + 1) * P]
                mm(dst, lf[:, t, :], tri[t][:, :], True, t != 1)
                if t == 1:
                    ins = mm(dst, lf[:, 0, :], ones[:, :], False, True)
            ins.then_inc(decay_full, 1)
            for t in range(TT):
                project(2 * CT + t)
            pe.wait_ge(cmul_done, 1)
            mm(bS[0][:, 0:NB], cmul[:, :, :].rearrange("p h q -> p (h q)"), of_stream[:, :]).then_inc(cq_full, 1)

            def scores_of(n):
                hd, q = unit(n)
                bank = bS[n % 2]
                if n == 0:
                    pe.wait_ge(decay_done, 1)
                if n >= 2:
                    pe.wait_ge(s_evac, n - 1)
                if hd is None:
                    b = q
                    new = slice(SEQ + b * NQ, SEQ + (b + 1) * NQ)
                    pe.wait_ge(t_evac, t_kc[b] + 1)
                    pe.wait_ge(lfx_done, b + 1)
                    mm(bank[:, 0:PAST], lfx[b % 2][:, :, :].rearrange("p h q -> p (h q)"), t_gt[:, :],
                       True, False, skip_group_check=True)
                    mm(bank[:, PAST:PAST + NQ], lfn[:, :, :].rearrange("p h q -> p (h q)"), t_str[:, b * NQ:(b + 1) * NQ],
                       False, False, skip_group_check=True)
                    for c in range(CT):
                        rows = slice(2 * NQ * c, 2 * NQ * (c + 1))
                        lhsT = qs[:, c, b, :, :].rearrange("p s q -> p (s q)")
                        mm(bank[rows, 0:PAST], lhsT, kc[b % 2][:, c, :], False, True, skip_group_check=True)
                        ins = mm(bank[rows, PAST:PAST + NQ], lhsT, kT[:, c, new], False, True, skip_group_check=True)
                else:
                    w = (q + 1) * P
                    mm(bank[:, 0:w], ident[:, hd:hd + 1].to_broadcast([P, P]), nc_p[:, 0:w], True, False)
                    ins = mm(bank[:, 0:w], qz[:, hd, q * P:(q + 1) * P], kT[:, hd // 2, 0:w], False, True)
                ins.then_inc(s_full, 1)

            def probs_transpose(n):
                hd, q = unit(n)
                blocks = 2 if hd is None else q + 1
                bank = t_bank(t_p[n])
                pe.wait_ge(pn_done, n + 1)
                for k in range(blocks):
                    ins = te.transpose(bank[:, k * P:(k + 1) * P], pnorm[n % 2][:, k * P:(k + 1) * P], ident[:, :])
                ins.then_inc(t_full, 1)

            def weighted_values(n):
                hd, q = unit(n)
                bank = bO[n % 2]
                pe.wait_ge(t_evac, t_p[n] + 1)
                if n >= 2:
                    pe.wait_ge(o_evac, n - 1)
                if n == 0:
                    pe.wait_ge(*g_place[2 * CT + TT - 1])
                if hd is None:
                    pe.wait_ge(ld_cv[q % 4], 16 * (q // 4 + 1))
                    for c in range(CT):
                        cs = slice(c * 2 * NQ, (c + 1) * 2 * NQ)
                        mm(bank[:, cs], cv[q % 4][:, c * P:(c + 1) * P], pT[n % 2][:, cs], True, False)
                        ins = mm(bank[:, cs], V[:, QT, c * P:(c + 1) * P], pT[n % 2][:, P + c * 2 * NQ:P + (c + 1) * 2 * NQ], False, True)
                else:
                    rows = slice((hd % 2) * HD, (hd % 2 + 1) * HD)
                    for k in range(q + 1):
                        ins = mm(bank[rows, 0:P], V[:, k, hd * HD:(hd + 1) * HD], pT[n % 2][:, k * P:(k + 1) * P], k == 0, k == q)
                ins.then_inc(pv_full, 1)

            def sums_of_squares(key):
                j = g_of[key]
                pe.wait_ge(*g_place[j - 2])
                pe.wait_ge(sq_done, 1 if key == ("ssB",) else key[1] + 2)
                for i, t in enumerate(range(TT) if key == ("ssB",) else [key[1]]):
                    for ct in range(CT):
                        ins = mm(bG[j % 2][:, i:i + 1], (sqB if key == ("ssB",) else sqA)[:, ct, t * P:(t + 1) * P], ones[:, 0:1],
                                 ct == 0, ct == CT - 1)
                ins.then_inc(g_full, 1)

            def out_project(key):
                (part, t, half), j = key, g_of[key]
                src, w = (oB, wo[1]) if part == "oB" else (oT, wo[0])
                pe.wait_ge(*g_place[j - 2])
                pe.wait_ge(ld_wo[1 if part == "oB" else 0], 16)
                pe.wait_ge(gain_done, 1 if part == "oB" else t + 2)
                for ct in range(CT):
                    ins = mm(bG[j % 2][:, :], src[:, ct, t * P:(t + 1) * P], w[:, ct, half * 512:(half + 1) * 512], ct == 0, ct == CT - 1)
                ins.then_inc(g_full, 1)

            def x2_transpose(t):
                pe.wait_ge(xn2_done, t + 1)
                for half in range(2):
                    bank = t_bank(t_x2[t] + half)
                    for k in range(4):
                        kk = half * 4 + k
                        ins = te.transpose(bank[:, k * P:(k + 1) * P], xn2[:, t, kk * P:(kk + 1) * P], ident[:, :])
                    ins.then_inc(t_full, 1)

            def router(key):
                t, j = key[1], g_of[key]
                pe.wait_ge(*g_place[j - 2])
                pe.wait_ge(ld_rt, 7 * 16)
                pe.wait_ge(t_evac, t_x2[t] + 2)
                for k in range(KT):
                    ins = mm(bG[j % 2][:, 0:G + E], x2T[:, t, k, :], wr[:, k, :], k == 0, k == KT - 1)
                ins.then_inc(g_full, 1)

            def job(key):
                if key[0] in "ChB":
                    project(g_of[key])
                elif key[0] in ("ssB", "ssA"):
                    sums_of_squares(key)
                elif key[0] in ("oB", "oA"):
                    out_project(key)
                elif key[0] == "x2":
                    x2_transpose(key[1])
                else:
                    router(key)

            for n in range(UNITS + 3):
                if 2 * H <= n + 1 < UNITS:
                    b = n + 1 - 2 * H
                    bank = t_bank(t_kc[b])
                    pe.wait_ge(ld_ck[b % 4], 16 * (b // 4 + 1))
                    for c in range(CT):
                        ins = te.transpose(bank[:, c * P:(c + 1) * P], ck[b % 4][:, c * P:(c + 1) * P], ident[:, :])
                    ins.then_inc(t_full, 1)
                if n < UNITS:
                    scores_of(n)
                for key in jobs_at.get(n, []):
                    job(key)
                if 0 <= n - 1 < UNITS:
                    probs_transpose(n - 1)
                if 0 <= n - 2 < UNITS:
                    weighted_values(n - 2)

            bank = t_bank(T_LAST)
            pe.wait_ge(last_done, CT)
            for ct in range(CT):
                ins = te.transpose(bank[0:2 + 2 * NB, ct * P:(ct + 1) * P], last[:, ct, :], ident[:, :])
            ins.then_inc(t_full, 1)
            for key in AFTER:
                job(key)
            pe.wait_ge(t_evac, t_jobs)
            for t in range(TT):
                pe.wait_ge(oh_done, t + 1)
                for tp in range(t + 1):
                    ins = mm(bT[0][:, t * E:(t + 1) * E], (t_lt if tp == t else ones)[:, :], ohs[:, tp, :], tp == 0, tp == t)
            ins.then_inc(rk_full, 1)
            for t in range(TT):
                ins = mm(bS[0][:, 0:E], ones[:, :], ohs[:, t, :], t == 0, t == TT - 1)
            ins.then_inc(cnt_full, 1)
            def pick_rows(n, buf, k0, k1, first):
                if k0 == 0:
                    pe.wait_ge(pick_done, n + 1)
                for k in range(k0, k1):
                    if k % 4 == 0 and not first:
                        pe.wait_ge(xgt_evac, n * 2 + (k // 4 - 1))
                    for t in range(TT):
                        ins = mm(bT[k // 4][:, (k % 4) * P:(k % 4 + 1) * P], xn2[:, t, k * P:(k + 1) * P], pick[buf][:, t, :],
                                 t == 0, t == TT - 1)
                    if k % 4 == 3:
                        ins.then_inc(xgt_full, 1)

            def gate_up(n, buf, turn, first):
                for r in (2 * buf, 2 * buf + 1):
                    pe.wait_ge(ld_gu[r], turn * 16 + 16)
                if not first:
                    pe.wait_ge(glu_done, n - 1)
                for k in range(KT):
                    if k % 4 == 0:
                        pe.wait_ge(xgt_evac, n * 2 + (k // 4 + 1))
                    for h in range(2):
                        rows = slice(h * SLOTS, (h + 1) * SLOTS)
                        ins = mm(bG[buf][rows, :], xgT[buf][:, k, rows], gu_ring[:, 2 * buf + h, k * 2 * F:(k + 1) * 2 * F], k == 0, k == KT - 1)
                ins.then_inc(gu_full, 1)

            def hidden_transpose(n, buf, first):
                pe.wait_ge(glu_done, n + 1)
                if not first:
                    pe.wait_ge(ht_evac, n)
                for j in range(FT):
                    ins = te.transpose(bS[0][:, j * P:(j + 1) * P], glu[buf][:, F + j * P:F + (j + 1) * P], ident[:, :])
                ins.then_inc(ht_full, 1)

            def down(n, buf, turn, first):
                pe.wait_ge(ht_evac, n + 1)
                for r in (2 * buf, 2 * buf + 1):
                    pe.wait_ge(ld_dn[r], turn * 16 + 16)
                for half, evac, done in ((0, y_evac_a, y_half), (1, y_evac_d, y_full)):
                    if not first:
                        pe.wait_ge(evac, n)
                    for j in range(FT):
                        for h in range(2):
                            rows = slice(h * SLOTS, (h + 1) * SLOTS)
                            ins = mm(bO[half][rows, :], hT[:, j, rows],
                                     dn_ring[:, 2 * buf + h, j * D + half * 512:j * D + half * 512 + 512], j == 0, j == FT - 1)
                    ins.then_inc(done, 1)

            def step(n, u, i, first, has_next):
                if has_next:
                    pick_rows(n + 1, 1 - u, 0, KT, False)
                hidden_transpose(n, u, first and u == 0)
                down(n, u, i, first and u == 0)
                if has_next:
                    gate_up(n + 1, 1 - u, i + u, first and u == 0)

            pe.wait_ge(xn2_scaled, TT)
            pick_rows(0, 0, 0, KT, True)
            pe.wait_ge(key_done, 1)
            for half in range(2):
                rows = slice(half * SLOTS, (half + 1) * SLOTS)
                for j in range(2 * TT):
                    ins = mm(bS[1][rows, 0:DUOS], ranked[:, j // TT, j % TT, :], oh[:, j // TT, j % TT, half::2], j == 0, j == 2 * TT - 1)
            ins.then_inc(sca_full, 1)
            gate_up(0, 0, 0, True)
            pe.wait_ge(ovr_done, 1)
            for c in range(3):
                mm(bO[0][0:1, c * OVROWS:(c + 1) * OVROWS], ovr[0:OVROWS, c:c + 1], ident[0:OVROWS, 0:OVROWS])
            mm(bO[1][:, 0:OVROWS], ovr[0:OVROWS, 1:2].to_broadcast([OVROWS, P]), ident[0:OVROWS, 0:OVROWS]).then_inc(ovr_full, 1)
            pe.wait_ge(ovr_regs, 1)
            for u in range(2):
                step(u, u, 0, True, True)
            with pe.Fori(1, LAST) as i:
                for u in range(2):
                    step(i * 2 + u, u, i, False, True)
            for u in range(2):
                step(LAST * 2 + u, u, LAST, False, u == 0)
            pe.wait_ge(y_evac_a, DUOS)
            pe.wait_ge(y_evac_d, DUOS)
            n_ov = pe.value_load(ov_regs[0:1, 2 * OVROWS:2 * OVROWS + 1], min_val=0, max_val=MAXOV)
            with pe.If(n_ov > 0):
                with pe.Fori(0, n_ov) as i:
                    pe.wait_ge(ov_pick, i + 1)
                    for k in range(KT):
                        for t in range(TT):
                            ins = mm(bT[k // 4][:, (k % 4) * SLOTS:(k % 4 + 1) * SLOTS], xn2[:, t, k * P:(k + 1) * P],
                                     pick[0][:, t, 0:SLOTS], t == 0, t == TT - 1)
                    ins.then_inc(ov_xt, 1)
                    for j in range(2 * TT):
                        ins = mm(bS[1][0:SLOTS, 0:1], ranked[:, j // TT, j % TT, :], pair_no[:, j:j + 1], j == 0, j == 2 * TT - 1)
                    ins.then_inc(ov_no, 1)
                    pe.wait_ge(ov_xe, i + 1)
                    pe.wait_ge(ov_w, i * 32 + 32)
                    for k in range(KT):
                        ins = mm(bG[0][0:SLOTS, :], xgT[0][:, k, 0:SLOTS], gu_ring[:, 0, k * 2 * F:(k + 1) * 2 * F], k == 0, k == KT - 1)
                    ins.then_inc(ov_gu, 1)
                    pe.wait_ge(ov_glu, i + 1)
                    pe.sem_inc(pe_paced, 1)
                    for j in range(FT):
                        ins = te.transpose(bS[0][:, j * SLOTS:(j + 1) * SLOTS], glu[0][0:SLOTS, F + j * P:F + (j + 1) * P],
                                           ident[0:SLOTS, 0:SLOTS])
                    ins.then_inc(ov_ht, 1)
                    pe.wait_ge(ov_he, i + 1)
                    pe.wait_ge(y_evac_a, i + DUOS)
                    pe.wait_ge(y_evac_d, i + DUOS)
                    for half in range(2):
                        for j in range(FT):
                            ins = mm(bO[half][0:SLOTS, :], hT[:, j, 0:SLOTS],
                                     dn_ring[:, 0, j * D + half * 512:j * D + half * 512 + 512], j == 0, j == FT - 1)
                    ins.then_inc(y_full, 1)


SHAPES = {
    "cache_k": (NB, PAST, A), "cache_v": (NB, PAST, A), "cache_logf": (NB, PAST, H), "state_conv": (2 * NB, C),
    "norm_mix_g": (D,), "w_in": (D, 3 * A + H + 3 * C), "b_forget": (H,), "conv_w": (3, C), "norm_attn_g": (A,),
    "norm_conv_g": (C,), "w_out": (A + C, D), "norm_ffn_g": (D,), "w_router_group": (D, G), "b_router_group": (G,),
    "w_router_expert": (G, D, EG), "b_router_expert": (E,), "w_expert_gate_up": (E, D, 2 * F),
    "w_expert_down": (E, F, D), "norm_final_g": (D,),
}
OUTPUTS = {
    "y_p": ((SEQ, D), (1, SEQ, D)), "y_s": ((NB * NQ, D), (NB, NQ, D)),
    "k_p": ((SEQ, A), (1, 1, SEQ, H, HD)), "v_p": ((SEQ, A), (1, 1, SEQ, H, HD)), "lf_p": ((SEQ, H), (1, 1, SEQ, H)),
    "conv_p": ((2, C), (1, 1, 2, C)), "k_s": ((NB * NQ, A), (1, NB, NQ, H, HD)), "v_s": ((NB * NQ, A), (1, NB, NQ, H, HD)),
    "lf_s": ((NB * NQ, H), (1, NB, NQ, H)), "conv_s": ((2 * NB, C), (1, NB, 2, C)),
}


def kernel(**inputs):
    import numpy as np
    import concourse.bacc as bacc
    from concourse.bass_utils import run_bass_kernel_spmd

    nc = bacc.Bacc("TRN2", target_bir_lowering=False, num_devices=1)
    arrays, a, o = {}, {}, {}
    rows = [np.asarray(inputs["x_prompt"]).reshape(SEQ, D), np.asarray(inputs["x_sample"]).reshape(NB * NQ, D)]
    laid = {"x": np.concatenate(rows)}
    for name, shape in SHAPES.items():
        laid[name] = np.asarray(inputs[name]).reshape(shape)
    for name, x in laid.items():
        x = np.ascontiguousarray(x)
        arrays[f"in_{name}"] = x
        a[name] = nc.dram_tensor(f"in_{name}", x.shape, mybir.dt.from_np(x.dtype), kind="ExternalInput").ap()
    for name, (shape, _) in OUTPUTS.items():
        o[name] = nc.dram_tensor(f"out_{name}", shape, mybir.dt.float32, kind="ExternalOutput").ap()
    build(nc, a, o)
    got = run_bass_kernel_spmd(nc, [arrays], core_ids=[0]).results[0]
    return tuple(got[f"out_{name}"].reshape(shape) for name, (_, shape) in OUTPUTS.items())
```
